# Optimizing a Trainium2 kernel written in Bass

```python
import jax, jax.numpy as jnp
from jax import lax
import numpy as np

D_MODEL = 1024
BATCH = 1
SEQ = 512
DEPTH = 1
DEC_BATCH = 8
DEC_SEQ = 8
PAST_LEN = 256
PAGE_SIZE = 128

N_HEADS = 8
HEAD_DIM = D_MODEL // N_HEADS
SB_WIDTH = N_HEADS * HEAD_DIM
Q_BLOCK = 128
SB_BIAS_INIT = -6.0
GM_GROUPS = 8
GM_CH = D_MODEL // GM_GROUPS
GM_WIDTH = GM_GROUPS * GM_CH
CHUNK = 128
PEER_HEADS = 8
N_KEYS = 128
N_EXPERTS = N_KEYS * N_KEYS
D_QUERY = 256
D_SUBKEY = D_QUERY // 2
TOPK = 16
PEER_BLOCK = 256
N_MOD = 6
EPS = 1e-6
OFF_Q = 0
OFF_K = OFF_Q + SB_WIDTH
OFF_V = OFF_K + SB_WIDTH
OFF_U = OFF_V + SB_WIDTH
OFF_GV = OFF_U + GM_WIDTH
OFF_GATE_A = OFF_GV + GM_WIDTH
OFF_GATE_B = OFF_GATE_A + D_MODEL
IN_WIDTH = OFF_GATE_B + D_MODEL

kernel_name = 'stick_gmlp_peer_hybrid_step'

def _rmsnorm(x, g):
    xf = x.astype(jnp.float32)
    y = xf * lax.rsqrt(jnp.mean(xf * xf, axis=-1, keepdims=True) + EPS)
    return y.astype(x.dtype) * g

def _layernorm(x, g, b):
    xf = x.astype(jnp.float32)
    mu = jnp.mean(xf, axis=-1, keepdims=True)
    var = jnp.mean(jnp.square(xf - mu), axis=-1, keepdims=True)
    return ((xf - mu) * lax.rsqrt(var + EPS)).astype(x.dtype) * g + b

def _stick_breaking_block(q, k, v, q_pos, k_pos, sb_bias):
    z = jnp.einsum('bqhd,bkhd->bhqk', q, k).astype(jnp.float32) * (HEAD_DIM ** -0.5)
    z = z + sb_bias.astype(jnp.float32)[None, :, None, None]
    readable = k_pos[None, :] < q_pos[:, None]
    log_keep = jnp.where(readable, jax.nn.log_sigmoid(-z), 0.0)
    log_after = lax.cumsum(log_keep, axis=3, reverse=True) - log_keep
    weights = jnp.where(readable, jnp.exp(jax.nn.log_sigmoid(z) + log_after), 0.0)
    return jnp.einsum('bhqk,bkhd->bqhd', weights.astype(v.dtype), v)

def _stick_breaking_attention(q, k, v, q_start, sb_bias):
    tq = q.shape[1]
    outs = []
    for s0 in range(0, tq, Q_BLOCK):
        s1 = min(s0 + Q_BLOCK, tq)
        k_end = q_start + s1
        q_pos = jnp.arange(q_start + s0, q_start + s1, dtype=jnp.int32)
        k_pos = jnp.arange(k_end, dtype=jnp.int32)
        outs.append(_stick_breaking_block(q[:, s0:s1], k[:, :k_end], v[:, :k_end], q_pos, k_pos, sb_bias))
    return jnp.concatenate(outs, axis=1)

def _chunk_spatial_gate(u, v, w_s, b_s):
    b, t, g, c = v.shape
    pad = (-t) % CHUNK
    n = (t + pad) // CHUNK
    vc = jnp.pad(v, ((0, 0), (0, pad), (0, 0), (0, 0))).reshape(b, n, CHUNK, g, c)
    w = w_s * jnp.tril(jnp.ones((CHUNK, CHUNK), w_s.dtype))
    mixed = jnp.einsum('gts,bnsgc->bntgc', w, vc) + b_s.T[:, :, None]
    return u * mixed.reshape(b, n * CHUNK, g, c)[:, :t]

def _peer_ffn(h, w_query, sub_keys, expert_down, expert_up):
    shape = h.shape
    x = h.reshape(-1, D_MODEL)
    n = x.shape[0]
    pad = (-n) % PEER_BLOCK
    blocks = jnp.pad(x, ((0, pad), (0, 0))).reshape(-1, PEER_BLOCK, D_MODEL)

    def one_block(xb):
        q = (xb @ w_query).reshape(PEER_BLOCK, PEER_HEADS, 2, D_SUBKEY)
        s = jnp.einsum('nhpd,pkd->nhpk', q, sub_keys).astype(jnp.float32)
        top_s, top_i = lax.top_k(s, TOPK)
        cand_s = (top_s[:, :, 0, :, None] + top_s[:, :, 1, None, :]).reshape(PEER_BLOCK, PEER_HEADS, TOPK * TOPK)
        cand_e = (top_i[:, :, 0, :, None] * N_KEYS + top_i[:, :, 1, None, :]).reshape(PEER_BLOCK, PEER_HEADS, TOPK * TOPK)
        best_s, best_j = lax.top_k(cand_s, TOPK)
        experts = jnp.take_along_axis(cand_e, best_j, axis=-1)
        gates = jax.nn.softmax(best_s, axis=-1)
        act = jax.nn.gelu(jnp.einsum('nd,nhkd->nhk', xb, expert_down[experts]), approximate=False)
        coef = (gates * act.astype(jnp.float32)).astype(xb.dtype)
        return jnp.einsum('nhk,nhkd->nd', coef, expert_up[experts])

    out = lax.map(one_block, blocks)
    return out.reshape(-1, D_MODEL)[:n].reshape(shape)

def _token_mixing(h, k_past, v_past, q_start, w_in, sb_bias, g_v, b_v, w_s, b_s, w_ba, w_bb, w_out):
    b, t, _ = h.shape
    proj = h @ w_in
    q = proj[..., OFF_Q:OFF_K].reshape(b, t, N_HEADS, HEAD_DIM)
    k = proj[..., OFF_K:OFF_V].reshape(b, t, N_HEADS, HEAD_DIM)
    v = proj[..., OFF_V:OFF_U].reshape(b, t, N_HEADS, HEAD_DIM)
    u = jax.nn.gelu(proj[..., OFF_U:OFF_GV], approximate=False).reshape(b, t, GM_GROUPS, GM_CH)
    gv = _layernorm(jax.nn.gelu(proj[..., OFF_GV:OFF_GATE_A], approximate=False), g_v, b_v).reshape(b, t, GM_GROUPS, GM_CH)
    gate_a = jax.nn.sigmoid(proj[..., OFF_GATE_A:OFF_GATE_B])
    gate_b = jax.nn.sigmoid(proj[..., OFF_GATE_B:IN_WIDTH])
    if k_past is None:
        keys, vals = k, v
    else:
        keys = jnp.concatenate([k_past, k], axis=1)
        vals = jnp.concatenate([v_past, v], axis=1)
    out_b = _stick_breaking_attention(q, keys, vals, q_start, sb_bias).reshape(b, t, SB_WIDTH)
    out_a = _chunk_spatial_gate(u, gv, w_s, b_s).reshape(b, t, GM_WIDTH)
    merged = gate_a * (out_a @ w_ba) + gate_b * (out_b @ w_bb)
    return merged @ w_out, k, v, gv

def _decoder_layer(x, c, k_past, v_past, q_start, params):
    (w_ada, b_ada, g1, w_in, sb_bias, g_v, b_v, w_s, b_s, w_ba, w_bb, w_out,
     g2, w_query, sub_keys, e_down, e_up) = params
    mod = (jax.nn.silu(c) @ w_ada + b_ada).reshape(c.shape[0], N_MOD, D_MODEL)
    shift1, scale1, gate1 = mod[:, 0, None, :], mod[:, 1, None, :], mod[:, 2, None, :]
    shift2, scale2, gate2 = mod[:, 3, None, :], mod[:, 4, None, :], mod[:, 5, None, :]
    h = _rmsnorm(x, g1) * (1.0 + scale1) + shift1
    mix, k_new, v_new, gv_new = _token_mixing(h, k_past, v_past, q_start, w_in, sb_bias, g_v, b_v, w_s, b_s, w_ba, w_bb, w_out)
    x = x + gate1 * mix
    h = _rmsnorm(x, g2) * (1.0 + scale2) + shift2
    x = x + gate2 * _peer_ffn(h, w_query, sub_keys, e_down, e_up)
    return x, k_new, v_new, gv_new

def setup_inputs(seed: int = 0) -> dict:
    key = jax.random.key(seed)
    ks = jax.random.split(key, 26)
    n_pages = PAST_LEN // PAGE_SIZE
    n_used = DEC_BATCH * n_pages
    n_phys = n_used + max(1, n_used // 4)

    def nrm(k, shape, scale):
        return jax.random.normal(k, shape, jnp.float32) * scale

    page_table = jax.random.permutation(ks[4], n_phys)[:n_used].reshape(DEC_BATCH, n_pages).astype(jnp.int32)
    L = DEPTH
    return {
        'x_prompt': nrm(ks[0], (BATCH, SEQ, D_MODEL), 1.0),
        'x_sample': nrm(ks[1], (DEC_BATCH, DEC_SEQ, D_MODEL), 1.0),
        'cache_k': nrm(ks[2], (L, n_phys, PAGE_SIZE, N_HEADS, HEAD_DIM), 1.0),
        'cache_v': nrm(ks[3], (L, n_phys, PAGE_SIZE, N_HEADS, HEAD_DIM), 1.0),
        'page_table': page_table,
        'c_prompt': nrm(ks[5], (BATCH, D_MODEL), 1.0),
        'c_sample': nrm(ks[6], (DEC_BATCH, D_MODEL), 1.0),
        'w_ada': nrm(ks[7], (L, D_MODEL, N_MOD * D_MODEL), 0.5 * D_MODEL ** -0.5),
        'b_ada': nrm(ks[8], (L, N_MOD * D_MODEL), 0.02),
        'g_norm1': 1.0 + nrm(ks[9], (L, D_MODEL), 0.02),
        'w_in': nrm(ks[10], (L, D_MODEL, IN_WIDTH), D_MODEL ** -0.5),
        'sb_bias': SB_BIAS_INIT + nrm(ks[24], (L, N_HEADS), 0.1),
        'g_v': 1.0 + nrm(ks[11], (L, GM_WIDTH), 0.02),
        'b_v': nrm(ks[12], (L, GM_WIDTH), 0.02),
        'w_spatial': nrm(ks[13], (L, GM_GROUPS, CHUNK, CHUNK), CHUNK ** -0.5),
        'b_spatial': 1.0 + nrm(ks[14], (L, GM_GROUPS, CHUNK), 0.02),
        'w_branch_a': nrm(ks[15], (L, GM_WIDTH, D_MODEL), GM_WIDTH ** -0.5),
        'w_branch_b': nrm(ks[16], (L, SB_WIDTH, D_MODEL), SB_WIDTH ** -0.5),
        'w_out': nrm(ks[17], (L, D_MODEL, D_MODEL), D_MODEL ** -0.5),
        'g_norm2': 1.0 + nrm(ks[18], (L, D_MODEL), 0.02),
        'w_query': nrm(ks[19], (L, D_MODEL, PEER_HEADS * D_QUERY), D_MODEL ** -0.5),
        'sub_keys': nrm(ks[20], (L, 2, N_KEYS, D_SUBKEY), D_SUBKEY ** -0.5),
        'expert_down': nrm(ks[21], (L, N_EXPERTS, D_MODEL), D_MODEL ** -0.5),
        'expert_up': nrm(ks[22], (L, N_EXPERTS, D_MODEL), 0.5),
        'g_final': 1.0 + nrm(ks[23], (D_MODEL,), 0.02),
    }

def reference(x_prompt, x_sample, cache_k, cache_v, page_table, c_prompt, c_sample,
              w_ada, b_ada, g_norm1, w_in, sb_bias, g_v, b_v, w_spatial, b_spatial,
              w_branch_a, w_branch_b, w_out, g_norm2, w_query, sub_keys,
              expert_down, expert_up, g_final):
    n_dec, n_pages = page_table.shape
    past_len = n_pages * cache_k.shape[2]
    xp, xs = x_prompt, x_sample
    kp_rows, vp_rows, ks_rows, vs_rows, gs_rows = [], [], [], [], []
    for l in range(DEPTH):
        params = (w_ada[l], b_ada[l], g_norm1[l], w_in[l], sb_bias[l], g_v[l], b_v[l], w_spatial[l], b_spatial[l],
                  w_branch_a[l], w_branch_b[l], w_out[l], g_norm2[l], w_query[l], sub_keys[l],
                  expert_down[l], expert_up[l])
        xp, kp, vp, _ = _decoder_layer(xp, c_prompt, None, None, 0, params)
        k_past = cache_k[l][page_table].reshape(n_dec, past_len, N_HEADS, HEAD_DIM)
        v_past = cache_v[l][page_table].reshape(n_dec, past_len, N_HEADS, HEAD_DIM)
        xs, ks_, vs_, gs_ = _decoder_layer(xs, c_sample, k_past, v_past, past_len, params)
        kp_rows.append(kp)
        vp_rows.append(vp)
        ks_rows.append(ks_)
        vs_rows.append(vs_)
        gs_rows.append(gs_)
    y_prompt = _rmsnorm(xp, g_final)
    y_sample = _rmsnorm(xs, g_final)
    new_k_prompt = jnp.stack(kp_rows)
    new_v_prompt = jnp.stack(vp_rows)
    new_k_sample = jnp.stack(ks_rows)
    new_v_sample = jnp.stack(vs_rows)
    new_gmlp_v_sample = jnp.stack(gs_rows)
    return (y_prompt, y_sample, new_k_prompt, new_v_prompt, new_k_sample, new_v_sample, new_gmlp_v_sample)


_drawn_inputs = setup_inputs


def setup_inputs(seed=0):
    import zlib

    import numpy as np

    out = dict(_drawn_inputs(seed))
    spreads = {}
    factors = {'cache_k': 4.14,
     'cache_v': 3.531,
     'sb_bias': 8.0,
     'g_v': 22.168,
     'b_v': 22.776,
     'b_spatial': 8.0,
     'g_norm2': 4.416,
     'g_final': 24.23}
    for name, (base, spread) in spreads.items():
        noise = np.random.default_rng([zlib.crc32(name.encode()), seed]).standard_normal(out[name].shape)
        drawn = base * np.exp(spread * noise) if base else spread * noise
        out[name] = __import__('jax').numpy.asarray(drawn.astype(out[name].dtype))
    for name, factor in factors.items():
        out[name] = (out[name] * factor).astype(out[name].dtype)
    return out
```

```python
from contextlib import ExitStack

import numpy as np

import concourse.bass as bass
from concourse import mybir

ALU = mybir.AluOpType
ACT = mybir.ActivationFunctionType
AX = mybir.AxisListType
F32 = mybir.dt.float32
I32 = mybir.dt.int32
U32 = mybir.dt.uint32

P = 128
D = 1024
KC = D // P
WC = 256
NH = 8
SEQ, NDEC, DSEQ = 512, 8, 8
NS = NDEC * DSEQ
NG = 1 + NDEC
NMOD = 6
TOPK = 16
NKEY = 128
SCALE = float(P) ** -0.5
EPS = 1e-6
LOWEST = -3.0e38
SLOTS = 8
TILES = 5
SAMPLE = 4
GROUPS = [[0, SAMPLE], [1, 2, 3]]
NADA = NMOD * D // WC
NCH = 48

ORDER = [0, SAMPLE, 1, 2, 3]
STEPS = {0: 8, SAMPLE: 4, 1: 8, 2: 8, 3: 8}


def slot_of(g, i):
    return i if g == 0 else 1 + i


def xslot_of(g, i):
    return 2 + i if g == 0 else 1 + i


def fill_base(g, phase):
    t = len(GROUPS[g])
    base = NADA if g == 0 else NADA + 64 + 16 * len(GROUPS[0])
    return base + {"q": 0, "k": 8, "v": 8 + 4 * t, "u": 8 + 8 * t, "gv": 16 + 8 * t,
                   "merge": 16 + 12 * t, "out": 48 + 12 * t, "query": 48 + 16 * t}[phase]


def turn_base(g, phase):
    t = len(GROUPS[g])
    base = 8 if g == 0 else 8 + 10 * len(GROUPS[0])
    return base + {"norm1": 0, "kT": 2 * t, "gate": 6 * t, "norm2": 8 * t}[phase]


def chunk_base(g, phase):
    return NADA + NCH * g + {"q": 0, "k": 4, "v": 8, "u": 12, "gv": 16, "merge": 20, "out": 36, "query": 40}[phase]


def last_fill(n):
    if n < NADA:
        return n
    g, m = divmod(n - NADA, NCH)
    t = len(GROUPS[g])
    for phase, fills in (("query", 2), ("out", t), ("merge", 2), ("gv", t), ("u", 2), ("v", t), ("k", t), ("q", 2)):
        c = n - chunk_base(g, phase)
        if c >= 0:
            return fill_base(g, phase) + fills * (c + 1) - 1


def tables(g):
    if g == 0:
        return [("A1", "p"), ("B1", "p"), ("A1", "s"), ("B1", "s"), ("gv", ""), ("bv", ""),
                ("G1", "p"), ("G1", "s"), ("A2", "p"), ("B2", "p"), ("A2", "s"), ("B2", "s")]
    return [("A1", "p"), ("B1", "p"), ("gv", ""), ("bv", ""), ("G1", "p"), ("A2", "p"), ("B2", "p")]


def table_number(g, what, kind):
    return (len(tables(0)) if g else 0) + tables(g).index((what, kind))


def build(nc, x_prompt, x_sample, cache_k, cache_v, page_table, c_prompt, c_sample, w_ada, b_ada,
          g_norm1, w_in, sb_bias, g_v, b_v, w_spatial, b_spatial, w_branch_a, w_branch_b, w_out,
          g_norm2, w_query, sub_keys, expert_down, expert_up, g_final,
          y_prompt, y_sample, nk_prompt, nv_prompt, nk_sample, nv_sample, ngv_sample):
    n_phys = cache_k.shape[1]
    xp = x_prompt.rearrange("b (t p) d -> (b t) p d", p=P)
    xs = x_sample.rearrange("b i d -> (b i) d")
    kpages = cache_k.rearrange("l n p h d -> (l n p) (h d)")
    vpages = cache_v.rearrange("l n p h d -> (l n p) (h d)")
    yp = y_prompt.rearrange("b (t p) d -> (b t) p d", p=P)
    ys = y_sample.rearrange("b i d -> (b i) d")
    nkp = nk_prompt.rearrange("l b (t p) h d -> (l b t) p (h d)", p=P)
    nvp = nv_prompt.rearrange("l b (t p) h d -> (l b t) p (h d)", p=P)
    nks = nk_sample.rearrange("l b i h d -> (l b i) (h d)")
    nvs = nv_sample.rearrange("l b i h d -> (l b i) (h d)")
    ngs = ngv_sample.rearrange("l b i h d -> (l b i) (h d)")
    down = expert_down.rearrange("l e d -> (l e) d")
    up = expert_up.rearrange("l e d -> (l e) d")

    def weights(w):
        return w.rearrange("l (k p) n -> p (l k) n", p=P)

    wv = {"ada": weights(w_ada), "in": weights(w_in), "ba": weights(w_branch_a),
          "bb": weights(w_branch_b), "out": weights(w_out), "query": weights(w_query)}

    mod_p = nc.dram_tensor("mod_prompt", (1, NMOD * D), F32, kind="Internal").ap()
    mod_s = nc.dram_tensor("mod_sample", (NS, NMOD * D), F32, kind="Internal").ap()
    x1_dram = nc.dram_tensor("x1_tiles", (TILES, P, D), F32, kind="Internal").ap()

    with ExitStack() as ctx:
        def sb(name, shape, dt=F32):
            return ctx.enter_context(nc.sbuf_tensor(name, shape, dt))

        def sem(name):
            return ctx.enter_context(nc.semaphore(name))

        bank = [ctx.enter_context(nc.psum_tensor(f"bank{i}", [P, 512], F32)) for i in range(8)]

        ring = sb("gather_ring", [P, SLOTS, D])
        wbuf = sb("weight_chunks", [P, 4, KC, WC])
        h2keep = sb("h2_group0", [P, 2, D])
        hTf = sb("hT", [P, 3072])
        kT = sb("kT", [P, 4, NH, P])
        vv = sb("v_tokens", [P, 4, D])
        qTf = sb("qT", [P, 3072])
        U = sb("u_and_gv", [P, 6144])
        sg = sb("sigmoids", [P, 4, 384])
        tab = sb("row_tables", [P, 3, D])
        acc = sb("expert_sums", [P, 2, D])
        WsT = sb("spatialT", [P, NH, P])
        bsb = sb("spatial_bias", [P, NH, P])
        skT = sb("sub_keysT", [P, 2, NKEY])
        junk = sb("scratch_row", [P, D])
        ident = sb("identity", [P, P])
        later = sb("later_keys", [P, P])
        ones = sb("ones", [P, P])
        strict = sb("strict_causal", [P, P])
        ownseq = sb("own_sequence", [NS, NS])
        expert = sb("expert_numbers", [P, TILES, P], I32)
        gates = sb("expert_gates", [P, TILES, P])
        stage = sb("gather_rows", [P, 2, TOPK], I32)
        cT = sb("condT", [P, KC, NG])
        bias_b = sb("stick_bias", [P, NH])
        iota_i = sb("iota_int", [P, TOPK], I32)
        iota_f = sb("iota", [P, TOPK])
        st = sb("norm_stats", [P, 16])
        dots = sb("expert_dots", [P, TOPK])
        acts = sb("expert_acts", [P, TOPK])
        coef = sb("expert_coefs", [P, TOPK])
        pt_sb = sb("page_numbers", [1, 2 * NDEC], I32)
        tk_m = sb("top_values", [P, 2, TOPK])
        tk_i = sb("top_places", [P, 2, TOPK], U32)
        tk_b = sb("best_places", [P, TOPK], U32)
        tk_hl = sb("best_halves", [P, 2, TOPK], U32)
        sm = sb("softmax_parts", [P, 2, NH])

        flat = ring[:, :, :].rearrange("p s d -> p (s d)")
        mod9 = flat[0:NG, 0:NMOD * D]
        c9 = flat[0:NG, 6144:7168]
        g1row = flat[0:NG, 7168:8192]
        g2row = acc[0:NG, 0, :]
        ws_nat = U[:, 2048:3072].rearrange("p (g s) -> p g s", g=NH)
        wss_nat = U[:, 5120:6144].rearrange("p (g s) -> p g s", g=NH)
        WsTs = hTf[:, 2048:3072].rearrange("p (g t) -> p g t", g=NH)
        bsbs = qTf[:, 2048:3072].rearrange("p (g t) -> p g t", g=NH)
        sk_nat = sg[:, 2, 0:256].rearrange("p (a d) -> p a d", a=2)
        causal = sg[:, 0, 0:P]

        def width(g):
            return P * len(GROUPS[g])

        def hT(g):
            return hTf[:, 0:KC * width(g)].rearrange("p (k n) -> p k n", k=KC)

        def qT(g):
            return qTf[:, 0:NH * width(g)].rearrange("p (k n) -> p k n", k=NH)

        def uT(g):
            return U[:, 0:NH * width(g)].rearrange("p (k n) -> p k n", k=NH)

        def mT(g):
            return U[:, 3072:3072 + NH * width(g)].rearrange("p (k n) -> p k n", k=NH)

        def gvt(i):
            return U[:, 3072 + D * i:3072 + D * (i + 1)]

        def h2(g, i):
            return h2keep[:, i, :] if g == 0 else gvt(i)

        def att(what, n):
            at = {"z": 0, "e": 1024, "s": 2048}[what] + 512 * (n % 2)
            return U[:, at:at + 512]

        def masked(n):
            return sg[:, n % 2, 0:P]

        kTf = kT[:, 2:4].rearrange("p s h d -> p (s h d)")
        vf = vv[:, 2:4].rearrange("p s d -> p (s d)")
        ef = ring[:, 6:8].rearrange("p s d -> p (s d)")
        zS = [kTf[:, 0:512], kTf[:, 512:1024], kTf[0:NS, 1024:1536]]
        sS = [vf[:, 0:512], vf[:, 512:1024], vf[0:NS, 1024:1536]]
        eS = [ef[:, 0:512], ef[:, 512:1024], ef[0:NS, 1024:1536]]
        smS = kTf[0:NS, 1536:2048]

        qh = U[:, 0:1536].rearrange("p (b a n) -> p b a n", b=2, a=2)
        sc = U[:, 1536:2304].rearrange("p (i a k) -> p i a k", i=3, a=2)
        sc2 = U[:, 2304:2560].rearrange("p (a k) -> p a k", a=2)
        cand = U[:, 2560:2816]
        cand2 = U[:, 2816:3072]
        chosen = qTf[:, 0:1920].rearrange("p (i a k) -> p i a k", i=3, a=5)
        onehot = qTf[:, 2048:3072]

        s_const = sem("s_const")
        s_cond = sem("s_cond")
        s_small = sem("s_small")
        s_pt = sem("s_pt")
        s_silu = sem("s_silu")
        s_zero = sem("s_zero")
        s_wss = sem("s_wss")
        s_mod = sem("s_mod")
        s_modst = sem("s_modst")
        s_wload = [sem(f"s_wload{i}") for i in range(4)]
        s_full = [sem(f"s_full{i}") for i in range(4)]
        s_free = [sem(f"s_free{i}") for i in range(4)]
        s_tfull = [sem(f"s_tfull{i}") for i in range(2)]
        s_tfree = [sem(f"s_tfree{i}") for i in range(2)]
        s_tab = [sem(f"s_tab{i}") for i in range(3)]
        s_tabfree = sem("s_tabfree")
        s_x = [sem("s_x_g0"), sem("s_x_g1")]
        s_xr = [sem("s_xr_g0"), sem("s_xr_g1")]
        s_n1v, s_n1s, s_n1h = sem("s_n1v"), sem("s_n1s"), sem("s_n1h")
        s_n2v, s_n2s, s_n2h = sem("s_n2v"), sem("s_n2s"), sem("s_n2h")
        s_lnv, s_lns, s_lnh = sem("s_lnv"), sem("s_lns"), sem("s_lnh")
        s_k = sem("s_k")
        s_kst = sem("s_kst")
        s_v = sem("s_v")
        s_vst = sem("s_vst")
        s_gv = sem("s_gv")
        s_gvst = sem("s_gvst")
        s_az = sem("s_az")
        s_azb = sem("s_azb")
        s_al = sem("s_al")
        s_as = sem("s_as")
        s_ac = sem("s_ac")
        s_ad = sem("s_ad")
        s_aw = sem("s_aw")
        s_am = sem("s_am")
        s_ao = sem("s_ao")
        s_ae = sem("s_ae")
        s_page = [sem(f"s_page{i}") for i in range(4)]
        s_pused = sem("s_pused")
        s_ktf = [sem("s_ktf0"), sem("s_ktf1")]
        s_kte = sem("s_kte")
        s_sz, s_szb, s_sl, s_ss = sem("s_sz"), sem("s_szb"), sem("s_sl"), sem("s_ss")
        s_scm, s_sd, s_sw, s_sm = sem("s_scm"), sem("s_sd"), sem("s_sw"), sem("s_sm")
        s_so, s_se = sem("s_so"), sem("s_se")
        s_gate = sem("s_gate")
        s_sga = sem("s_sga")
        s_mrg = sem("s_mrg")
        s_x1 = sem("s_x1")
        s_x1st = sem("s_x1st")
        s_hTe = sem("s_hTe")
        s_qh = sem("s_qh")
        s_sfull = [sem(f"s_sfull{i}") for i in range(3)]
        s_sev = [sem(f"s_sev{i}") for i in range(3)]
        s_tk = [sem(f"s_tk{i}") for i in range(3)]
        s_nb = sem("s_nb")
        s_ex = sem("s_ex")
        s_dn = sem("s_dn")
        s_up = sem("s_up")
        s_gath = [sem(f"s_gath{i}") for i in range(SLOTS)]
        s_slot = sem("s_slot")
        s_dots = sem("s_dots")
        s_acts = sem("s_acts")
        s_coef = sem("s_coef")
        s_fin = sem("s_fin")
        s_half = sem("s_half")
        s_fold = sem("s_fold")
        s_fv, s_fs, s_fy = sem("s_fv"), sem("s_fs"), sem("s_fy")
        s_y = sem("s_y")

        NCONST = 12

        block = ctx.enter_context(nc.Block())

        @block.sync
        def _(sp):
            def load_weight(n, src):
                if n >= 4:
                    f = last_fill(n - 4)
                    sp.wait_ge(s_full[f % 4], f // 4 + 1)
                sp.dma_start(wbuf[:, n % 4], src).then_inc(s_wload[n % 4], 16)

            def columns(name, at):
                return wv[name][:, :, at:at + WC]

            def load_table(g, what, kind):
                n = table_number(g, what, kind)
                if n >= 3:
                    sp.wait_ge(s_tabfree, n - 2)
                dst = tab[:, n % 3, :]
                if what in ("gv", "bv"):
                    sp.dma_start(dst, (g_v if what == "gv" else b_v).broadcast_to([P, D])).then_inc(s_tab[n % 3], 32)
                    return
                m = {"B1": 0, "A1": 1, "G1": 2, "B2": 3, "A2": 4}[what]
                if kind == "p":
                    sp.dma_start(dst, mod_p[:, m * D:(m + 1) * D].broadcast_to([P, D])).then_inc(s_tab[n % 3], 32)
                else:
                    for half in range(2):
                        sp.dma_start(tab[half * NS:(half + 1) * NS, n % 3, :],
                                     mod_s[:, m * D:(m + 1) * D]).then_inc(s_tab[n % 3], 16)

            def load_x(g, slots, signal):
                for i, t in enumerate(GROUPS[g]):
                    dst = vv[:, slots[i], :]
                    if t == SAMPLE:
                        for half in range(2):
                            sp.dma_start(vv[half * NS:(half + 1) * NS, slots[i], :], xs).then_inc(signal, 16)
                    else:
                        sp.dma_start(dst, xp[t]).then_inc(signal, 32)

            sp.dma_start(c9[0:1, :], c_prompt).then_inc(s_cond, 16)
            sp.dma_start(c9[1:NG, :], c_sample).then_inc(s_cond, 16)
            for n in range(4):
                load_weight(n, columns("ada", n * WC))
            sp.dma_start(mod9, b_ada.broadcast_to([NG, NMOD * D])).then_inc(s_cond, 16)
            sp.dma_start(g1row, g_norm1.broadcast_to([NG, D])).then_inc(s_cond, 16)
            sp.dma_start(g2row, g_norm2.broadcast_to([NG, D])).then_inc(s_cond, 16)
            sp.dma_start(pt_sb[:], page_table.rearrange("(o b) n -> o (b n)", o=1)).then_inc(s_pt, 16)
            sp.dma_start(ws_nat, w_spatial.rearrange("l g t s -> t (l g) s")).then_inc(s_small, 16)
            sp.dma_start(sk_nat, sub_keys.rearrange("l a k d -> k (l a) d")).then_inc(s_small, 16)
            sp.dma_start(bias_b[:], sb_bias.broadcast_to([P, NH])).then_inc(s_small, 16)
            sp.dma_start(bsb[:].rearrange("p g t -> p (g t)"),
                         b_spatial.rearrange("l g t -> l (g t)").broadcast_to([P, NH * P])).then_inc(s_small, 16)
            for b in range(P // DSEQ):
                sp.dma_start(bsbs[:, :, b * DSEQ:(b + 1) * DSEQ],
                             b_spatial[:, :, 0:DSEQ].broadcast_to([P, NH, DSEQ])).then_inc(s_small, 16)
            sp.wait_ge(s_zero, 1)
            for b in range(P // DSEQ):
                sp.dma_start(wss_nat[b * DSEQ:(b + 1) * DSEQ, :, b * DSEQ:(b + 1) * DSEQ],
                             w_spatial[0, :, 0:DSEQ, 0:DSEQ].rearrange("g t s -> t g s")).then_inc(s_wss, 16)
            load_x(0, [slot_of(0, i) for i in range(2)], s_x[0])
            for n in range(4, NADA):
                load_weight(n, columns("ada", n * WC))
            sp.wait_ge(s_mod, NADA + 2)
            sp.dma_start(mod_p, mod9[0:1, :]).then_inc(s_modst, 16)
            sp.dma_start(mod_s.rearrange("(b i) n -> b i n", i=DSEQ),
                         mod9[1:NG, :].unsqueeze(1).broadcast_to([NDEC, DSEQ, NMOD * D])).then_inc(s_modst, 16)
            sp.wait_ge(s_modst, 32)

            for g, tiles in enumerate(GROUPS):
                T = len(tiles)
                before = sum(len(GROUPS[j]) for j in range(g))
                if g:
                    sp.wait_ge(s_x1st, 16 * before)
                    load_x(g, [slot_of(g, i) for i in range(T)], s_x[g])
                for n in range(4):
                    load_weight(chunk_base(g, "q") + n, columns("in", n * WC))
                if g == 0:
                    for w in ("A1", "B1"):
                        load_table(g, w, "p")
                    for w in ("A1", "B1"):
                        load_table(g, w, "s")
                else:
                    for w in ("A1", "B1"):
                        load_table(g, w, "p")
                for n in range(4, 12):
                    load_weight(chunk_base(g, "q") + n, columns("in", n * WC))
                sp.wait_ge(s_k, 4 * (before + T))
                for i, t in enumerate(tiles):
                    if t == SAMPLE:
                        sp.dma_start(nks, gvt(i)[0:NS, :]).then_inc(s_kst, 16)
                    else:
                        sp.dma_start(nkp[t], gvt(i)).then_inc(s_kst, 16)
                sp.wait_ge(s_v, 4 * (before + T))
                for i, t in enumerate(tiles):
                    if t == SAMPLE:
                        sp.dma_start(nvs, vv[0:NS, slot_of(g, i), :]).then_inc(s_vst, 16)
                    else:
                        sp.dma_start(nvp[t], vv[:, slot_of(g, i), :]).then_inc(s_vst, 16)
                if g == 0:
                    sp.wait_ge(s_pt, 16)
                    for m in range(4 * NDEC):
                        page = m % (2 * NDEC)
                        number = sp.value_load(pt_sb[0:1, page:page + 1], min_val=0, max_val=n_phys - 1)
                        if m >= 4:
                            sp.wait_ge(s_pused, m - 3)
                        store = kpages if m < 2 * NDEC else vpages
                        sp.dma_start(ring[:, m % 4, :], store[bass.ds(number * P, P), :]).then_inc(s_page[m % 4], 16)
                for n in range(12, 16):
                    load_weight(chunk_base(g, "q") + n, columns("in", n * WC))
                load_table(g, "gv", "")
                load_table(g, "bv", "")
                for n in range(16, 20):
                    load_weight(chunk_base(g, "q") + n, columns("in", n * WC))
                if g == 0:
                    sp.wait_ge(s_lnh, 2)
                    sp.dma_start(ngs, gvt(1)[0:NS, :]).then_inc(s_gvst, 16)
                load_table(g, "G1", "p")
                if g == 0:
                    load_table(g, "G1", "s")
                sp.wait_ge(s_ae, NH * (1 if g == 0 else 4))
                if g == 0:
                    sp.wait_ge(s_sm, 1)
                    sp.wait_ge(s_so, 1)
                sp.wait_ge(s_vst, 16 * (before + T))
                load_x(g, [xslot_of(g, i) for i in range(T)], s_xr[g])
                for j in range(4):
                    n = chunk_base(g, "merge") + 4 * j
                    load_weight(n, columns("in", 5 * D + j * WC))
                    load_weight(n + 1, columns("ba", j * WC))
                    load_weight(n + 2, columns("in", 6 * D + j * WC))
                    load_weight(n + 3, columns("bb", j * WC))
                for c in range(4):
                    load_weight(chunk_base(g, "out") + c, columns("out", c * WC))
                load_table(g, "A2", "p")
                load_table(g, "B2", "p")
                if g == 0:
                    load_table(g, "A2", "s")
                    load_table(g, "B2", "s")
                for c in range(4):
                    load_weight(chunk_base(g, "query") + c, columns("query", c * WC))
                for i, t in enumerate(tiles):
                    sp.wait_ge(s_x1, before + i + 1)
                    sp.dma_start(x1_dram[t], vv[:, xslot_of(g, i), :]).then_inc(s_x1st, 16)
                for c in range(4, 8):
                    load_weight(chunk_base(g, "query") + c, columns("query", c * WC))
            sp.wait_ge(s_kst, 16 * TILES)
            sp.wait_ge(s_vst, 16 * TILES)
            sp.wait_ge(s_gvst, 16)
            sp.wait_ge(s_x1st, 16 * TILES)
            sp.wait_ge(s_y, 16 * TILES)

        @block.gpsimd
        def _(pool):
            done = [0]

            def const(ins):
                done[0] += 1
                ins.then_inc(s_const, 1)
                pool.wait_ge(s_const, done[0])

            const(nc.gpsimd.memset(ident[:], 0.0))
            const(nc.gpsimd.affine_select(out=ident[:], in_=ident[:], compare_op=ALU.not_equal, fill=1.0,
                                          base=0, pattern=[[-1, P]], channel_multiplier=1))
            const(nc.gpsimd.memset(ones[:], 1.0))
            const(nc.gpsimd.affine_select(out=later[:], in_=ones[:], compare_op=ALU.is_gt, fill=0.0,
                                          base=0, pattern=[[-1, P]], channel_multiplier=1))
            const(nc.gpsimd.affine_select(out=strict[:], in_=ones[:], compare_op=ALU.is_gt, fill=0.0,
                                          base=0, pattern=[[1, P]], channel_multiplier=-1))
            const(nc.gpsimd.affine_select(out=causal, in_=ones[:], compare_op=ALU.is_ge, fill=0.0,
                                          base=0, pattern=[[1, P]], channel_multiplier=-1))
            blocks = ownseq[:].rearrange("p (b i) -> p b i", i=DSEQ)
            const(nc.gpsimd.affine_select(out=blocks, in_=strict[0:NS, 0:NS].rearrange("p (b i) -> p b i", i=DSEQ),
                                          compare_op=ALU.is_ge, fill=0.0, base=0,
                                          pattern=[[-DSEQ, NDEC], [0, DSEQ]], channel_multiplier=1))
            const(nc.gpsimd.affine_select(out=blocks, in_=blocks, compare_op=ALU.is_ge, fill=0.0, base=DSEQ - 1,
                                          pattern=[[DSEQ, NDEC], [0, DSEQ]], channel_multiplier=-1))
            const(nc.gpsimd.iota(iota_i[:], pattern=[[1, TOPK]], base=0, channel_multiplier=0))
            const(nc.gpsimd.tensor_copy(iota_f[:], iota_i[:]))
            const(nc.gpsimd.memset(wss_nat, 0.0))
            const(nc.gpsimd.memset(stage[:], 0))
            assert done[0] == NCONST

            claimed = pool.alloc_register("slots_claimed")
            pool.reg_mov(claimed, 0)
            batches = [0, 0]

            def gather(table, which, k):
                pool.reg_add(claimed, claimed, 1)
                pool.wait_ge(s_const, NCONST)
                pool.wait_ge(s_slot, claimed)
                pool.indirect_dma_start(
                    out=ring[:, k % SLOTS, :], out_offset=None, in_=table,
                    in_offset=bass.IndirectOffsetOnAxis(ap=stage[:, which, k:k + 1], axis=0),
                ).then_inc(s_gath[k % SLOTS], 16)

            def gather_down(n):
                pool.wait_ge(s_dn, n)
                for k in range(TOPK):
                    gather(down, 0, k)

            def gather_up(n):
                pool.wait_ge(s_up, n)
                for k in range(TOPK):
                    gather(up, 1, k)

            first = 0
            for order, t in enumerate(ORDER):
                H = STEPS[t]
                gather_down(first + 1)
                with pool.Fori(1, H) as h:
                    gather_down(h + (first + 1))
                    gather_up(h + first)
                gather_up(first + H)
                first += H
                pool.reg_add(claimed, claimed, 3)
                pool.wait_ge(s_const, NCONST)
                pool.wait_ge(s_slot, claimed)
                if t == SAMPLE:
                    for half in range(2):
                        pool.dma_start(ring[half * NS:(half + 1) * NS, 0, :],
                                       mod_s[:, 5 * D:6 * D]).then_inc(s_fin, 16)
                else:
                    pool.dma_start(ring[:, 0, :], mod_p[:, 5 * D:6 * D].broadcast_to([P, D])).then_inc(s_fin, 32)
                pool.dma_start(ring[:, 1, :], g_final.rearrange("(o d) -> o d", o=1).broadcast_to([P, D])).then_inc(s_fin, 16)
                pool.dma_start(ring[:, 2, :], x1_dram[t]).then_inc(s_fin, 16)
                if t == SAMPLE:
                    pool.wait_ge(s_half, 1)
                    pool.dma_start(ring[0:NS, 3, :], acc[NS:P, 0, :]).then_inc(s_fold, 16)
                pool.reg_add(claimed, claimed, SLOTS - 3)

        @block.tensor
        def _(pe):
            def weight(n):
                pe.wait_ge(s_wload[n % 4], 16 * (n // 4 + 1))
                return wbuf[:, n % 4]

            def take(f):
                if f >= 4:
                    pe.wait_ge(s_free[f % 4], f // 4)
                return bank[f % 4]

            def take_turn(t):
                if t >= 2:
                    pe.wait_ge(s_tfree[t % 2], t // 2)
                return bank[4 + t % 2]

            def token_major(n, f, src):
                w = weight(n)
                out = take(f)
                for k in range(KC):
                    mm = nc.tensor.matmul(out[:, 0:WC], src[:, k, :], w[:, k, :], start=(k == 0), stop=(k == KC - 1))
                mm.then_inc(s_full[f % 4], 1)
                return mm

            def channel_major(n, f, src, N):
                w = weight(n)
                for j in range(2):
                    out = take(f + j)
                    for k in range(KC):
                        mm = nc.tensor.matmul(out[:, 0:N], w[:, k, j * P:(j + 1) * P], src[:, k, :],
                                              start=(k == 0), stop=(k == KC - 1))
                    mm.then_inc(s_full[(f + j) % 4], 1)

            def turn_four(t, blocks):
                out = take_turn(t)
                for j, b in enumerate(blocks):
                    mm = nc.tensor.transpose(out[0:b.shape[1], j * P:j * P + b.shape[0]], b, ident[0:b.shape[0], 0:b.shape[0]])
                mm.then_inc(s_tfull[t % 2], 1)

            pe.wait_ge(s_const, NCONST)
            pe.wait_ge(s_silu, 1)
            for t in range(2):
                out = take_turn(t)
                for j in range(4):
                    k = 4 * t + j
                    mm = nc.tensor.transpose(out[:, j * NG:(j + 1) * NG], c9[:, k * P:(k + 1) * P], ident[0:NG, 0:NG])
                mm.then_inc(s_tfull[t], 1)
            pe.wait_ge(s_tfree[0], 1)
            pe.wait_ge(s_tfree[1], 1)
            for n in range(NADA):
                w = weight(n)
                out = take(n)
                for k in range(KC):
                    mm = nc.tensor.matmul(out[0:NG, 0:WC], cT[:, k, :], w[:, k, :], start=(k == 0), stop=(k == KC - 1))
                mm.then_inc(s_full[n % 4], 1)
            pe.wait_ge(s_small, 16 * 20)
            pe.wait_ge(s_wss, 16 * (P // DSEQ))
            for half in range(2):
                turn_four(2 + half, [ws_nat[:, 4 * half + j, :] for j in range(4)])
            for half in range(2):
                turn_four(4 + half, [wss_nat[:, 4 * half + j, :] for j in range(4)])
            for a in range(2):
                turn_four(6 + a, [sk_nat[:, a, :]])

            heads = 0
            for g, tiles in enumerate(GROUPS):
                T, N = len(tiles), width(g)
                before = sum(len(GROUPS[j]) for j in range(g))
                for i in range(T):
                    pe.wait_ge(s_n1h, before + i + 1)
                    for half in range(2):
                        x = vv[:, slot_of(g, i), :]
                        turn_four(turn_base(g, "norm1") + 2 * i + half,
                                  [x[:, (4 * half + j) * P:(4 * half + j + 1) * P] for j in range(4)])
                pe.wait_ge(s_hTe, 2 * (2 * before + T))
                h = hT(g)
                for c in range(4):
                    channel_major(chunk_base(g, "q") + c, fill_base(g, "q") + 2 * c, h, N)
                for c in range(4):
                    n = chunk_base(g, "k") + c
                    for i in range(T):
                        token_major(n, fill_base(g, "k") + c * T + i, h[:, :, i * P:(i + 1) * P])
                    if c:
                        pe.wait_ge(s_k, 4 * before + c * T)
                        for i in range(T):
                            turn_four(turn_base(g, "kT") + (c - 1) * T + i,
                                      [gvt(i)[:, (2 * (c - 1) + j) * P:(2 * (c - 1) + j + 1) * P] for j in range(2)])
                for c in range(4):
                    n = chunk_base(g, "v") + c
                    for i in range(T):
                        token_major(n, fill_base(g, "v") + c * T + i, h[:, :, i * P:(i + 1) * P])
                    if c == 0:
                        pe.wait_ge(s_k, 4 * (before + T))
                        for i in range(T):
                            turn_four(turn_base(g, "kT") + 3 * T + i,
                                      [gvt(i)[:, (6 + j) * P:(7 + j) * P] for j in range(2)])
                for b in range(2):
                    pe.wait_ge(s_tfree[b], turn_base(g, "gate") // 2)
                pe.wait_ge(s_v, 4 * (before + T))
                q = qT(g)

                def scores(n, i, t, hd):
                    if n >= 2:
                        pe.wait_ge(s_azb, n - 1)
                    for kb in range(t + 1):
                        mm = nc.tensor.matmul(bank[6 + n % 2][:, kb * P:(kb + 1) * P], kT[:, kb, hd, :],
                                              q[:, hd, i * P:(i + 1) * P], start=True, stop=True)
                    mm.then_inc(s_az, 1)

                def later_sums(n, t):
                    pe.wait_ge(s_as, n + 1)
                    if n:
                        pe.wait_ge(s_ad, n)
                    for kb in range(t + 1):
                        own = masked(n) if kb == t else att("s", n)[:, kb * P:(kb + 1) * P]
                        mm = nc.tensor.matmul(bank[4][:, kb * P:(kb + 1) * P], later[:], own, start=True, stop=(kb == t))
                        for k2 in range(kb + 1, t + 1):
                            part = masked(n) if k2 == t else att("s", n)[:, k2 * P:(k2 + 1) * P]
                            mm = nc.tensor.matmul(bank[4][:, kb * P:(kb + 1) * P], ones[:], part,
                                                  start=False, stop=(k2 == t))
                    mm.then_inc(s_ac, 1)

                def outputs(n, t, hd):
                    pe.wait_ge(s_am, n + 1)
                    if n:
                        pe.wait_ge(s_ae, n)
                    for kb in range(t + 1):
                        mm = nc.tensor.matmul(bank[5][:, 0:P], vv[:, kb, hd * P:(hd + 1) * P],
                                              att("e", n)[:, kb * P:(kb + 1) * P], start=(kb == 0), stop=(kb == t))
                    mm.then_inc(s_ao, 1)

                work = [(i, t, hd) for i, t in enumerate(tiles) if t != SAMPLE for hd in range(NH)]
                scores(heads, *work[0])
                for w, (i, t, hd) in enumerate(work):
                    if w + 1 < len(work):
                        scores(heads + w + 1, *work[w + 1])
                    later_sums(heads + w, t)
                    outputs(heads + w, t, hd)
                heads += len(work)
                pe.wait_ge(s_ae, heads)
                pe.wait_ge(s_azb, heads)

                if g == 0:
                    pe.wait_ge(s_free[0], fill_base(g, "u") // 4)
                    pe.wait_ge(s_free[1], fill_base(g, "u") // 4)
                    pe.wait_ge(s_free[2], fill_base(g, "u") // 4)
                    pe.wait_ge(s_free[3], fill_base(g, "u") // 4)
                    for hd in range(NH):
                        nc.tensor.matmul(bank[0][0:NS, hd * NS:(hd + 1) * NS], kT[:, 1, hd, 0:NS],
                                         q[:, hd, P:P + NS], start=True, stop=True)
                    for m in range(2 * NDEC):
                        b, page = m // 2, m % 2
                        pe.wait_ge(s_page[m % 4], 16 * (m // 4 + 1))
                        for half in range(2):
                            if m:
                                pe.wait_ge(s_kte, 2 * m - 1 + half)
                            for j in range(4):
                                mm = nc.tensor.transpose(bank[4 + half][:, j * P:(j + 1) * P],
                                                         ring[:, m % 4, (4 * half + j) * P:(4 * half + j + 1) * P], ident[:])
                            mm.then_inc(s_ktf[half], 1)
                        nc.tensor.drain().then_inc(s_pused, 1)
                        pe.wait_ge(s_kte, 2 * m + 2)
                        for hd in range(NH):
                            at = hd * NS + b * DSEQ
                            mm = nc.tensor.matmul(bank[6 + page][:, at:at + DSEQ],
                                                  ring[:, 4 + m % 2, hd * P:(hd + 1) * P],
                                                  q[:, hd, P + b * DSEQ:P + (b + 1) * DSEQ], start=True, stop=True)
                        mm.then_inc(s_sz, 1)
                    pe.wait_ge(s_ss, 1)
                    nc.tensor.matmul(bank[3][0:NS, :], later[0:NS, 0:NS], smS, start=True, stop=True)
                    nc.tensor.matmul(bank[2][:, :], later[:], sS[1], start=True, stop=False)
                    nc.tensor.matmul(bank[2][:, :], ones[0:NS, :], smS, start=False, stop=True)
                    nc.tensor.matmul(bank[1][:, :], later[:], sS[0], start=True, stop=False)
                    nc.tensor.matmul(bank[1][:, :], ones[:], sS[1], start=False, stop=False)
                    nc.tensor.matmul(bank[1][:, :], ones[0:NS, :], smS, start=False, stop=True).then_inc(s_scm, 1)
                    pe.wait_ge(s_sm, 1)
                    for b in range(NDEC):
                        m0 = 2 * NDEC + 2 * b
                        for page in range(2):
                            m = m0 + page
                            pe.wait_ge(s_page[m % 4], 16 * (m // 4 + 1))
                        for hd in range(NH):
                            at = slice(hd * NS + b * DSEQ, hd * NS + (b + 1) * DSEQ)
                            nc.tensor.matmul(bank[4][:, at], vv[0:NS, 1, hd * P:(hd + 1) * P], eS[2][:, at],
                                             start=True, stop=False)
                            for page in range(2):
                                mm = nc.tensor.matmul(bank[4][:, at], ring[:, (m0 + page) % 4, hd * P:(hd + 1) * P],
                                                      eS[page][:, at], start=False, stop=(page == 1))
                        mm.then_inc(s_pused, 2)
                    nc.tensor.drain().then_inc(s_so, 1)
                    pe.wait_ge(s_se, 1)
                    pe.wait_ge(s_sd, 1)

                for c in range(4):
                    channel_major(chunk_base(g, "u") + c, fill_base(g, "u") + 2 * c, h, N)
                for c in range(4):
                    n = chunk_base(g, "gv") + c
                    for i in range(T):
                        token_major(n, fill_base(g, "gv") + c * T + i, h[:, :, i * P:(i + 1) * P])
                for i, t in enumerate(tiles):
                    pe.wait_ge(s_lnh, before + i + 1)
                    mix = WsTs if t == SAMPLE else WsT
                    for half in range(2):
                        f = turn_base(g, "gate") + 2 * i + half
                        out = take_turn(f)
                        for j in range(4):
                            gr = 4 * half + j
                            mm = nc.tensor.matmul(out[:, j * P:(j + 1) * P], gvt(i)[:, gr * P:(gr + 1) * P], mix[:, gr, :],
                                                  start=True, stop=True)
                        mm.then_inc(s_tfull[f % 2], 1)
                pe.wait_ge(s_gate, 2 * (before + T))
                u = uT(g)
                for j in range(4):
                    n, f = chunk_base(g, "merge") + 4 * j, fill_base(g, "merge") + 8 * j
                    channel_major(n, f, h, N)
                    channel_major(n + 1, f + 2, u, N)
                    channel_major(n + 2, f + 4, h, N)
                    channel_major(n + 3, f + 6, q, N)
                pe.wait_ge(s_mrg, 16 * (g + 1))
                m = mT(g)
                for c in range(4):
                    n = chunk_base(g, "out") + c
                    for i in range(T):
                        token_major(n, fill_base(g, "out") + c * T + i, m[:, :, i * P:(i + 1) * P])
                for i in range(T):
                    pe.wait_ge(s_n2h, before + i + 1)
                    for half in range(2):
                        turn_four(turn_base(g, "norm2") + 2 * i + half,
                                  [h2(g, i)[:, (4 * half + j) * P:(4 * half + j + 1) * P] for j in range(4)])
                pe.wait_ge(s_hTe, 2 * (2 * before + 2 * T))
                def key_scores(c):
                    pe.wait_ge(s_qh, 2 * (8 * g + c + 1))
                    for i in range(T):
                        if c or g:
                            done = c + (8 * g if i < 2 else 0)
                            if done:
                                pe.wait_ge(s_sev[i], done)
                        for a in range(2):
                            mm = nc.tensor.matmul(bank[5 + i][:, a * NKEY:(a + 1) * NKEY], qh[:, c % 2, a, i * P:(i + 1) * P],
                                                  skT[:, a, :], start=True, stop=True)
                        mm.then_inc(s_sfull[i], 1)
                for c in range(NH):
                    channel_major(chunk_base(g, "query") + c, fill_base(g, "query") + 2 * c, h, N)
                    if c:
                        key_scores(c - 1)
                key_scores(NH - 1)
                for i in range(T):
                    pe.wait_ge(s_sev[i], NH * (g + 1) if i < 2 else NH)

        @block.scalar
        def _(act):
            def read(f):
                act.wait_ge(s_full[f % 4], f // 4 + 1)
                return bank[f % 4]

            def read_turn(t):
                act.wait_ge(s_tfull[t % 2], t // 2 + 1)
                return bank[4 + t % 2]

            def root(wait, n, signal, col):
                act.wait_ge(wait, n)
                nc.scalar.activation(st[:, col + 1:col + 2], st[:, col:col + 1], ACT.Sqrt).then_inc(signal, 1)

            act.wait_ge(s_cond, 16 * 5)
            nc.scalar.activation(c9, c9, ACT.Silu).then_inc(s_silu, 1)
            for t in range(2):
                out = read_turn(t)
                nc.scalar.copy(cT[:, 4 * t:4 * t + 4, :].rearrange("p k r -> p (k r)"), out[:, 0:4 * NG]).then_inc(s_tfree[t], 1)
            for a in range(2):
                f = 6 + a
                nc.scalar.copy(skT[:, a, :], read_turn(f)[:, 0:NKEY]).then_inc(s_tfree[f % 2], 1)

            heads = 0
            sig = 0
            for g, tiles in enumerate(GROUPS):
                T, N = len(tiles), width(g)
                before = sum(len(GROUPS[j]) for j in range(g))

                def transposed(phase, i):
                    for half in range(2):
                        f = turn_base(g, phase) + 2 * i + half
                        src = read_turn(f)[:, :].rearrange("p (j n) -> p j n", j=4)
                        nc.scalar.copy(hT(g)[:, 4 * half:4 * half + 4, i * P:(i + 1) * P], src).then_inc(s_hTe, 1)
                        nc.scalar.drain().then_inc(s_tfree[f % 2], 1)

                for i in range(T):
                    root(s_n1v, before + i + 1, s_n1s, 0)
                for i in range(T):
                    transposed("norm1", i)
                for j in range(NH):
                    f = fill_base(g, "q") + j
                    nc.scalar.copy(qT(g)[:, j, :], read(f)[:, 0:N]).then_inc(s_free[f % 4], 1)

                def keys_turned(c):
                    for i in range(T):
                        f = turn_base(g, "kT") + c * T + i
                        nc.scalar.copy(kT[:, slot_of(g, i), 2 * c:2 * c + 2, :].rearrange("p h n -> p (h n)"),
                                       read_turn(f)[:, 0:2 * P]).then_inc(s_tfree[f % 2], 1)
                for c in range(4):
                    for i in range(T):
                        f = fill_base(g, "k") + c * T + i
                        nc.scalar.copy(gvt(i)[:, c * WC:(c + 1) * WC], read(f)[:, 0:WC]).then_inc(s_k, 1)
                        nc.scalar.drain().then_inc(s_free[f % 4], 1)
                    if c:
                        keys_turned(c - 1)
                for c in range(4):
                    for i in range(T):
                        f = fill_base(g, "v") + c * T + i
                        nc.scalar.copy(vv[:, slot_of(g, i), c * WC:(c + 1) * WC], read(f)[:, 0:WC]).then_inc(s_v, 1)
                        nc.scalar.drain().then_inc(s_free[f % 4], 1)
                    if c == 0:
                        keys_turned(3)
                work = [(i, t, hd) for i, t in enumerate(tiles) if t != SAMPLE for hd in range(NH)]

                def log_part(n, t):
                    cols = (t + 1) * P
                    act.wait_ge(s_azb, n + 1)
                    if n >= 2:
                        act.wait_ge(s_ao, n - 1)
                    e = att("e", n)[:, 0:cols]
                    nc.scalar.activation(e, att("z", n)[:, 0:cols], ACT.Abs)
                    act.drain()
                    nc.scalar.activation(e, e, ACT.Exp, scale=-1.0)
                    act.drain()
                    nc.scalar.activation(e, e, ACT.Ln, bias=1.0).then_inc(s_al, 1)

                log_part(heads, work[0][1])
                for w, (i, t, hd) in enumerate(work):
                    n = heads + w
                    cols = (t + 1) * P
                    if w + 1 < len(work):
                        log_part(n + 1, work[w + 1][1])
                    act.wait_ge(s_ad, n + 1)
                    nc.scalar.activation(att("e", n)[:, 0:cols], att("z", n)[:, 0:cols], ACT.Exp).then_inc(s_aw, 1)
                    act.wait_ge(s_ao, n + 1)
                    nc.scalar.copy(qT(g)[:, hd, i * P:(i + 1) * P], bank[5][:, 0:P]).then_inc(s_ae, 1)
                heads += len(work)
                if g == 0:
                    for m in range(2 * NDEC):
                        if m >= 2:
                            act.wait_ge(s_sz, m - 1)
                        for half in range(2):
                            act.wait_ge(s_ktf[half], m + 1)
                            nc.scalar.copy(ring[:, 4 + m % 2, half * 512:(half + 1) * 512], bank[4 + half][:, :]).then_inc(s_kte, 1)
                    act.wait_ge(s_szb, 1)
                    for part in range(3):
                        nc.scalar.activation(eS[part], zS[part], ACT.Abs)
                    act.drain()
                    for part in range(3):
                        nc.scalar.activation(eS[part], eS[part], ACT.Exp, scale=-1.0)
                    act.drain()
                    for part in range(3):
                        ins = nc.scalar.activation(eS[part], eS[part], ACT.Ln, bias=1.0)
                    ins.then_inc(s_sl, 1)
                    act.wait_ge(s_sd, 1)
                    for part in range(3):
                        ins = nc.scalar.activation(eS[part], zS[part], ACT.Exp)
                    ins.then_inc(s_sw, 1)
                    act.wait_ge(s_so, 1)
                    src = bank[4][:, :].rearrange("p (h n) -> p h n", h=NH)
                    nc.scalar.copy(qT(g)[:, :, P:P + NS], src)
                    nc.scalar.copy(qT(g)[:, :, P + NS:2 * P], src).then_inc(s_se, 1)
                act.wait_ge(s_kst, 16 * (before + T))
                for j in range(NH):
                    f = fill_base(g, "u") + j
                    nc.scalar.activation(uT(g)[:, j, :], read(f)[:, 0:N], ACT.Gelu).then_inc(s_free[f % 4], 1)
                for c in range(4):
                    for i in range(T):
                        f = fill_base(g, "gv") + c * T + i
                        nc.scalar.activation(gvt(i)[:, c * WC:(c + 1) * WC], read(f)[:, 0:WC], ACT.Gelu).then_inc(s_gv, 1)
                        nc.scalar.drain().then_inc(s_free[f % 4], 1)
                for i in range(T):
                    root(s_lnv, before + i + 1, s_lns, 4)
                for j in range(4):
                    for which in range(2):
                        f = fill_base(g, "merge") + 8 * j + 4 * which
                        for b in range(2):
                            if sig >= 4:
                                act.wait_ge(s_mrg, sig // 2 - 1)
                            nc.scalar.activation(sg[:, 2 * which + b, 0:N], read(f + b)[:, 0:N], ACT.Sigmoid).then_inc(s_sga, 1)
                            nc.scalar.drain().then_inc(s_free[(f + b) % 4], 1)
                            sig += 1
                for i in range(T):
                    root(s_n2v, before + i + 1, s_n2s, 8)
                for i in range(T):
                    transposed("norm2", i)

                def scores_out(c):
                    for i in range(T):
                        done = c + (8 * g if i < 2 else 0)
                        act.wait_ge(s_sfull[i], done + 1)
                        if done:
                            act.wait_ge(s_tk[i], done)
                        nc.scalar.copy(sc[:, i].rearrange("p a k -> p (a k)"), bank[5 + i][:, 0:2 * NKEY]).then_inc(s_sev[i], 1)
                for c in range(NH):
                    for a in range(2):
                        f = fill_base(g, "query") + 2 * c + a
                        if c >= 2:
                            for i in range(T):
                                act.wait_ge(s_sfull[i], c - 1 + (8 * g if i < 2 else 0))
                        nc.scalar.copy(qh[:, c % 2, a, 0:N], read(f)[:, 0:N]).then_inc(s_qh, 1)
                        nc.scalar.drain().then_inc(s_free[f % 4], 1)
                    if c:
                        scores_out(c - 1)
                scores_out(NH - 1)
                for i in range(T):
                    act.wait_ge(s_nb, before + i + 1)
                    nc.scalar.activation(chosen[:, i, 0, :], chosen[:, i, 0, :], ACT.Exp).then_inc(s_ex, 1)

            first = 0
            for order, t in enumerate(ORDER):
                with act.Fori(0, STEPS[t]) as h:
                    act.wait_ge(s_dots, h + (first + 1))
                    act.wait_ge(s_coef, h + first)
                    nc.scalar.activation(acts[:], dots[:], ACT.Gelu).then_inc(s_acts, 1)
                first += STEPS[t]
                root(s_fv, order + 1, s_fs, 12)
                act.wait_ge(s_fy, order + 1)
                dst = ys if t == SAMPLE else yp[t]
                act.dma_start(dst, acc[0:dst.shape[0], 0, :]).then_inc(s_y, 16)

        @block.vector
        def _(dve):
            scored = [dve.alloc_register(f"scores_of_tile_{i}") for i in range(3)]

            def read(f):
                dve.wait_ge(s_full[f % 4], f // 4 + 1)
                return bank[f % 4]

            def read_turn(t):
                dve.wait_ge(s_tfull[t % 2], t // 2 + 1)
                return bank[4 + t % 2]

            def table(g, what, kind):
                n = table_number(g, what, kind)
                dve.wait_ge(s_tab[n % 3], 32 * (n // 3 + 1))
                return tab[:, n % 3, :]

            def mean_square(src, col, signal):
                nc.vector.tensor_tensor_reduce(out=junk[:], in0=src, in1=src, scale=1.0, scalar=0.0,
                                               op0=ALU.mult, op1=ALU.add, accum_out=st[:, col:col + 1])
                dve.drain()
                nc.vector.tensor_scalar(st[:, col:col + 1], st[:, col:col + 1], 1.0 / D, EPS, ALU.mult, ALU.add).then_inc(signal, 1)

            def reciprocal_root(wait, n, col):
                dve.wait_ge(wait, n)
                nc.vector.reciprocal(st[:, col + 2:col + 3], st[:, col + 1:col + 2])
                dve.drain()
                return st[:, col + 2:col + 3]

            dve.wait_ge(s_const, NCONST)
            nc.vector.memset(acc[0:1, 1, 0:1], 0.0).then_inc(s_zero, 1)
            dve.wait_ge(s_cond, 16 * 5)
            for n in range(NADA):
                m = mod9[:, n * WC:(n + 1) * WC]
                nc.vector.tensor_tensor(m, read(n)[0:NG, 0:WC], m, ALU.add).then_inc(s_mod, 1)
                nc.vector.drain().then_inc(s_free[n % 4], 1)
            dve.drain()
            for m, gain in ((1, g1row), (4, g2row)):
                row = mod9[:, m * D:(m + 1) * D]
                nc.vector.scalar_tensor_tensor(out=row, in0=row, scalar=1.0, in1=gain, op0=ALU.add,
                                               op1=ALU.mult).then_inc(s_mod, 1)
            for f, dst in ((2, WsT[:]), (4, WsTs)):
                for half in range(2):
                    src = read_turn(f + half)[:, :].rearrange("p (j n) -> p j n", j=4)
                    nc.vector.tensor_tensor(dst[:, 4 * half:4 * half + 4, :], src,
                                            causal.unsqueeze(1).broadcast_to([P, 4, P]), ALU.mult).then_inc(s_tfree[half], 1)

            heads = 0
            merged = 0
            for g, tiles in enumerate(GROUPS):
                T, N = len(tiles), width(g)
                before = sum(len(GROUPS[j]) for j in range(g))

                dve.wait_ge(s_x[g], 32 * T)
                for i, t in enumerate(tiles):
                    kind = "s" if t == SAMPLE else "p"
                    x = vv[:, slot_of(g, i), :]
                    mean_square(x, 0, s_n1v)
                    r = reciprocal_root(s_n1s, before + i + 1, 0)
                    nc.vector.scalar_tensor_tensor(out=x, in0=x, scalar=r, in1=table(g, "A1", kind), op0=ALU.mult, op1=ALU.mult)
                    dve.drain()
                    nc.vector.tensor_tensor(x, x, table(g, "B1", kind), ALU.add).then_inc(s_n1h, 1)
                    if g == 0 or i == T - 1:
                        nc.vector.drain().then_inc(s_tabfree, 2)

                work = [(i, t, hd) for i, t in enumerate(tiles) if t != SAMPLE for hd in range(NH)]
                def biased(n, t, hd):
                    cols = (t + 1) * P
                    dve.wait_ge(s_az, n + 1)
                    if n >= 2:
                        dve.wait_ge(s_aw, n - 1)
                    nc.vector.tensor_scalar(att("z", n)[:, 0:cols], bank[6 + n % 2][:, 0:cols], SCALE,
                                            bias_b[:, hd:hd + 1], ALU.mult, ALU.add).then_inc(s_azb, 1)

                biased(heads, *work[0][1:])
                for w, (i, t, hd) in enumerate(work):
                    n = heads + w
                    cols = (t + 1) * P
                    if w + 1 < len(work):
                        biased(n + 1, *work[w + 1][1:])
                    z, e, s = att("z", n)[:, 0:cols], att("e", n)[:, 0:cols], att("s", n)[:, 0:cols]
                    dve.wait_ge(s_al, n + 1)
                    if n >= 2:
                        dve.wait_ge(s_ac, n - 1)
                    nc.vector.scalar_tensor_tensor(out=s, in0=z, scalar=0.0, in1=e, op0=ALU.max, op1=ALU.add)
                    dve.drain()
                    nc.vector.tensor_tensor(masked(n), s[:, t * P:cols], strict[:], ALU.mult)
                    nc.vector.tensor_tensor(z, z, s, ALU.subtract).then_inc(s_as, 1)
                    dve.wait_ge(s_as, n + 1)
                    dve.wait_ge(s_ac, n + 1)
                    nc.vector.tensor_tensor(z, z, bank[4][:, 0:cols], ALU.subtract).then_inc(s_ad, 1)
                    dve.wait_ge(s_aw, n + 1)
                    nc.vector.tensor_tensor(e[:, t * P:cols], e[:, t * P:cols], strict[:], ALU.mult).then_inc(s_am, 1)
                heads += len(work)

                if g == 0:
                    dve.wait_ge(s_sz, 2 * NDEC)
                    bias = bias_b[:].unsqueeze(2).broadcast_to([P, NH, NS])
                    for part, src in ((0, bank[6]), (1, bank[7]), (2, bank[0])):
                        rows = NS if part == 2 else P
                        ins = nc.vector.scalar_tensor_tensor(
                            out=zS[part].rearrange("p (h n) -> p h n", h=NH),
                            in0=src[0:rows, :].rearrange("p (h n) -> p h n", h=NH), scalar=SCALE,
                            in1=bias[0:rows], op0=ALU.mult, op1=ALU.add)
                    ins.then_inc(s_szb, 1)
                    own = ownseq[:].unsqueeze(1).broadcast_to([NS, NH, NS])
                    dve.wait_ge(s_sl, 1)
                    for part in range(3):
                        nc.vector.scalar_tensor_tensor(out=sS[part], in0=zS[part], scalar=0.0, in1=eS[part],
                                                       op0=ALU.max, op1=ALU.add)
                    dve.drain()
                    nc.vector.tensor_tensor(smS.rearrange("p (h n) -> p h n", h=NH),
                                            sS[2].rearrange("p (h n) -> p h n", h=NH), own, ALU.mult)
                    for part in range(3):
                        ins = nc.vector.tensor_tensor(zS[part], zS[part], sS[part], ALU.subtract)
                    ins.then_inc(s_ss, 1)
                    dve.wait_ge(s_ss, 1)
                    dve.wait_ge(s_scm, 1)
                    for part in range(3):
                        ins = nc.vector.tensor_tensor(zS[part], zS[part], bank[1 + part][0:zS[part].shape[0], :], ALU.subtract)
                    ins.then_inc(s_sd, 1)
                    dve.wait_ge(s_sw, 1)
                    w2 = eS[2].rearrange("p (h n) -> p h n", h=NH)
                    nc.vector.tensor_tensor(w2, w2, own, ALU.mult).then_inc(s_sm, 1)

                gain, shift = None, None
                for i, t in enumerate(tiles):
                    dve.wait_ge(s_gv, 4 * (before + T))
                    x = gvt(i)
                    nc.vector.tensor_reduce(st[:, 7:8], x, AX.X, ALU.add)
                    dve.drain()
                    nc.vector.tensor_scalar(st[:, 7:8], st[:, 7:8], -1.0 / D, None, ALU.mult)
                    dve.drain()
                    nc.vector.tensor_scalar(x, x, st[:, 7:8], None, ALU.add)
                    dve.drain()
                    mean_square(x, 4, s_lnv)
                    r = reciprocal_root(s_lns, before + i + 1, 4)
                    nc.vector.scalar_tensor_tensor(out=x, in0=x, scalar=r, in1=table(g, "gv", ""), op0=ALU.mult, op1=ALU.mult)
                    dve.drain()
                    nc.vector.tensor_tensor(x, x, table(g, "bv", ""), ALU.add).then_inc(s_lnh, 1)
                nc.vector.drain().then_inc(s_tabfree, 2)
                for i, t in enumerate(tiles):
                    bs = bsbs if t == SAMPLE else bsb[:]
                    for half in range(2):
                        f = turn_base(g, "gate") + 2 * i + half
                        src = read_turn(f)[:, :].rearrange("p (j n) -> p j n", j=4)
                        mixed = junk[:, half * 512:(half + 1) * 512].rearrange("p (j n) -> p j n", j=4)
                        uu = uT(g)[:, 4 * half:4 * half + 4, i * P:(i + 1) * P]
                        nc.vector.tensor_tensor(mixed, src, bs[:, 4 * half:4 * half + 4, :], ALU.add)
                        dve.drain()
                        nc.vector.tensor_tensor(uu, uu, mixed, ALU.mult).then_inc(s_gate, 1)
                        nc.vector.drain().then_inc(s_tfree[f % 2], 1)

                if g == 0:
                    dve.wait_ge(s_gvst, 16)
                m = mT(g)
                for j in range(4):
                    for which in range(2):
                        f = fill_base(g, "merge") + 8 * j + 4 * which + 2
                        for b in range(2):
                            merged += 1
                            dve.wait_ge(s_sga, merged)
                            s = sg[:, 2 * which + b, 0:N]
                            src = read(f + b)[:, 0:N]
                            if which == 0:
                                ins = nc.vector.tensor_tensor(m[:, 2 * j + b, :], src, s, ALU.mult)
                            else:
                                nc.vector.tensor_tensor(s, src, s, ALU.mult)
                                dve.drain()
                                ins = nc.vector.tensor_tensor(m[:, 2 * j + b, :], m[:, 2 * j + b, :], s, ALU.add)
                            ins.then_inc(s_free[(f + b) % 4], 1)
                        nc.vector.drain().then_inc(s_mrg, 2)

                dve.wait_ge(s_xr[g], 32 * T)
                for c in range(4):
                    for i, t in enumerate(tiles):
                        f = fill_base(g, "out") + c * T + i
                        cols = slice(c * WC, (c + 1) * WC)
                        part = junk[:, (f % 2) * 512:(f % 2) * 512 + WC]
                        gate = table(g, "G1", "s" if t == SAMPLE else "p")
                        nc.vector.tensor_tensor(part, read(f)[:, 0:WC], gate[:, cols], ALU.mult)
                        dve.drain()
                        x = vv[:, xslot_of(g, i), cols]
                        ins = nc.vector.tensor_tensor(x, x, part, ALU.add)
                        ins.then_inc(s_free[f % 4], 1)
                nc.vector.drain().then_inc(s_tabfree, 2 if g == 0 else 1)
                nc.vector.drain().then_inc(s_x1, T)

                for i, t in enumerate(tiles):
                    kind = "s" if t == SAMPLE else "p"
                    x, out = vv[:, xslot_of(g, i), :], h2(g, i)
                    mean_square(x, 8, s_n2v)
                    r = reciprocal_root(s_n2s, before + i + 1, 8)
                    nc.vector.scalar_tensor_tensor(out=out, in0=x, scalar=r, in1=table(g, "A2", kind), op0=ALU.mult, op1=ALU.mult)
                    dve.drain()
                    nc.vector.tensor_tensor(out, out, table(g, "B2", kind), ALU.add).then_inc(s_n2h, 1)
                    if g == 0 or i == T - 1:
                        nc.vector.drain().then_inc(s_tabfree, 2)

                def top16(src, work, vals, idx):
                    nc.vector.max(vals[:, 0:8], src)
                    dve.drain()
                    nc.vector.max_index(idx[:, 0:8], vals[:, 0:8], src)
                    nc.vector.match_replace(work, vals[:, 0:8], src, LOWEST)
                    dve.drain()
                    nc.vector.max(vals[:, 8:16], work)
                    dve.drain()
                    nc.vector.max_index(idx[:, 8:16], vals[:, 8:16], work)

                for i in range(T):
                    dve.reg_mov(scored[i], NH * g if i < 2 else 0)
                with dve.Fori(0, NH) as hd:
                    for i in range(T):
                        dve.reg_add(scored[i], scored[i], 1)
                        dve.wait_ge(s_const, NCONST)
                        dve.wait_ge(s_sev[i], scored[i])
                        for a in range(2):
                            top16(sc[:, i, a, :], sc2[:, a, :], tk_m[:, a, :], tk_i[:, a, :])
                        dve.drain()
                        nc.vector.tensor_copy(chosen[:, i, 3:5, bass.ds(hd * TOPK, TOPK)], tk_i[:])
                        nc.vector.tensor_tensor(cand.rearrange("p (a b) -> p a b", a=TOPK),
                                                tk_m[:, 0, :].unsqueeze(2).broadcast_to([P, TOPK, TOPK]),
                                                tk_m[:, 1, :].unsqueeze(1).broadcast_to([P, TOPK, TOPK]),
                                                ALU.add).then_inc(s_tk[i], 1)
                        dve.drain()
                        top16(cand, cand2, tk_m[:, 0, :], tk_b[:])
                        dve.drain()
                        nc.vector.tensor_copy(chosen[:, i, 0, bass.ds(hd * TOPK, TOPK)], tk_m[:, 0, :])
                        nc.vector.tensor_scalar(tk_hl[:, 0, :], tk_b[:], 4, None, ALU.logical_shift_right)
                        nc.vector.tensor_scalar(tk_hl[:, 1, :], tk_b[:], TOPK - 1, None, ALU.bitwise_and)
                        dve.drain()
                        nc.vector.tensor_copy(chosen[:, i, 1:3, bass.ds(hd * TOPK, TOPK)], tk_hl[:])
                        dve.drain()
                for i, t in enumerate(tiles):
                    for a in range(2):
                        for part in range(2):
                            heads4 = slice(part * 64, (part + 1) * 64)
                            hot = onehot.rearrange("p (j r) -> p j r", r=TOPK)
                            hot4 = onehot.rearrange("p (h j r) -> p h j r", h=4, r=TOPK)
                            place = chosen[:, i, 1 + a, heads4]
                            nc.vector.tensor_tensor(hot, place.unsqueeze(2).broadcast_to([P, 64, TOPK]),
                                                    iota_f[:].unsqueeze(1).broadcast_to([P, 64, TOPK]), ALU.is_equal)
                            dve.drain()
                            keys = chosen[:, i, 3 + a, heads4].rearrange("p (h r) -> p h r", h=4)
                            nc.vector.tensor_tensor(hot4, hot4, keys.unsqueeze(2).broadcast_to([P, 4, TOPK, TOPK]), ALU.mult)
                            dve.drain()
                            nc.vector.tensor_reduce(place, hot, AX.X, ALU.add)
                            dve.drain()
                    e = chosen[:, i, 1, :]
                    nc.vector.scalar_tensor_tensor(out=e, in0=e, scalar=float(NKEY), in1=chosen[:, i, 2, :],
                                                   op0=ALU.mult, op1=ALU.add)
                    best = chosen[:, i, 0, :].rearrange("p (h k) -> p h k", h=NH)
                    nc.vector.tensor_copy(sm[:, 0, :], best[:, :, 0])
                    dve.drain()
                    nc.vector.tensor_tensor(best, best, sm[:, 0, :].unsqueeze(2).broadcast_to([P, NH, TOPK]),
                                            ALU.subtract).then_inc(s_nb, 1)
                    dve.wait_ge(s_ex, before + i + 1)
                    nc.vector.tensor_reduce(sm[:, 0, :], best, AX.X, ALU.add)
                    dve.drain()
                    nc.vector.reciprocal(sm[:, 1, :], sm[:, 0, :])
                    dve.drain()
                    nc.vector.tensor_tensor(best, best, sm[:, 1, :].unsqueeze(2).broadcast_to([P, NH, TOPK]), ALU.mult)
                    dve.drain()
                    if t == SAMPLE:
                        for half in range(2):
                            rows = slice(half * NS, (half + 1) * NS)
                            for src, dst in ((chosen[rows, i, 1, :], expert[rows, t, 0:P // 2]),
                                             (chosen[rows, i, 0, :], gates[rows, t, 0:P // 2])):
                                nc.vector.tensor_copy(dst, src.rearrange("p (k two) -> p k two", two=2)[:, :, half])
                    else:
                        nc.vector.tensor_copy(expert[:, t, :], chosen[:, i, 1, :])
                        nc.vector.tensor_copy(gates[:, t, :], chosen[:, i, 0, :])
                    dve.drain()

            nc.vector.drain().then_inc(s_slot, SLOTS)
            where = {t: (g, i) for g, ts in enumerate(GROUPS) for i, t in enumerate(ts)}

            def stage_rows(which, t, h, signal):
                nc.vector.tensor_copy(stage[:, which, :], expert[:, t, bass.ds(h * TOPK, TOPK)]).then_inc(signal, 1)

            def dot_step(x, used):
                for k in range(TOPK):
                    row = ring[:, k % SLOTS, :]
                    dve.wait_ge(s_gath[k % SLOTS], used * 32 + 16 * (k // SLOTS + 1))
                    nc.vector.tensor_tensor_reduce(out=row, in0=row, in1=x, scale=1.0, scalar=0.0, op0=ALU.mult,
                                                   op1=ALU.add, accum_out=dots[:, k:k + 1]).then_inc(s_slot, 1)
                nc.vector.drain().then_inc(s_dots, 1)

            def sum_step(t, h, n, used):
                dve.wait_ge(s_acts, n + 1)
                nc.vector.tensor_tensor(coef[:], acts[:], gates[:, t, bass.ds(h * TOPK, TOPK)], ALU.mult).then_inc(s_coef, 1)
                dve.drain()
                for k in range(TOPK):
                    row = ring[:, k % SLOTS, :]
                    a = acc[:, k % 2, :]
                    dve.wait_ge(s_gath[k % SLOTS], used * 32 + 16 * (k // SLOTS + 1))
                    nc.vector.scalar_tensor_tensor(out=a, in0=row, scalar=coef[:, k:k + 1], in1=a, op0=ALU.mult,
                                                   op1=ALU.add).then_inc(s_slot, 1)
                    dve.drain()

            first = 0
            for order, t in enumerate(ORDER):
                H = STEPS[t]
                x = h2(*where[t])
                if order:
                    dve.wait_ge(s_y, 16 * order)
                nc.vector.memset(acc[:], 0.0)
                stage_rows(0, t, 0, s_dn)
                dot_step(x, 2 * first)
                stage_rows(1, t, 0, s_up)
                with dve.Fori(1, H) as h:
                    stage_rows(0, t, h, s_dn)
                    dve.wait_ge(s_acts, h + first)
                    dot_step(x, (h + first) * 2 - 1)
                    sum_step(t, h - 1, h + (first - 1), (h + first) * 2)
                    stage_rows(1, t, h, s_up)
                sum_step(t, H - 1, first + H - 1, 2 * (first + H) - 1)
                first += H
                total = acc[:, 0, :]
                nc.vector.tensor_tensor(total, total, acc[:, 1, :], ALU.add)
                dve.drain()
                dve.wait_ge(s_fin, 64 * (order + 1))
                if t == SAMPLE:
                    nc.vector.drain().then_inc(s_half, 1)
                    dve.wait_ge(s_fold, 16)
                    nc.vector.tensor_tensor(total[0:NS, :], total[0:NS, :], ring[0:NS, 3, :], ALU.add)
                    dve.drain()
                nc.vector.tensor_tensor(total, total, ring[:, 0, :], ALU.mult)
                dve.drain()
                nc.vector.tensor_tensor(total, total, ring[:, 2, :], ALU.add)
                dve.drain()
                mean_square(total, 12, s_fv)
                r = reciprocal_root(s_fs, order + 1, 12)
                nc.vector.scalar_tensor_tensor(out=total, in0=total, scalar=r, in1=ring[:, 1, :], op0=ALU.mult,
                                               op1=ALU.mult).then_inc(s_fy, 1)
                nc.vector.drain().then_inc(s_slot, SLOTS)


_OUTS = [((1, SEQ, D), "y_prompt"), ((NDEC, DSEQ, D), "y_sample"),
         ((1, 1, SEQ, NH, P), "new_k_prompt"), ((1, 1, SEQ, NH, P), "new_v_prompt"),
         ((1, NDEC, DSEQ, NH, P), "new_k_sample"), ((1, NDEC, DSEQ, NH, P), "new_v_sample"),
         ((1, NDEC, DSEQ, NH, P), "new_gmlp_v_sample")]
_INS = ["x_prompt", "x_sample", "cache_k", "cache_v", "page_table", "c_prompt", "c_sample", "w_ada", "b_ada",
        "g_norm1", "w_in", "sb_bias", "g_v", "b_v", "w_spatial", "b_spatial", "w_branch_a", "w_branch_b",
        "w_out", "g_norm2", "w_query", "sub_keys", "expert_down", "expert_up", "g_final"]


def kernel(**inputs):
    import concourse.bacc as bacc
    from concourse.bass_utils import run_bass_kernel_spmd

    nc = bacc.Bacc("TRN2", target_bir_lowering=False, num_devices=1)
    arrays, args = {}, []
    for name in _INS:
        a = np.ascontiguousarray(inputs[name])
        arrays[f"in_{name}"] = a
        args.append(nc.dram_tensor(f"in_{name}", a.shape, mybir.dt.from_np(a.dtype), kind="ExternalInput").ap())
    for shape, name in _OUTS:
        args.append(nc.dram_tensor(f"out_{name}", shape, F32, kind="ExternalOutput").ap())
    build(nc, *args)
    got = run_bass_kernel_spmd(nc, [arrays], core_ids=[0])
    return tuple(got.results[0][f"out_{name}"] for _, name in _OUTS)
```

```python
from contextlib import ExitStack

import numpy as np

import concourse.bass as bass
from concourse import mybir

ALU = mybir.AluOpType
ACT = mybir.ActivationFunctionType
AX = mybir.AxisListType
F32 = mybir.dt.float32
I32 = mybir.dt.int32
U32 = mybir.dt.uint32

P = 128
D = 1024
KC = D // P
WC = 256
NH = 8
SEQ, NDEC, DSEQ = 512, 8, 8
NS = NDEC * DSEQ
NG = 1 + NDEC
NMOD = 6
TOPK = 16
NKEY = 128
SCALE = float(P) ** -0.5
EPS = 1e-6
LOWEST = -3.0e38
MASKED = -1.0e30
SLOTS = 8
TILES = 5
SAMPLE = 4
GROUPS = [[0, SAMPLE], [1, 2, 3]]
NADA = NMOD * D // WC
NCH = 48

ORDER = [0, SAMPLE, 1, 2, 3]
STEPS = {0: 8, SAMPLE: 4, 1: 8, 2: 8, 3: 8}
FIRST = {t: sum(STEPS[o] for o in ORDER[:ORDER.index(t)]) for t in ORDER}
CHOOSING = {0: 0, 1: 1}
WOVEN = [0, SAMPLE]
DVE_PIECES = {0: [3, 0, 0, 0, 0, 0, 0, 0, 0], SAMPLE: [3, 5, 3, 5, 5]}
ACT_PIECES = {0: [3, 4, 4, 6, 6, 6, 6, 4, 3], SAMPLE: [3, 3, 3, 2, 3]}


def slot_of(g, i):
    return i if g == 0 else 1 + i


def xslot_of(g, i):
    return 2 + i if g == 0 else 1 + i


def fill_base(g, phase):
    t = len(GROUPS[g])
    base = NADA if g == 0 else NADA + 64 + 16 * len(GROUPS[0])
    return base + {"q": 0, "k": 8, "v": 8 + 4 * t, "u": 8 + 8 * t, "gv": 16 + 8 * t,
                   "merge": 16 + 12 * t, "out": 48 + 12 * t, "query": 48 + 16 * t}[phase]


def turn_base(g, phase):
    t = len(GROUPS[g])
    base = 8 if g == 0 else 8 + 10 * len(GROUPS[0])
    return base + {"norm1": 0, "kT": 2 * t, "gate": 6 * t, "norm2": 8 * t}[phase]


def chunk_base(g, phase):
    return NADA + NCH * g + {"q": 0, "k": 4, "v": 8, "u": 12, "gv": 16, "merge": 20, "out": 36, "query": 40}[phase]


def last_fill(n):
    if n < NADA:
        return n
    g, m = divmod(n - NADA, NCH)
    t = len(GROUPS[g])
    for phase, fills in (("query", 2), ("out", t), ("merge", 2), ("gv", t), ("u", 2), ("v", t), ("k", t), ("q", 2)):
        c = n - chunk_base(g, phase)
        if c >= 0:
            return fill_base(g, phase) + fills * (c + 1) - 1


def tables(g):
    if g == 0:
        return [("A1", "p"), ("B1", "p"), ("A1", "s"), ("B1", "s"), ("gv", ""), ("bv", ""),
                ("G1", "p"), ("G1", "s"), ("A2", "p"), ("B2", "p"), ("A2", "s"), ("B2", "s")]
    return [("A1", "p"), ("B1", "p"), ("gv", ""), ("bv", ""), ("G1", "p"), ("A2", "p"), ("B2", "p")]


def table_number(g, what, kind):
    return (len(tables(0)) if g else 0) + tables(g).index((what, kind))


def build(nc, x_prompt, x_sample, cache_k, cache_v, page_table, c_prompt, c_sample, w_ada, b_ada,
          g_norm1, w_in, sb_bias, g_v, b_v, w_spatial, b_spatial, w_branch_a, w_branch_b, w_out,
          g_norm2, w_query, sub_keys, expert_down, expert_up, g_final,
          y_prompt, y_sample, nk_prompt, nv_prompt, nk_sample, nv_sample, ngv_sample):
    n_phys = cache_k.shape[1]
    xp = x_prompt.rearrange("b (t p) d -> (b t) p d", p=P)
    xs = x_sample.rearrange("b i d -> (b i) d")
    kpages = cache_k.rearrange("l n p h d -> (l n p) (h d)")
    vpages = cache_v.rearrange("l n p h d -> (l n p) (h d)")
    yp = y_prompt.rearrange("b (t p) d -> (b t) p d", p=P)
    ys = y_sample.rearrange("b i d -> (b i) d")
    nkp = nk_prompt.rearrange("l b (t p) h d -> (l b t) p (h d)", p=P)
    nvp = nv_prompt.rearrange("l b (t p) h d -> (l b t) p (h d)", p=P)
    nks = nk_sample.rearrange("l b i h d -> (l b i) (h d)")
    nvs = nv_sample.rearrange("l b i h d -> (l b i) (h d)")
    ngs = ngv_sample.rearrange("l b i h d -> (l b i) (h d)")
    down = expert_down.rearrange("l e d -> (l e) d")
    up = expert_up.rearrange("l e d -> (l e) d")

    def weights(w):
        return w.rearrange("l (k p) n -> p (l k) n", p=P)

    wv = {"ada": weights(w_ada), "in": weights(w_in), "ba": weights(w_branch_a),
          "bb": weights(w_branch_b), "out": weights(w_out), "query": weights(w_query)}

    mod_p = nc.dram_tensor("mod_prompt", (1, NMOD * D), F32, kind="Internal").ap()
    mod_s = nc.dram_tensor("mod_sample", (NS, NMOD * D), F32, kind="Internal").ap()
    score_dram = [nc.dram_tensor(f"key_scores_{g}", (NH * P, len(ts) * 2 * NKEY), F32, kind="Internal").ap()
                  for g, ts in enumerate(GROUPS)]
    x1_dram = nc.dram_tensor("x1_tiles", (TILES, P, D), F32, kind="Internal").ap()

    with ExitStack() as ctx:
        def sb(name, shape, dt=F32):
            return ctx.enter_context(nc.sbuf_tensor(name, shape, dt))

        def sem(name):
            return ctx.enter_context(nc.semaphore(name))

        bank = [ctx.enter_context(nc.psum_tensor(f"bank{i}", [P, 512], F32)) for i in range(8)]

        ring = sb("gather_ring", [P, SLOTS, D])
        wbuf = sb("weight_chunks", [P, 4, KC, WC])
        h2keep = sb("h2_group0", [P, 2, D])
        hTf = sb("hT", [P, 3072])
        kT = sb("kT", [P, 4, NH, P])
        vv = sb("v_tokens", [P, 4, D])
        qTf = sb("qT", [P, 3072])
        U = sb("u_and_gv", [P, 6144])
        sg = sb("sigmoids", [P, 4, 384])
        tab = sb("row_tables", [P, 3, D])
        acc = sb("expert_sums", [P, 2, D])
        WsT = sb("spatialT", [P, NH, P])
        bsb = sb("spatial_bias", [P, NH, P])
        skT = sb("sub_keysT", [P, 2, NKEY])
        junk = sb("scratch_row", [P, D])
        ident = sb("identity", [P, P])
        later = sb("later_keys", [P, P])
        ones = sb("ones", [P, P])
        since = sb("since_keys", [P, P])
        hidden = sb("hidden_keys", [P, P])
        hidden_s = sb("hidden_sample_keys", [NS, NS])
        expert = sb("expert_numbers", [P, TILES, P], I32)
        gates = sb("expert_gates", [P, TILES, P])
        stage = sb("gather_rows", [P, 2, TOPK], I32)
        cT = sb("condT", [P, KC, NG])
        bias_b = sb("stick_bias", [P, NH])
        iota_i = sb("iota_int", [P, TOPK], I32)
        iota_f = sb("iota", [P, TOPK])
        st = sb("norm_stats", [P, 16])
        dots = sb("expert_dots", [P, TOPK])
        acts = sb("expert_acts", [P, TOPK])
        coef = sb("expert_coefs", [P, TOPK])
        pt_sb = sb("page_numbers", [1, 2 * NDEC], I32)
        nbias_b = sb("minus_stick_bias", [P, NH])
        sc = sb("key_scores", [P, 3, 2, NKEY])
        work = junk[:, 0:6 * NKEY].rearrange("p (i n) -> p i n", i=3)
        cand = sb("pair_scores", [P, 3, TOPK * TOPK])
        top_v = sb("top_values", [P, 3, 2, TOPK])
        top_i = sb("top_places", [P, 3, 2, TOPK], U32)
        top_k = sb("top_keys", [P, 3, 2, TOPK])
        best_v = sb("best_values", [P, 3, TOPK])
        best_i = sb("best_places", [P, 3, TOPK], U32)
        halves_i = top_i[:].rearrange("p i a k -> p (i a k)").rearrange("p (a i k) -> p a i k", a=2, i=3)
        halves = sb("best_halves", [P, 2, 3, TOPK])
        pick = halves
        nmax = sb("minus_best", [P, 3])
        expo = sb("exponentials", [P, 3, TOPK])
        esum = sb("exponential_sums", [P, 2, 3])

        flat = ring[:, :, :].rearrange("p s d -> p (s d)")
        mod9 = flat[0:NG, 0:NMOD * D]
        c9 = flat[0:NG, 6144:7168]
        g1row = flat[0:NG, 7168:8192]
        g2row = acc[0:NG, 0, :]
        ws_nat = U[:, 2048:3072].rearrange("p (g s) -> p g s", g=NH)
        wss_nat = U[:, 5120:6144].rearrange("p (g s) -> p g s", g=NH)
        WsTs = hTf[:, 2048:3072].rearrange("p (g t) -> p g t", g=NH)
        bsbs = qTf[:, 2048:3072].rearrange("p (g t) -> p g t", g=NH)
        sk_nat = sg[:, 2, 0:256].rearrange("p (a d) -> p a d", a=2)
        causal = sg[:, 0, 0:P]

        def width(g):
            return P * len(GROUPS[g])

        def hT(g):
            return hTf[:, 0:KC * width(g)].rearrange("p (k n) -> p k n", k=KC)

        def qT(g):
            return qTf[:, 0:NH * width(g)].rearrange("p (k n) -> p k n", k=NH)

        def uT(g):
            return U[:, 0:NH * width(g)].rearrange("p (k n) -> p k n", k=NH)

        def mT(g):
            return U[:, 3072:3072 + NH * width(g)].rearrange("p (k n) -> p k n", k=NH)

        def gvt(i):
            return U[:, 3072 + D * i:3072 + D * (i + 1)]

        def h2(g, i):
            return h2keep[:, i, :] if g == 0 else gvt(i)

        def att(what, n):
            at = {"log": 0, "pos": 1024, "neg": 2048}[what] + 512 * (n % 2)
            return U[:, at:at + 512]

        kTf = kT[:, 2:4].rearrange("p s h d -> p (s h d)")
        vf = vv[:, 2:4].rearrange("p s d -> p (s d)")
        ef = ring[:, 6:8].rearrange("p s d -> p (s d)")
        pos_s = [kTf[:, 0:512], kTf[:, 512:1024], kTf[0:NS, 1024:1536]]
        neg_s = [vf[:, 0:512], vf[:, 512:1024], vf[0:NS, 1024:1536]]
        bias_row = ef[0:1, 1536:2048]
        log_s = [ef[:, 0:512], ef[:, 512:1024], ef[0:NS, 1024:1536]]

        diag = acc[:, 1, :].rearrange("p (k n) -> p k n", k=SLOTS)

        qh = U[:, 0:1536].rearrange("p (b a n) -> p b a n", b=2, a=2)
        sc_out = U[:, 1536:3072].rearrange("p (b n) -> p b n", b=2)

        s_const = sem("s_const")
        s_cond = sem("s_cond")
        s_small = sem("s_small")
        s_pt = sem("s_pt")
        s_silu = sem("s_silu")
        s_zero = sem("s_zero")
        s_wss = sem("s_wss")
        s_mod = sem("s_mod")
        s_modst = sem("s_modst")
        s_wload = [sem(f"s_wload{i}") for i in range(4)]
        s_full = [sem(f"s_full{i}") for i in range(4)]
        s_free = [sem(f"s_free{i}") for i in range(4)]
        s_tfull = [sem(f"s_tfull{i}") for i in range(2)]
        s_tfree = [sem(f"s_tfree{i}") for i in range(2)]
        s_tab = [sem(f"s_tab{i}") for i in range(3)]
        s_tabfree = sem("s_tabfree")
        s_x = [sem("s_x_g0"), sem("s_x_g1")]
        s_xr = [sem("s_xr_g0"), sem("s_xr_g1")]
        s_n1v, s_n1s, s_n1h = sem("s_n1v"), sem("s_n1s"), sem("s_n1h")
        s_n2v, s_n2s, s_n2h = sem("s_n2v"), sem("s_n2s"), sem("s_n2h")
        s_lnv, s_lns, s_lnh = sem("s_lnv"), sem("s_lns"), sem("s_lnh")
        s_kst = sem("s_kst")
        s_vst = sem("s_vst")
        s_gvst = sem("s_gvst")
        s_az = sem("s_az")
        s_ar = sem("s_ar")
        s_al = sem("s_al")
        s_ac = sem("s_ac")
        s_aw = sem("s_aw")
        s_ao = sem("s_ao")
        s_ae = sem("s_ae")
        s_page = [sem(f"s_page{i}") for i in range(4)]
        s_ktf = [sem("s_ktf0"), sem("s_ktf1")]
        s_kte = sem("s_kte")
        s_sz = sem("s_sz")
        s_sl = sem("s_sl")
        s_scm = sem("s_scm")
        s_sw = sem("s_sw")
        s_sv = sem("s_sv")
        s_se = sem("s_se")
        s_bias = sem("s_bias")
        s_x1st = sem("s_x1st")
        s_sfull = [sem(f"s_sfull{i}") for i in range(3)]
        s_sev = [sem(f"s_sev{i}") for i in range(3)]
        s_scst = [sem("s_scst0"), sem("s_scst1")]
        s_scld = sem("s_scld")
        s_tk = sem("s_tk")
        s_nb = sem("s_nb")
        s_ex = sem("s_ex")
        s_dn = sem("s_dn")
        s_up = sem("s_up")
        s_gath = [sem(f"s_gath{i}") for i in range(SLOTS)]
        s_ring = sem("s_ring")
        s_dotted = sem("s_dotted")
        s_summed = sem("s_summed")
        s_zeroed = sem("s_zeroed")
        s_diag = sem("s_diag")
        s_dots = sem("s_dots")
        s_acts = sem("s_acts")
        s_coef = sem("s_coef")
        s_fin = sem("s_fin")
        s_half = sem("s_half")
        s_fold = sem("s_fold")
        s_fv, s_fs, s_fy = sem("s_fv"), sem("s_fs"), sem("s_fy")
        s_y = sem("s_y")

        NCONST = 14

        def evacuated(eng, f):
            for b in range(4):
                n = (f - b + 3) // 4
                if n > 0:
                    eng.wait_ge(s_free[b], n)

        def turned(eng, t):
            for b in range(2):
                eng.wait_ge(s_tfree[b], (t - b + 1) // 2)

        block = ctx.enter_context(nc.Block())

        @block.sync
        def _(sp):
            def load_weight(n, src):
                if n >= 4:
                    f = last_fill(n - 4)
                    sp.wait_ge(s_full[f % 4], f // 4 + 1)
                sp.dma_start(wbuf[:, n % 4], src).then_inc(s_wload[n % 4], 16)

            def columns(name, at):
                return wv[name][:, :, at:at + WC]

            def load_table(g, what, kind):
                n = table_number(g, what, kind)
                if n >= 3:
                    sp.wait_ge(s_tabfree, n - 2)
                dst = tab[:, n % 3, :]
                if what in ("gv", "bv"):
                    sp.dma_start(dst, (g_v if what == "gv" else b_v).broadcast_to([P, D])).then_inc(s_tab[n % 3], 32)
                    return
                m = {"B1": 0, "A1": 1, "G1": 2, "B2": 3, "A2": 4}[what]
                if kind == "p":
                    sp.dma_start(dst, mod_p[:, m * D:(m + 1) * D].broadcast_to([P, D])).then_inc(s_tab[n % 3], 32)
                else:
                    for half in range(2):
                        sp.dma_start(tab[half * NS:(half + 1) * NS, n % 3, :],
                                     mod_s[:, m * D:(m + 1) * D]).then_inc(s_tab[n % 3], 16)

            def load_x(g, slots, signal):
                for i, t in enumerate(GROUPS[g]):
                    dst = vv[:, slots[i], :]
                    if t == SAMPLE:
                        for half in range(2):
                            sp.dma_start(vv[half * NS:(half + 1) * NS, slots[i], :], xs).then_inc(signal, 16)
                    else:
                        sp.dma_start(dst, xp[t]).then_inc(signal, 32)

            sp.dma_start(c9[0:1, :], c_prompt).then_inc(s_cond, 16)
            sp.dma_start(c9[1:NG, :], c_sample).then_inc(s_cond, 16)
            for n in range(4):
                load_weight(n, columns("ada", n * WC))
            sp.dma_start(mod9, b_ada.broadcast_to([NG, NMOD * D])).then_inc(s_cond, 16)
            sp.dma_start(g1row, g_norm1.broadcast_to([NG, D])).then_inc(s_cond, 16)
            sp.dma_start(g2row, g_norm2.broadcast_to([NG, D])).then_inc(s_cond, 16)
            sp.dma_start(pt_sb[:], page_table.rearrange("(o b) n -> o (b n)", o=1)).then_inc(s_pt, 16)
            sp.dma_start(ws_nat, w_spatial.rearrange("l g t s -> t (l g) s")).then_inc(s_small, 16)
            sp.dma_start(sk_nat, sub_keys.rearrange("l a k d -> k (l a) d")).then_inc(s_small, 16)
            sp.dma_start(bias_b[:], sb_bias.broadcast_to([P, NH])).then_inc(s_small, 16)
            sp.dma_start(bsb[:].rearrange("p g t -> p (g t)"),
                         b_spatial.rearrange("l g t -> l (g t)").broadcast_to([P, NH * P])).then_inc(s_small, 16)
            for b in range(P // DSEQ):
                sp.dma_start(bsbs[:, :, b * DSEQ:(b + 1) * DSEQ],
                             b_spatial[:, :, 0:DSEQ].broadcast_to([P, NH, DSEQ])).then_inc(s_small, 16)
            sp.wait_ge(s_zero, 1)
            for b in range(P // DSEQ):
                sp.dma_start(wss_nat[b * DSEQ:(b + 1) * DSEQ, :, b * DSEQ:(b + 1) * DSEQ],
                             w_spatial[0, :, 0:DSEQ, 0:DSEQ].rearrange("g t s -> t g s")).then_inc(s_wss, 16)
            load_x(0, [slot_of(0, i) for i in range(2)], s_x[0])
            for n in range(4, NADA):
                load_weight(n, columns("ada", n * WC))
            evacuated(sp, NADA)
            sp.wait_ge(s_mod, 2)
            sp.dma_start(mod_p, mod9[0:1, :]).then_inc(s_modst, 16)
            sp.dma_start(mod_s.rearrange("(b i) n -> b i n", i=DSEQ),
                         mod9[1:NG, :].unsqueeze(1).broadcast_to([NDEC, DSEQ, NMOD * D])).then_inc(s_modst, 16)
            sp.wait_ge(s_modst, 32)

            for g, tiles in enumerate(GROUPS):
                T = len(tiles)
                before = sum(len(GROUPS[j]) for j in range(g))
                if g:
                    sp.wait_ge(s_x1st, 16 * before)
                    load_x(g, [slot_of(g, i) for i in range(T)], s_x[g])
                for n in range(4):
                    load_weight(chunk_base(g, "q") + n, columns("in", n * WC))
                if g == 0:
                    for w in ("A1", "B1"):
                        load_table(g, w, "p")
                    for w in ("A1", "B1"):
                        load_table(g, w, "s")
                else:
                    for w in ("A1", "B1"):
                        load_table(g, w, "p")
                for n in range(4, 12):
                    load_weight(chunk_base(g, "q") + n, columns("in", n * WC))
                evacuated(sp, fill_base(g, "k") + 4 * T)
                for i, t in enumerate(tiles):
                    if t == SAMPLE:
                        sp.dma_start(nks, gvt(i)[0:NS, :]).then_inc(s_kst, 16)
                    else:
                        sp.dma_start(nkp[t], gvt(i)).then_inc(s_kst, 16)
                evacuated(sp, fill_base(g, "v") + 4 * T)
                for i, t in enumerate(tiles):
                    if t == SAMPLE:
                        sp.dma_start(nvs, vv[0:NS, slot_of(g, i), :]).then_inc(s_vst, 16)
                    else:
                        sp.dma_start(nvp[t], vv[:, slot_of(g, i), :]).then_inc(s_vst, 16)
                if g == 0:
                    sp.wait_ge(s_pt, 16)
                    for m in range(4 * NDEC):
                        page = m % (2 * NDEC)
                        number = sp.value_load(pt_sb[0:1, page:page + 1], min_val=0, max_val=n_phys - 1)
                        if 4 <= m < 2 * NDEC + 4:
                            sp.wait_ge(s_ktf[1], m - 3)
                        elif m >= 2 * NDEC + 4:
                            sp.wait_ge(s_sv, (m - 4 - 2 * NDEC) // 2 + 1)
                        store = kpages if m < 2 * NDEC else vpages
                        sp.dma_start(ring[:, m % 4, :], store[bass.ds(number * P, P), :]).then_inc(s_page[m % 4], 16)
                for n in range(12, 16):
                    load_weight(chunk_base(g, "q") + n, columns("in", n * WC))
                load_table(g, "gv", "")
                load_table(g, "bv", "")
                for n in range(16, 20):
                    load_weight(chunk_base(g, "q") + n, columns("in", n * WC))
                if g == 0:
                    sp.wait_ge(s_lnh, 2)
                    sp.dma_start(ngs, gvt(1)[0:NS, :]).then_inc(s_gvst, 16)
                load_table(g, "G1", "p")
                if g == 0:
                    load_table(g, "G1", "s")
                sp.wait_ge(s_ae, NH * (1 if g == 0 else 4))
                if g == 0:
                    sp.wait_ge(s_se, 1)
                sp.wait_ge(s_vst, 16 * (before + T))
                load_x(g, [xslot_of(g, i) for i in range(T)], s_xr[g])
                for j in range(4):
                    n = chunk_base(g, "merge") + 4 * j
                    load_weight(n, columns("in", 5 * D + j * WC))
                    load_weight(n + 1, columns("ba", j * WC))
                    load_weight(n + 2, columns("in", 6 * D + j * WC))
                    load_weight(n + 3, columns("bb", j * WC))
                for c in range(4):
                    load_weight(chunk_base(g, "out") + c, columns("out", c * WC))
                load_table(g, "A2", "p")
                load_table(g, "B2", "p")
                if g == 0:
                    load_table(g, "A2", "s")
                    load_table(g, "B2", "s")
                for c in range(4):
                    load_weight(chunk_base(g, "query") + c, columns("query", c * WC))
                evacuated(sp, fill_base(g, "out") + 4 * T)
                for i, t in enumerate(tiles):
                    sp.dma_start(x1_dram[t], vv[:, xslot_of(g, i), :]).then_inc(s_x1st, 16)
                for c in range(4, 8):
                    load_weight(chunk_base(g, "query") + c, columns("query", c * WC))
            sp.wait_ge(s_kst, 16 * TILES)
            sp.wait_ge(s_vst, 16 * TILES)
            sp.wait_ge(s_gvst, 16)
            sp.wait_ge(s_x1st, 16 * TILES)
            sp.wait_ge(s_y, 16 * TILES)

        @block.gpsimd
        def _(pool):
            done = [0]

            def const(ins):
                done[0] += 1
                ins.then_inc(s_const, 1)
                pool.wait_ge(s_const, done[0])

            const(nc.gpsimd.memset(ident[:], 0.0))
            const(nc.gpsimd.affine_select(out=ident[:], in_=ident[:], compare_op=ALU.not_equal, fill=1.0,
                                          base=0, pattern=[[-1, P]], channel_multiplier=1))
            const(nc.gpsimd.memset(ones[:], 1.0))
            const(nc.gpsimd.affine_select(out=later[:], in_=ones[:], compare_op=ALU.is_gt, fill=0.0,
                                          base=0, pattern=[[-1, P]], channel_multiplier=1))
            const(nc.gpsimd.affine_select(out=since[:], in_=ones[:], compare_op=ALU.is_ge, fill=0.0,
                                          base=0, pattern=[[-1, P]], channel_multiplier=1))
            const(nc.gpsimd.memset(hidden[:], 0.0))
            const(nc.gpsimd.affine_select(out=hidden[:], in_=hidden[:], compare_op=ALU.is_gt, fill=MASKED,
                                          base=0, pattern=[[1, P]], channel_multiplier=-1))
            const(nc.gpsimd.affine_select(out=causal, in_=ones[:], compare_op=ALU.is_ge, fill=0.0,
                                          base=0, pattern=[[1, P]], channel_multiplier=-1))
            blocks = hidden_s[:].rearrange("p (b i) -> p b i", i=DSEQ)
            const(nc.gpsimd.affine_select(out=blocks, in_=hidden[0:NS, 0:NS].rearrange("p (b i) -> p b i", i=DSEQ),
                                          compare_op=ALU.is_ge, fill=MASKED, base=0,
                                          pattern=[[-DSEQ, NDEC], [0, DSEQ]], channel_multiplier=1))
            const(nc.gpsimd.affine_select(out=blocks, in_=blocks, compare_op=ALU.is_ge, fill=MASKED, base=DSEQ - 1,
                                          pattern=[[DSEQ, NDEC], [0, DSEQ]], channel_multiplier=-1))
            const(nc.gpsimd.iota(iota_i[:], pattern=[[1, TOPK]], base=0, channel_multiplier=0))
            const(nc.gpsimd.tensor_copy(iota_f[:], iota_i[:]))
            const(nc.gpsimd.memset(wss_nat, 0.0))
            const(nc.gpsimd.memset(stage[:], 0))
            assert done[0] == NCONST

            rows_used = {s_dotted: pool.alloc_register("dotted_rows"), s_summed: pool.alloc_register("summed_rows")}
            for r in rows_used.values():
                pool.reg_mov(r, 0)

            def used(signal):
                pool.reg_add(rows_used[signal], rows_used[signal], 1)
                pool.wait_ge(s_const, NCONST)
                pool.wait_ge(signal, rows_used[signal])

            def gather(table, which, own, before):
                for k in range(TOPK):
                    if k >= SLOTS:
                        used(own)
                    elif before is not None:
                        used(before)
                    pool.indirect_dma_start(
                        out=ring[:, k % SLOTS, :], out_offset=None, in_=table,
                        in_offset=bass.IndirectOffsetOnAxis(ap=stage[:, which, k:k + 1], axis=0),
                    ).then_inc(s_gath[k % SLOTS], 16)

            def gather_down(n, before):
                pool.wait_ge(s_dn, n)
                gather(down, 0, s_dotted, before)

            def gather_up(n, before):
                pool.wait_ge(s_up, n)
                gather(up, 1, s_summed, before)

            def load_scores(g, h):
                for b in range(2):
                    pool.wait_ge(s_scst[b], 16 * (NH // 2) * (g + 1))
                if isinstance(h, int):
                    if g + h:
                        pool.wait_ge(s_tk, NH * g + h)
                else:
                    pool.wait_ge(s_tk, h + NH * g)
                T = len(GROUPS[g])
                pool.dma_start(sc[:, 0:T].rearrange("p i a k -> p (i a k)"),
                               score_dram[g][bass.ds(h * P, P), :]).then_inc(s_scld, 16)

            for order, t in enumerate(ORDER):
                H, first, g = STEPS[t], FIRST[t], CHOOSING.get(t)
                if g is not None:
                    load_scores(g, 0)
                    load_scores(g, 1)
                pool.wait_ge(s_ring, order + 1)
                gather_down(first + 1, None)
                if g is not None:
                    load_scores(g, 2)
                gather_down(first + 2, s_dotted)
                gather_up(first + 1, s_dotted)
                if g is not None:
                    with pool.Fori(2, H - 1) as h:
                        load_scores(g, h + 1)
                        gather_down(h + (first + 1), s_summed)
                        gather_up(h + first, s_dotted)
                    gather_down(first + H, s_summed)
                    gather_up(first + H - 1, s_dotted)
                else:
                    with pool.Fori(2, H) as h:
                        gather_down(h + (first + 1), s_summed)
                        gather_up(h + first, s_dotted)
                gather_up(first + H, s_summed)
                pool.wait_ge(s_summed, TOPK * (first + H))
                pool.reg_add(rows_used[s_summed], rows_used[s_summed], SLOTS)
                if t == SAMPLE:
                    for half in range(2):
                        pool.dma_start(ring[half * NS:(half + 1) * NS, 0, :],
                                       mod_s[:, 5 * D:6 * D]).then_inc(s_fin, 16)
                else:
                    pool.dma_start(ring[:, 0, :], mod_p[:, 5 * D:6 * D].broadcast_to([P, D])).then_inc(s_fin, 32)
                pool.dma_start(ring[:, 1, :], g_final.rearrange("(o d) -> o d", o=1).broadcast_to([P, D])).then_inc(s_fin, 16)
                pool.dma_start(ring[:, 2, :], x1_dram[t]).then_inc(s_fin, 16)
                if t == SAMPLE:
                    pool.wait_ge(s_half, 1)
                    pool.dma_start(ring[0:NS, 3, :], acc[NS:P, 0, :]).then_inc(s_fold, 16)

        @block.tensor
        def _(pe):
            def weight(n):
                pe.wait_ge(s_wload[n % 4], 16 * (n // 4 + 1))
                return wbuf[:, n % 4]

            def take(f):
                if f >= 4:
                    pe.wait_ge(s_free[f % 4], f // 4)
                return bank[f % 4]

            def take_turn(t):
                if t >= 2:
                    pe.wait_ge(s_tfree[t % 2], t // 2)
                return bank[4 + t % 2]

            def token_major(n, f, src):
                w = weight(n)
                out = take(f)
                for k in range(KC):
                    mm = nc.tensor.matmul(out[:, 0:WC], src[:, k, :], w[:, k, :], start=(k == 0), stop=(k == KC - 1))
                mm.then_inc(s_full[f % 4], 1)
                return mm

            def channel_major(n, f, src, N):
                w = weight(n)
                for j in range(2):
                    out = take(f + j)
                    for k in range(KC):
                        mm = nc.tensor.matmul(out[:, 0:N], w[:, k, j * P:(j + 1) * P], src[:, k, :],
                                              start=(k == 0), stop=(k == KC - 1))
                    mm.then_inc(s_full[(f + j) % 4], 1)

            def turn_four(t, blocks):
                out = take_turn(t)
                for j, b in enumerate(blocks):
                    mm = nc.tensor.transpose(out[0:b.shape[1], j * P:j * P + b.shape[0]], b, ident[0:b.shape[0], 0:b.shape[0]])
                mm.then_inc(s_tfull[t % 2], 1)

            pe.wait_ge(s_const, NCONST)
            pe.wait_ge(s_silu, 1)
            for t in range(2):
                out = take_turn(t)
                for j in range(4):
                    k = 4 * t + j
                    mm = nc.tensor.transpose(out[:, j * NG:(j + 1) * NG], c9[:, k * P:(k + 1) * P], ident[0:NG, 0:NG])
                mm.then_inc(s_tfull[t], 1)
            pe.wait_ge(s_tfree[0], 1)
            pe.wait_ge(s_tfree[1], 1)
            for n in range(NADA):
                w = weight(n)
                out = take(n)
                for k in range(KC):
                    mm = nc.tensor.matmul(out[0:NG, 0:WC], cT[:, k, :], w[:, k, :], start=(k == 0), stop=(k == KC - 1))
                mm.then_inc(s_full[n % 4], 1)
            pe.wait_ge(s_small, 16 * 20)
            pe.wait_ge(s_wss, 16 * (P // DSEQ))
            for half in range(2):
                turn_four(2 + half, [ws_nat[:, 4 * half + j, :] for j in range(4)])
            for half in range(2):
                turn_four(4 + half, [wss_nat[:, 4 * half + j, :] for j in range(4)])
            for a in range(2):
                turn_four(6 + a, [sk_nat[:, a, :]])

            heads = 0
            for g, tiles in enumerate(GROUPS):
                T, N = len(tiles), width(g)
                before = sum(len(GROUPS[j]) for j in range(g))
                for i in range(T):
                    pe.wait_ge(s_n1h, before + i + 1)
                    for half in range(2):
                        x = vv[:, slot_of(g, i), :]
                        turn_four(turn_base(g, "norm1") + 2 * i + half,
                                  [x[:, (4 * half + j) * P:(4 * half + j + 1) * P] for j in range(4)])
                turned(pe, turn_base(g, "kT"))
                h = hT(g)
                for c in range(4):
                    channel_major(chunk_base(g, "q") + c, fill_base(g, "q") + 2 * c, h, N)
                for c in range(4):
                    n = chunk_base(g, "k") + c
                    for i in range(T):
                        token_major(n, fill_base(g, "k") + c * T + i, h[:, :, i * P:(i + 1) * P])
                    if c:
                        evacuated(pe, fill_base(g, "k") + c * T)
                        for i in range(T):
                            turn_four(turn_base(g, "kT") + (c - 1) * T + i,
                                      [gvt(i)[:, (2 * (c - 1) + j) * P:(2 * (c - 1) + j + 1) * P] for j in range(2)])
                for c in range(4):
                    n = chunk_base(g, "v") + c
                    for i in range(T):
                        token_major(n, fill_base(g, "v") + c * T + i, h[:, :, i * P:(i + 1) * P])
                    if c == 0:
                        evacuated(pe, fill_base(g, "k") + 4 * T)
                        for i in range(T):
                            turn_four(turn_base(g, "kT") + 3 * T + i,
                                      [gvt(i)[:, (6 + j) * P:(7 + j) * P] for j in range(2)])
                turned(pe, turn_base(g, "gate"))
                evacuated(pe, fill_base(g, "u"))
                pe.wait_ge(s_bias, 1)
                q = qT(g)

                def scores(n, i, t, hd):
                    if n >= 2:
                        pe.wait_ge(s_ar, n - 1)
                    z = bank[6 + n % 2]
                    for kb in range(t + 1):
                        nc.tensor.matmul(z[:, kb * P:(kb + 1) * P], kT[:, kb, hd, :], q[:, hd, i * P:(i + 1) * P],
                                         start=True, stop=(kb < t))
                    nc.tensor.matmul(z[:, t * P:(t + 1) * P], ident[:], hidden[:], start=False, stop=True).then_inc(s_az, 1)

                def exponents(n, t):
                    pe.wait_ge(s_al, n + 1)
                    if n >= 2:
                        pe.wait_ge(s_aw, n - 1)
                    for kb in range(t + 1):
                        out = bank[4 + n % 2][:, kb * P:(kb + 1) * P]
                        cols = slice(kb * P, (kb + 1) * P)
                        nc.tensor.matmul(out, since[:], att("log", n)[:, cols], start=True, stop=False)
                        nc.tensor.matmul(out, later[:], att("pos", n)[:, cols], start=False, stop=False)
                        mm = nc.tensor.matmul(out, ident[:], att("neg", n)[:, cols], start=False, stop=(kb == t))
                        for k2 in range(kb + 1, t + 1):
                            cols = slice(k2 * P, (k2 + 1) * P)
                            nc.tensor.matmul(out, ones[:], att("log", n)[:, cols], start=False, stop=False)
                            mm = nc.tensor.matmul(out, ones[:], att("pos", n)[:, cols], start=False, stop=(k2 == t))
                    mm.then_inc(s_ac, 1)

                def outputs(n, t, hd):
                    pe.wait_ge(s_aw, n + 1)
                    if n >= 2:
                        pe.wait_ge(s_ae, n - 1)
                    for kb in range(t + 1):
                        mm = nc.tensor.matmul(bank[2 + n % 2][:, 0:P], vv[:, kb, hd * P:(hd + 1) * P],
                                              att("log", n)[:, kb * P:(kb + 1) * P], start=(kb == 0), stop=(kb == t))
                    mm.then_inc(s_ao, 1)

                work_list = [(i, t, hd) for i, t in enumerate(tiles) if t != SAMPLE for hd in range(NH)]
                scores(heads, *work_list[0])
                for w in range(len(work_list) + 1):
                    if w + 1 < len(work_list):
                        scores(heads + w + 1, *work_list[w + 1])
                    if w < len(work_list):
                        exponents(heads + w, work_list[w][1])
                    if w:
                        outputs(heads + w - 1, *work_list[w - 1][1:])
                heads += len(work_list)
                pe.wait_ge(s_ae, heads)

                if g == 0:
                    nc.tensor.matmul(bank[0][0:NS, :], ones[0:1, 0:NS], bias_row, start=True, stop=False)
                    for page in range(2):
                        nc.tensor.matmul(bank[6 + page][:, :], ones[0:1, :], bias_row, start=True, stop=False)
                    for hd in range(NH):
                        nc.tensor.matmul(bank[0][0:NS, hd * NS:(hd + 1) * NS], kT[:, 1, hd, 0:NS],
                                         q[:, hd, P:P + NS], start=False, stop=False)
                    nc.tensor.matmul(bank[0][0:NS, :].rearrange("p (h n) -> p h n", h=NH), ident[0:NS, 0:NS],
                                     hidden_s[:].unsqueeze(1).broadcast_to([NS, NH, NS]), start=False, stop=True)

                    def turn_page(m):
                        pe.wait_ge(s_page[m % 4], 16 * (m // 4 + 1))
                        for half in range(2):
                            if m >= 2:
                                pe.wait_ge(s_kte, 2 * (m - 2) + half + 1)
                            for j in range(4):
                                mm = nc.tensor.transpose(bank[4 - 2 * (m % 2) + half][:, j * P:(j + 1) * P],
                                                         ring[:, m % 4, (4 * half + j) * P:(4 * half + j + 1) * P], ident[:])
                            mm.then_inc(s_ktf[half], 1)

                    turn_page(0)
                    for m in range(2 * NDEC):
                        b, page = m // 2, m % 2
                        if m + 1 < 2 * NDEC:
                            turn_page(m + 1)
                        pe.wait_ge(s_kte, 2 * m + 2)
                        for hd in range(NH):
                            at = hd * NS + b * DSEQ
                            mm = nc.tensor.matmul(bank[6 + page][:, at:at + DSEQ],
                                                  ring[:, 4 + m % 2, hd * P:(hd + 1) * P],
                                                  q[:, hd, P + b * DSEQ:P + (b + 1) * DSEQ], start=False,
                                                  stop=(b == NDEC - 1 and hd == NH - 1))
                        mm.then_inc(s_sz, 1)
                    pe.wait_ge(s_sl, 1)
                    for part in (2, 1, 0):
                        rows = NS if part == 2 else P
                        out = bank[1 + part][0:rows, :]
                        nc.tensor.matmul(out, since[0:rows, 0:rows], log_s[part], start=True, stop=False)
                        nc.tensor.matmul(out, later[0:rows, 0:rows], pos_s[part], start=False, stop=False)
                        mm = nc.tensor.matmul(out, ident[0:rows, 0:rows], neg_s[part], start=False, stop=(part == 2))
                        for behind in range(part + 1, 3):
                            r = NS if behind == 2 else P
                            nc.tensor.matmul(out, ones[0:r, :], log_s[behind], start=False, stop=False)
                            mm = nc.tensor.matmul(out, ones[0:r, :], pos_s[behind], start=False, stop=(behind == 2))
                    mm.then_inc(s_scm, 1)
                    pe.wait_ge(s_sw, 1)
                    for b in range(NDEC):
                        m0 = 2 * NDEC + 2 * b
                        for page in range(2):
                            m = m0 + page
                            pe.wait_ge(s_page[m % 4], 16 * (m // 4 + 1))
                        for hd in range(NH):
                            at = slice(hd * NS + b * DSEQ, hd * NS + (b + 1) * DSEQ)
                            nc.tensor.matmul(bank[4][:, at], vv[0:NS, 1, hd * P:(hd + 1) * P], log_s[2][:, at],
                                             start=True, stop=False)
                            for page in range(2):
                                mm = nc.tensor.matmul(bank[4][:, at], ring[:, (m0 + page) % 4, hd * P:(hd + 1) * P],
                                                      log_s[page][:, at], start=False, stop=(page == 1))
                        mm.then_inc(s_sv, 1)
                    pe.wait_ge(s_se, 1)

                for c in range(4):
                    channel_major(chunk_base(g, "u") + c, fill_base(g, "u") + 2 * c, h, N)
                for c in range(4):
                    n = chunk_base(g, "gv") + c
                    for i in range(T):
                        token_major(n, fill_base(g, "gv") + c * T + i, h[:, :, i * P:(i + 1) * P])
                for i, t in enumerate(tiles):
                    pe.wait_ge(s_lnh, before + i + 1)
                    mix = WsTs if t == SAMPLE else WsT
                    for half in range(2):
                        f = turn_base(g, "gate") + 2 * i + half
                        out = take_turn(f)
                        for j in range(4):
                            gr = 4 * half + j
                            mm = nc.tensor.matmul(out[:, j * P:(j + 1) * P], gvt(i)[:, gr * P:(gr + 1) * P], mix[:, gr, :],
                                                  start=True, stop=True)
                        mm.then_inc(s_tfull[f % 2], 1)
                turned(pe, turn_base(g, "norm2"))
                u = uT(g)
                for j in range(4):
                    n, f = chunk_base(g, "merge") + 4 * j, fill_base(g, "merge") + 8 * j
                    channel_major(n, f, h, N)
                    channel_major(n + 1, f + 2, u, N)
                    channel_major(n + 2, f + 4, h, N)
                    channel_major(n + 3, f + 6, q, N)
                evacuated(pe, fill_base(g, "out"))
                m = mT(g)
                for c in range(4):
                    n = chunk_base(g, "out") + c
                    for i in range(T):
                        token_major(n, fill_base(g, "out") + c * T + i, m[:, :, i * P:(i + 1) * P])
                for i in range(T):
                    pe.wait_ge(s_n2h, before + i + 1)
                    for half in range(2):
                        turn_four(turn_base(g, "norm2") + 2 * i + half,
                                  [h2(g, i)[:, (4 * half + j) * P:(4 * half + j + 1) * P] for j in range(4)])
                turned(pe, turn_base(g, "norm2") + 2 * T)
                def key_scores(c):
                    evacuated(pe, fill_base(g, "query") + 2 * c + 2)
                    for i in range(T):
                        if c or g:
                            done = c + (8 * g if i < 2 else 0)
                            if done:
                                pe.wait_ge(s_sev[i], done)
                        for a in range(2):
                            mm = nc.tensor.matmul(bank[5 + i][:, a * NKEY:(a + 1) * NKEY], qh[:, c % 2, a, i * P:(i + 1) * P],
                                                  skT[:, a, :], start=True, stop=True)
                        mm.then_inc(s_sfull[i], 1)
                for c in range(NH):
                    channel_major(chunk_base(g, "query") + c, fill_base(g, "query") + 2 * c, h, N)
                    if c:
                        key_scores(c - 1)
                key_scores(NH - 1)
                for i in range(T):
                    pe.wait_ge(s_sev[i], NH * (g + 1) if i < 2 else NH)

            def sum_step(n, batch, last):
                for k in range(TOPK):
                    pe.wait_ge(s_diag, (n - first_here) * TOPK + k + 1)
                    pe.wait_ge(s_gath[k % SLOTS], batch * 32 + 16 * (k // SLOTS + 1))
                    for half in range(2):
                        mm = nc.tensor.matmul(bank[6 + half][:, :], diag[:, k % SLOTS, :],
                                              ring[:, k % SLOTS, half * 512:(half + 1) * 512],
                                              start=False, stop=(last and k == TOPK - 1))
                    mm.then_inc(s_summed, 1)

            first_here = FIRST[1]
            for order, t in enumerate(ORDER):
                if t in WOVEN:
                    continue
                H, first = STEPS[t], FIRST[t]
                pe.wait_ge(s_zeroed, order + 1)
                for half in range(2):
                    nc.tensor.matmul(bank[6 + half][:, :], ident[:], acc[:, 0, half * 512:(half + 1) * 512],
                                     start=True, stop=False)
                with pe.Fori(1, H) as h:
                    sum_step(h + (first - 1), (h + first) * 2, False)
                sum_step(first + H - 1, 2 * (first + H) - 1, True)

        @block.scalar
        def _(act):
            def read(f):
                act.wait_ge(s_full[f % 4], f // 4 + 1)
                return bank[f % 4]

            def read_turn(t):
                act.wait_ge(s_tfull[t % 2], t // 2 + 1)
                return bank[4 + t % 2]

            def root(wait, n, signal, col):
                act.wait_ge(wait, n)
                nc.scalar.activation(st[:, col + 1:col + 2], st[:, col:col + 1], ACT.Sqrt).then_inc(signal, 1)

            act.wait_ge(s_cond, 16 * 5)
            nc.scalar.activation(c9, c9, ACT.Silu).then_inc(s_silu, 1)
            for t in range(2):
                out = read_turn(t)
                nc.scalar.copy(cT[:, 4 * t:4 * t + 4, :].rearrange("p k r -> p (k r)"), out[:, 0:4 * NG]).then_inc(s_tfree[t], 1)
            for a in range(2):
                f = 6 + a
                nc.scalar.copy(skT[:, a, :], read_turn(f)[:, 0:NKEY]).then_inc(s_tfree[f % 2], 1)

            def exponentials(g, ready):
                act.wait_ge(s_nb, ready)
                for i in range(len(GROUPS[g])):
                    nc.scalar.activation(expo[:, i, :], best_v[:, i, :], ACT.Exp, bias=nmax[:, i:i + 1],
                                         accum_out=esum[:, 0, i:i + 1]).then_inc(s_ex, 1)

            def front(g):
                tiles = GROUPS[g]
                T, N = len(tiles), width(g)
                before = sum(len(GROUPS[j]) for j in range(g))

                def transposed(phase, i):
                    for half in range(2):
                        f = turn_base(g, phase) + 2 * i + half
                        src = read_turn(f)[:, :].rearrange("p (j n) -> p j n", j=4)
                        nc.scalar.copy(hT(g)[:, 4 * half:4 * half + 4, i * P:(i + 1) * P], src).then_inc(s_tfree[f % 2], 1)

                for i in range(T):
                    root(s_n1v, before + i + 1, s_n1s, 0)
                for i in range(T):
                    transposed("norm1", i)
                yield
                for j in range(NH):
                    f = fill_base(g, "q") + j
                    nc.scalar.copy(qT(g)[:, j, :], read(f)[:, 0:N]).then_inc(s_free[f % 4], 1)
                    if j % 4 == 3:
                        yield

                def keys_turned(c):
                    for i in range(T):
                        f = turn_base(g, "kT") + c * T + i
                        nc.scalar.copy(kT[:, slot_of(g, i), 2 * c:2 * c + 2, :].rearrange("p h n -> p (h n)"),
                                       read_turn(f)[:, 0:2 * P]).then_inc(s_tfree[f % 2], 1)
                for c in range(4):
                    for i in range(T):
                        f = fill_base(g, "k") + c * T + i
                        nc.scalar.copy(gvt(i)[:, c * WC:(c + 1) * WC], read(f)[:, 0:WC]).then_inc(s_free[f % 4], 1)
                    if c:
                        keys_turned(c - 1)
                    yield
                for c in range(4):
                    for i in range(T):
                        f = fill_base(g, "v") + c * T + i
                        nc.scalar.copy(vv[:, slot_of(g, i), c * WC:(c + 1) * WC], read(f)[:, 0:WC]).then_inc(s_free[f % 4], 1)
                    if c == 0:
                        keys_turned(3)
                    yield

                def log_part(n, i, t, hd):
                    cols = (t + 1) * P
                    act.wait_ge(s_az, n + 1)
                    if n >= 2:
                        act.wait_ge(s_ao, n - 1)
                    z = bank[6 + n % 2][:, 0:cols]
                    log = att("log", n)[:, 0:cols]
                    nc.scalar.activation(log, z, ACT.Abs, scale=SCALE, bias=bias_b[:, hd:hd + 1])
                    nc.scalar.activation(att("pos", n)[:, 0:cols], z, ACT.Relu, scale=SCALE, bias=bias_b[:, hd:hd + 1])
                    nc.scalar.activation(att("neg", n)[:, 0:cols], z, ACT.Relu, scale=-SCALE,
                                         bias=nbias_b[:, hd:hd + 1]).then_inc(s_ar, 1)
                    act.wait_ge(s_ar, n + 1)
                    nc.scalar.activation(log, log, ACT.Exp, scale=-1.0)
                    act.drain()
                    nc.scalar.activation(log, log, ACT.Ln, bias=1.0).then_inc(s_al, 1)

                def weights_part(n, t):
                    act.wait_ge(s_ac, n + 1)
                    nc.scalar.activation(att("log", n)[:, 0:(t + 1) * P], bank[4 + n % 2][:, 0:(t + 1) * P], ACT.Exp,
                                         scale=-1.0).then_inc(s_aw, 1)

                def output_part(n, i, hd):
                    act.wait_ge(s_ao, n + 1)
                    nc.scalar.copy(qT(g)[:, hd, i * P:(i + 1) * P], bank[2 + n % 2][:, 0:P]).then_inc(s_ae, 1)

                if g:
                    for b in range(2):
                        act.wait_ge(s_scst[b], 16 * (NH // 2))
                act.wait_ge(s_bias, 1)
                heads = NH * sum(t != SAMPLE for ts in GROUPS[:g] for t in ts)
                items = [(i, t, hd) for i, t in enumerate(tiles) if t != SAMPLE for hd in range(NH)]
                log_part(heads, *items[0])
                for w in range(len(items) + 1):
                    if w + 1 < len(items):
                        log_part(heads + w + 1, *items[w + 1])
                    if w < len(items):
                        weights_part(heads + w, items[w][1])
                    if w:
                        output_part(heads + w - 1, items[w - 1][0], items[w - 1][2])
                    yield
                if g == 0:
                    for m in range(2 * NDEC):
                        if m >= 2:
                            act.wait_ge(s_sz, m - 1)
                        for half in range(2):
                            act.wait_ge(s_ktf[half], m + 1)
                            nc.scalar.copy(ring[:, 4 + m % 2, half * 512:(half + 1) * 512],
                                           bank[4 - 2 * (m % 2) + half][:, :]).then_inc(s_kte, 1)
                    act.wait_ge(s_sz, 2 * NDEC)
                    for part, src in enumerate((bank[6][:, :], bank[7][:, :], bank[0][0:NS, :])):
                        nc.scalar.activation(log_s[part], src, ACT.Abs, scale=SCALE)
                        nc.scalar.activation(pos_s[part], src, ACT.Relu, scale=SCALE)
                        nc.scalar.activation(neg_s[part], src, ACT.Relu, scale=-SCALE)
                    act.drain()
                    for part in range(3):
                        nc.scalar.activation(log_s[part], log_s[part], ACT.Exp, scale=-1.0)
                    act.drain()
                    for part in range(3):
                        ins = nc.scalar.activation(log_s[part], log_s[part], ACT.Ln, bias=1.0)
                    ins.then_inc(s_sl, 1)
                    act.wait_ge(s_scm, 1)
                    for part in range(3):
                        rows = NS if part == 2 else P
                        ins = nc.scalar.activation(log_s[part], bank[1 + part][0:rows, :], ACT.Exp, scale=-1.0)
                    ins.then_inc(s_sw, 1)
                    act.wait_ge(s_sv, NDEC)
                    src = bank[4][:, :].rearrange("p (h n) -> p h n", h=NH)
                    nc.scalar.copy(qT(g)[:, :, P:P + NS], src)
                    nc.scalar.copy(qT(g)[:, :, P + NS:2 * P], src).then_inc(s_se, 1)
                act.wait_ge(s_kst, 16 * (before + T))
                for j in range(NH):
                    f = fill_base(g, "u") + j
                    nc.scalar.activation(uT(g)[:, j, :], read(f)[:, 0:N], ACT.Gelu).then_inc(s_free[f % 4], 1)
                    if j % 4 == 3:
                        yield
                for c in range(4):
                    for i in range(T):
                        f = fill_base(g, "gv") + c * T + i
                        nc.scalar.activation(gvt(i)[:, c * WC:(c + 1) * WC], read(f)[:, 0:WC], ACT.Gelu).then_inc(s_free[f % 4], 1)
                    yield
                for i in range(T):
                    root(s_lnv, before + i + 1, s_lns, 4)
                    yield
                for j in range(4):
                    for which in range(2):
                        f = fill_base(g, "merge") + 8 * j + 4 * which
                        for b in range(2):
                            if j:
                                used = f - 8 + 2 + b
                                act.wait_ge(s_free[used % 4], used // 4 + 1)
                            nc.scalar.activation(sg[:, 2 * which + b, 0:N], read(f + b)[:, 0:N],
                                                 ACT.Sigmoid).then_inc(s_free[(f + b) % 4], 1)
                        yield
                for i in range(T):
                    root(s_n2v, before + i + 1, s_n2s, 8)
                    yield
                for i in range(T):
                    transposed("norm2", i)
                yield

                def scores_out(c):
                    if c >= 2:
                        act.wait_ge(s_scst[c % 2], 16 * (NH // 2 * g + c // 2))
                    for i in range(T):
                        done = c + (NH * g if i < 2 else 0)
                        act.wait_ge(s_sfull[i], done + 1)
                        nc.scalar.copy(sc_out[:, c % 2, i * 2 * NKEY:(i + 1) * 2 * NKEY],
                                       bank[5 + i][:, 0:2 * NKEY]).then_inc(s_sev[i], 1)
                    for i in range(T):
                        act.wait_ge(s_sev[i], c + (NH * g if i < 2 else 0) + 1)
                    act.dma_start(score_dram[g][c * P:(c + 1) * P, :],
                                  sc_out[:, c % 2, 0:T * 2 * NKEY]).then_inc(s_scst[c % 2], 16)
                for c in range(NH):
                    for a in range(2):
                        f = fill_base(g, "query") + 2 * c + a
                        if c >= 2:
                            for i in range(T):
                                act.wait_ge(s_sfull[i], c - 1 + (NH * g if i < 2 else 0))
                        nc.scalar.copy(qh[:, c % 2, a, 0:N], read(f)[:, 0:N]).then_inc(s_free[f % 4], 1)
                    if c:
                        scores_out(c - 1)
                    yield
                scores_out(NH - 1)

            for _ in front(0):
                pass
            other = front(1)
            for order, t in enumerate(ORDER):
                H, first, g = STEPS[t], FIRST[t], CHOOSING.get(t)

                def gelu(h):
                    act.wait_ge(s_dots, h + (first + 1))
                    nc.scalar.activation(acts[:], dots[:], ACT.Gelu).then_inc(s_acts, 1)

                def diagonals(h):
                    n = h + (first - FIRST[1])
                    act.wait_ge(s_coef, n + 1)
                    for k in range(TOPK):
                        if k >= SLOTS:
                            act.wait_ge(s_summed, (n + FIRST[1]) * TOPK + k - SLOTS + 1)
                        nc.scalar.activation(diag[:, k % SLOTS, :], ident[:], ACT.Copy,
                                             scale=coef[:, k:k + 1]).then_inc(s_diag, 1)

                if t in WOVEN:
                    if g is not None:
                        exponentials(g, NH * g + 1)
                    for h in range(H):
                        for _ in range(ACT_PIECES[t][h]):
                            next(other, None)
                        gelu(h)
                        if g is not None and h < H - 1:
                            exponentials(g, NH * g + h + 2)
                    for _ in range(ACT_PIECES[t][H]):
                        next(other, None)
                else:
                    if g is not None:
                        exponentials(g, NH * g + 1)
                    gelu(0)
                    if g is not None:
                        exponentials(g, NH * g + 2)
                    with act.Fori(1, H - 1) as h:
                        act.wait_ge(s_summed, (h + (first - 1)) * TOPK)
                        diagonals(h - 1)
                        gelu(h)
                        if g is not None:
                            exponentials(g, h + (NH * g + 2))
                    for h in (H - 2, H - 1):
                        act.wait_ge(s_summed, (h + first) * TOPK)
                        diagonals(h)
                        if h == H - 2:
                            gelu(H - 1)
                root(s_fv, order + 1, s_fs, 12)
                act.wait_ge(s_fy, order + 1)
                dst = ys if t == SAMPLE else yp[t]
                act.dma_start(dst, acc[0:dst.shape[0], 0, :]).then_inc(s_y, 16)
                if t == WOVEN[-1]:
                    for _ in other:
                        pass

        @block.vector
        def _(dve):

            def read(f):
                dve.wait_ge(s_full[f % 4], f // 4 + 1)
                return bank[f % 4]

            def read_turn(t):
                dve.wait_ge(s_tfull[t % 2], t // 2 + 1)
                return bank[4 + t % 2]

            def table(g, what, kind):
                n = table_number(g, what, kind)
                dve.wait_ge(s_tab[n % 3], 32 * (n // 3 + 1))
                return tab[:, n % 3, :]

            def mean_square(src, col, signal):
                nc.vector.tensor_tensor_reduce(out=junk[:], in0=src, in1=src, scale=1.0, scalar=0.0,
                                               op0=ALU.mult, op1=ALU.add, accum_out=st[:, col:col + 1])
                dve.drain()
                nc.vector.tensor_scalar(st[:, col:col + 1], st[:, col:col + 1], 1.0 / D, EPS, ALU.mult, ALU.add).then_inc(signal, 1)

            def reciprocal_root(wait, n, col):
                dve.wait_ge(wait, n)
                nc.vector.reciprocal(st[:, col + 2:col + 3], st[:, col + 1:col + 2])
                dve.drain()
                return st[:, col + 2:col + 3]

            dve.wait_ge(s_const, NCONST)
            nc.vector.memset(acc[0:1, 1, 0:1], 0.0).then_inc(s_zero, 1)
            dve.wait_ge(s_cond, 16 * 5)
            for n in range(NADA):
                m = mod9[:, n * WC:(n + 1) * WC]
                nc.vector.tensor_tensor(m, read(n)[0:NG, 0:WC], m, ALU.add).then_inc(s_free[n % 4], 1)
            dve.drain()
            for m, gain in ((1, g1row), (4, g2row)):
                row = mod9[:, m * D:(m + 1) * D]
                nc.vector.scalar_tensor_tensor(out=row, in0=row, scalar=1.0, in1=gain, op0=ALU.add,
                                               op1=ALU.mult).then_inc(s_mod, 1)
            for f, dst in ((2, WsT[:]), (4, WsTs)):
                for half in range(2):
                    src = read_turn(f + half)[:, :].rearrange("p (j n) -> p j n", j=4)
                    nc.vector.tensor_tensor(dst[:, 4 * half:4 * half + 4, :], src,
                                            causal.unsqueeze(1).broadcast_to([P, 4, P]), ALU.mult).then_inc(s_tfree[half], 1)

            dve.wait_ge(s_small, 16 * 20)
            nc.vector.tensor_scalar(nbias_b[:], bias_b[:], -1.0, None, ALU.mult)
            nc.vector.tensor_scalar(bias_row.rearrange("p (h n) -> p h n", h=NH),
                                    bias_b[0:1, :].unsqueeze(2).broadcast_to([1, NH, NS]),
                                    1.0 / SCALE, None, ALU.mult).then_inc(s_bias, 1)

            def front(g):
                tiles = GROUPS[g]
                T, N = len(tiles), width(g)
                before = sum(len(GROUPS[j]) for j in range(g))

                dve.wait_ge(s_x[g], 32 * T)
                for i, t in enumerate(tiles):
                    kind = "s" if t == SAMPLE else "p"
                    x = vv[:, slot_of(g, i), :]
                    dve.drain()
                    mean_square(x, 0, s_n1v)
                    r = reciprocal_root(s_n1s, before + i + 1, 0)
                    nc.vector.scalar_tensor_tensor(out=x, in0=x, scalar=r, in1=table(g, "A1", kind), op0=ALU.mult, op1=ALU.mult)
                    dve.drain()
                    nc.vector.tensor_tensor(x, x, table(g, "B1", kind), ALU.add).then_inc(s_n1h, 1)
                    if g == 0 or i == T - 1:
                        nc.vector.drain().then_inc(s_tabfree, 2)
                    yield

                for i, t in enumerate(tiles):
                    evacuated(dve, fill_base(g, "gv") + 4 * T)
                    x = gvt(i)
                    dve.drain()
                    nc.vector.tensor_reduce(st[:, 7:8], x, AX.X, ALU.add)
                    dve.drain()
                    nc.vector.tensor_scalar(st[:, 7:8], st[:, 7:8], -1.0 / D, None, ALU.mult)
                    dve.drain()
                    nc.vector.tensor_scalar(x, x, st[:, 7:8], None, ALU.add)
                    dve.drain()
                    mean_square(x, 4, s_lnv)
                    r = reciprocal_root(s_lns, before + i + 1, 4)
                    nc.vector.scalar_tensor_tensor(out=x, in0=x, scalar=r, in1=table(g, "gv", ""), op0=ALU.mult, op1=ALU.mult)
                    dve.drain()
                    nc.vector.tensor_tensor(x, x, table(g, "bv", ""), ALU.add).then_inc(s_lnh, 1)
                    yield
                nc.vector.drain().then_inc(s_tabfree, 2)
                for i, t in enumerate(tiles):
                    bs = bsbs if t == SAMPLE else bsb[:]
                    for half in range(2):
                        f = turn_base(g, "gate") + 2 * i + half
                        src = read_turn(f)[:, :].rearrange("p (j n) -> p j n", j=4)
                        mixed = junk[:, half * 512:(half + 1) * 512].rearrange("p (j n) -> p j n", j=4)
                        uu = uT(g)[:, 4 * half:4 * half + 4, i * P:(i + 1) * P]
                        dve.drain()
                        nc.vector.tensor_tensor(mixed, src, bs[:, 4 * half:4 * half + 4, :], ALU.add)
                        dve.drain()
                        nc.vector.tensor_tensor(uu, uu, mixed, ALU.mult).then_inc(s_tfree[f % 2], 1)
                    yield

                if g == 0:
                    dve.wait_ge(s_gvst, 16)
                m = mT(g)
                for j in range(4):
                    for which in range(2):
                        f = fill_base(g, "merge") + 8 * j + 4 * which + 2
                        for b in range(2):
                            dve.wait_ge(s_free[(f - 2 + b) % 4], (f - 2 + b) // 4 + 1)
                            s = sg[:, 2 * which + b, 0:N]
                            src = read(f + b)[:, 0:N]
                            if which == 0:
                                ins = nc.vector.tensor_tensor(m[:, 2 * j + b, :], src, s, ALU.mult)
                            else:
                                nc.vector.tensor_tensor(s, src, s, ALU.mult)
                                dve.drain()
                                ins = nc.vector.tensor_tensor(m[:, 2 * j + b, :], m[:, 2 * j + b, :], s, ALU.add)
                            ins.then_inc(s_free[(f + b) % 4], 1)
                        yield

                dve.wait_ge(s_xr[g], 32 * T)
                for c in range(4):
                    for i, t in enumerate(tiles):
                        f = fill_base(g, "out") + c * T + i
                        cols = slice(c * WC, (c + 1) * WC)
                        part = junk[:, (f % 2) * 512:(f % 2) * 512 + WC]
                        gate = table(g, "G1", "s" if t == SAMPLE else "p")
                        nc.vector.tensor_tensor(part, read(f)[:, 0:WC], gate[:, cols], ALU.mult)
                        dve.drain()
                        x = vv[:, xslot_of(g, i), cols]
                        ins = nc.vector.tensor_tensor(x, x, part, ALU.add)
                        ins.then_inc(s_free[f % 4], 1)
                    yield
                nc.vector.drain().then_inc(s_tabfree, 2 if g == 0 else 1)

                for i, t in enumerate(tiles):
                    kind = "s" if t == SAMPLE else "p"
                    x, out = vv[:, xslot_of(g, i), :], h2(g, i)
                    dve.drain()
                    mean_square(x, 8, s_n2v)
                    r = reciprocal_root(s_n2s, before + i + 1, 8)
                    nc.vector.scalar_tensor_tensor(out=out, in0=x, scalar=r, in1=table(g, "A2", kind), op0=ALU.mult, op1=ALU.mult)
                    dve.drain()
                    nc.vector.tensor_tensor(out, out, table(g, "B2", kind), ALU.add).then_inc(s_n2h, 1)
                    if g == 0 or i == T - 1:
                        nc.vector.drain().then_inc(s_tabfree, 2)
                    yield

            loaded = dve.alloc_register("score_loads")
            raised = dve.alloc_register("exponentials_made")
            dve.reg_mov(loaded, 0)
            dve.reg_mov(raised, 0)

            def top16(sets, last=None):
                for src, _, values, _ in sets:
                    nc.vector.max(values[:, 0:8], src)
                dve.drain()
                for src, work_, values, places in sets:
                    nc.vector.max_index(places[:, 0:8], values[:, 0:8], src)
                    ins = nc.vector.match_replace(work_, values[:, 0:8], src, LOWEST)
                if last is not None:
                    ins.then_inc(last, 1)
                dve.drain()
                for _, work_, values, _ in sets:
                    nc.vector.max(values[:, 8:16], work_)
                dve.drain()
                for _, work_, values, places in sets:
                    nc.vector.max_index(places[:, 8:16], values[:, 8:16], work_)
                dve.drain()

            def choose(g, h):
                tiles = GROUPS[g]
                T = len(tiles)
                dve.reg_add(loaded, loaded, 16)
                dve.wait_ge(s_const, NCONST)
                dve.wait_ge(s_scld, loaded)
                top16([(sc[:, i, a, :], work[:, i, a * NKEY:(a + 1) * NKEY], top_v[:, i, a, :], top_i[:, i, a, :])
                       for i in range(T) for a in range(2)], s_tk)
                pairs = cand[:, 0:T].rearrange("p i (a b) -> p i a b", a=TOPK)
                nc.vector.tensor_copy(top_k[:, 0:T], top_i[:, 0:T])
                for i in range(T):
                    nc.vector.tensor_tensor(pairs[:, i], top_v[:, i, 0, :].unsqueeze(2).broadcast_to([P, TOPK, TOPK]),
                                            top_v[:, i, 1, :].unsqueeze(1).broadcast_to([P, TOPK, TOPK]), ALU.add)
                dve.drain()
                top16([(cand[:, i, :], work[:, i, :], best_v[:, i, :], best_i[:, i, :]) for i in range(T)])
                nc.vector.tensor_scalar(nmax[:, 0:T], best_v[:, 0:T, 0], -1.0, None, ALU.mult).then_inc(s_nb, 1)
                nc.vector.tensor_scalar(halves_i[:, 0, 0:T], best_i[:, 0:T], 4, None, ALU.logical_shift_right)
                nc.vector.tensor_scalar(halves_i[:, 1, 0:T], best_i[:, 0:T], TOPK - 1, None, ALU.bitwise_and)
                dve.drain()
                nc.vector.tensor_copy(halves[:, :, 0:T], halves_i[:, :, 0:T])
                dve.drain()
                hots = [buf[:, 0:T].rearrange("p i (j r) -> p i j r", r=TOPK) for buf in (work, cand)]
                for a in range(2):
                    nc.vector.tensor_tensor(hots[a].rearrange("p i j r -> p (i j) r"),
                                            halves[:, a, 0:T].rearrange("p i j -> p (i j)").unsqueeze(2).broadcast_to([P, T * TOPK, TOPK]),
                                            iota_f[:].unsqueeze(1).broadcast_to([P, T * TOPK, TOPK]), ALU.is_equal)
                dve.drain()
                for a in range(2):
                    nc.vector.tensor_tensor(hots[a], hots[a], top_k[:, 0:T, a, :].unsqueeze(2).broadcast_to([P, T, TOPK, TOPK]),
                                            ALU.mult)
                dve.drain()
                for a in range(2):
                    nc.vector.tensor_reduce(pick[:, a, 0:T].rearrange("p i j -> p (i j)"),
                                            hots[a].rearrange("p i j r -> p (i j) r"), AX.X, ALU.add)
                dve.drain()
                nc.vector.scalar_tensor_tensor(out=pick[:, 0, 0:T], in0=pick[:, 0, 0:T], scalar=float(NKEY),
                                               in1=pick[:, 1, 0:T], op0=ALU.mult, op1=ALU.add)
                dve.drain()
                for i, t in enumerate(tiles):
                    write_choice(expert, pick[:, 0, i, :], t, h)
                dve.drain()

            def write_choice(dst, src, t, h):
                if t == SAMPLE:
                    for half in range(2):
                        rows = slice(half * NS, (half + 1) * NS)
                        nc.vector.tensor_copy(dst[rows, t, bass.ds(h * (TOPK // 2), TOPK // 2)],
                                              src[rows, :].rearrange("p (k two) -> p k two", two=2)[:, :, half])
                else:
                    nc.vector.tensor_copy(dst[:, t, bass.ds(h * TOPK, TOPK)], src)

            def weigh(g, h):
                tiles = GROUPS[g]
                T = len(tiles)
                dve.reg_add(raised, raised, T)
                dve.wait_ge(s_const, NCONST)
                dve.wait_ge(s_ex, raised)
                nc.vector.reciprocal(esum[:, 1, 0:T], esum[:, 0, 0:T])
                dve.drain()
                nc.vector.tensor_tensor(expo[:, 0:T], expo[:, 0:T],
                                        esum[:, 1, 0:T].unsqueeze(2).broadcast_to([P, T, TOPK]), ALU.mult)
                dve.drain()
                for i, t in enumerate(tiles):
                    write_choice(gates, expo[:, i, :], t, h)
                dve.drain()

            def stage_rows(which, t, h, signal):
                nc.vector.tensor_copy(stage[:, which, :], expert[:, t, bass.ds(h * TOPK, TOPK)]).then_inc(signal, 1)

            def dots_of(t, h, batch, between):
                for k in range(TOPK):
                    if k == SLOTS and h is not None:
                        stage_rows(1, t, h - 1, s_up)
                    row = ring[:, k % SLOTS, :]
                    dve.wait_ge(s_gath[k % SLOTS], batch * 32 + 16 * (k // SLOTS + 1))
                    nc.vector.tensor_tensor_reduce(out=row, in0=row, in1=x_of[t], scale=1.0, scalar=0.0, op0=ALU.mult,
                                                   op1=ALU.add, accum_out=dots[:, k:k + 1]).then_inc(s_dotted, 1)
                    if k % 4 == 3:
                        between()
                nc.vector.drain().then_inc(s_dots, 1)

            def coefficients(t, h):
                dve.wait_ge(s_acts, h + (FIRST[t] + 1))
                if t not in WOVEN:
                    ins = nc.vector.tensor_tensor(coef[:], acts[:], gates[:, t, bass.ds(h * TOPK, TOPK)], ALU.mult)
                    ins.then_inc(s_coef, 1)
                else:
                    dve.drain()
                    nc.vector.tensor_tensor(coef[:], acts[:], gates[:, t, bass.ds(h * TOPK, TOPK)], ALU.mult)
                    dve.drain()

            def sums_of(n, batch, between):
                for k in range(TOPK):
                    row = ring[:, k % SLOTS, :]
                    a = acc[:, k % 2, :]
                    dve.wait_ge(s_gath[k % SLOTS], batch * 32 + 16 * (k // SLOTS + 1))
                    if n * TOPK + k - 1 > 0:
                        dve.wait_ge(s_summed, n * TOPK + k - 1)
                    nc.vector.scalar_tensor_tensor(out=a, in0=row, scalar=coef[:, k:k + 1], in1=a, op0=ALU.mult,
                                                   op1=ALU.add).then_inc(s_summed, 1)
                    if k % 4 == 3:
                        between()

            x_of = {t: h2(g, i) for g, ts in enumerate(GROUPS) for i, t in enumerate(ts)}

            for _ in front(0):
                pass
            other = front(1)

            for order, t in enumerate(ORDER):
                H, first, g = STEPS[t], FIRST[t], CHOOSING.get(t)
                nc.vector.drain().then_inc(s_ring, 1)
                if order:
                    dve.wait_ge(s_y, 16 * order)
                nc.vector.memset(acc[:], 0.0)
                nc.vector.drain().then_inc(s_zeroed, 1)
                if g is not None:
                    choose(g, 0)
                stage_rows(0, t, 0, s_dn)

                at = {"step": 0, "call": 0, "pieces": 0}
                calls = TOPK // 4

                def weave():
                    if t in WOVEN:
                        at["call"] += 1
                        in_step = calls if at["step"] in (0, 1) else 2 * calls
                        while at["pieces"] < DVE_PIECES[t][at["step"]] * at["call"] // in_step:
                            next(other, None)
                            at["pieces"] += 1
                        if at["call"] == in_step:
                            at.update(step=at["step"] + 1, call=0, pieces=0)

                dots_of(t, None, 2 * first, weave)
                if g is not None:
                    weigh(g, 0)
                    choose(g, 1)
                stage_rows(0, t, 1, s_dn)

                def step(h, last):
                    if g is not None:
                        weigh(g, h)
                    coefficients(t, h - 1)
                    dots_of(t, h, (h + first) * 2 - 1, weave)
                    if not last:
                        if g is not None:
                            choose(g, h + 1)
                        stage_rows(0, t, h + 1, s_dn)
                    if t in WOVEN:
                        sums_of(h + (first - 1), (h + first) * 2, weave)

                if t in WOVEN:
                    for h in range(1, H - 1):
                        step(h, False)
                else:
                    with dve.Fori(1, H - 1) as h:
                        step(h, False)
                step(H - 1, True)
                for slot in range(SLOTS):
                    dve.wait_ge(s_gath[slot], 32 * (2 * (first + H) - 1))
                stage_rows(1, t, H - 1, s_up)
                if t in WOVEN:
                    coefficients(t, H - 1)
                    sums_of(first + H - 1, 2 * (first + H) - 1, weave)
                else:
                    coefficients(t, H - 1)
                    dve.wait_ge(s_summed, (first + H) * TOPK)

                total = acc[:, 0, :]
                dve.drain()
                if t in WOVEN:
                    nc.vector.tensor_tensor(total, total, acc[:, 1, :], ALU.add)
                    dve.drain()
                dve.wait_ge(s_fin, 64 * (order + 1))
                if t == SAMPLE:
                    nc.vector.drain().then_inc(s_half, 1)
                    dve.wait_ge(s_fold, 16)
                    nc.vector.tensor_tensor(total[0:NS, :], total[0:NS, :], ring[0:NS, 3, :], ALU.add)
                    dve.drain()
                for half in range(2):
                    cols = slice(half * 512, (half + 1) * 512)
                    src = total[:, cols] if t in WOVEN else bank[6 + half][:, :]
                    nc.vector.tensor_tensor(total[:, cols], src, ring[:, 0, cols], ALU.mult)
                dve.drain()
                nc.vector.tensor_tensor(total, total, ring[:, 2, :], ALU.add)
                dve.drain()
                mean_square(total, 12, s_fv)
                r = reciprocal_root(s_fs, order + 1, 12)
                nc.vector.scalar_tensor_tensor(out=total, in0=total, scalar=r, in1=ring[:, 1, :], op0=ALU.mult,
                                               op1=ALU.mult).then_inc(s_fy, 1)
                if t == WOVEN[-1]:
                    for _ in other:
                        pass


_OUTS = [((1, SEQ, D), "y_prompt"), ((NDEC, DSEQ, D), "y_sample"),
         ((1, 1, SEQ, NH, P), "new_k_prompt"), ((1, 1, SEQ, NH, P), "new_v_prompt"),
         ((1, NDEC, DSEQ, NH, P), "new_k_sample"), ((1, NDEC, DSEQ, NH, P), "new_v_sample"),
         ((1, NDEC, DSEQ, NH, P), "new_gmlp_v_sample")]
_INS = ["x_prompt", "x_sample", "cache_k", "cache_v", "page_table", "c_prompt", "c_sample", "w_ada", "b_ada",
        "g_norm1", "w_in", "sb_bias", "g_v", "b_v", "w_spatial", "b_spatial", "w_branch_a", "w_branch_b",
        "w_out", "g_norm2", "w_query", "sub_keys", "expert_down", "expert_up", "g_final"]


def kernel(**inputs):
    import concourse.bacc as bacc
    from concourse.bass_utils import run_bass_kernel_spmd

    nc = bacc.Bacc("TRN2", target_bir_lowering=False, num_devices=1)
    arrays, args = {}, []
    for name in _INS:
        a = np.ascontiguousarray(inputs[name])
        arrays[f"in_{name}"] = a
        args.append(nc.dram_tensor(f"in_{name}", a.shape, mybir.dt.from_np(a.dtype), kind="ExternalInput").ap())
    for shape, name in _OUTS:
        args.append(nc.dram_tensor(f"out_{name}", shape, F32, kind="ExternalOutput").ap())
    build(nc, *args)
    got = run_bass_kernel_spmd(nc, [arrays], core_ids=[0])
    return tuple(got.results[0][f"out_{name}"] for _, name in _OUTS)
```

```python
from contextlib import ExitStack
from itertools import chain

import numpy as np

import concourse.bass as bass
from concourse import mybir

ALU = mybir.AluOpType
ACT = mybir.ActivationFunctionType
AX = mybir.AxisListType
F32 = mybir.dt.float32
I32 = mybir.dt.int32
U32 = mybir.dt.uint32

P = 128
D = 1024
KC = D // P
WC = 256
NH = 8
SEQ, NDEC, DSEQ = 512, 8, 8
NS = NDEC * DSEQ
NG = 1 + NDEC
NMOD = 6
TOPK = 16
NKEY = 128
SCALE = float(P) ** -0.5
EPS = 1e-6
LOWEST = -3.0e38
MASKED = -1.0e30
SLOTS = 8
TILES = 5
SAMPLE = 4
GROUPS = [[0, SAMPLE], [1, 2, 3]]
NADA = NMOD * D // WC
NCH = 48

ORDER = [0, SAMPLE, 1, 2, 3]
STEPS = {0: 8, SAMPLE: 4, 1: 8, 2: 8, 3: 8}
FIRST = {t: sum(STEPS[o] for o in ORDER[:ORDER.index(t)]) for t in ORDER}
CHOOSING = {0: 0, 1: 1}
WOVEN = [0, SAMPLE]
LATER = [1, 2, 3]
END_SLOT = {0: 5, SAMPLE: 0}
DVE_PIECES = {0: [0, 0, 0, 0, 0, 0, 0, 0, 2], SAMPLE: [1, 2, 3, 4, 0]}
ACT_PIECES = {0: [7, 3, 6, 5, 5, 5, 3, 2, 2], SAMPLE: [3, 1, 3, 1, 2]}


def slot_of(g, i):
    return i if g == 0 else 1 + i


def xslot_of(g, i):
    return 2 + i if g == 0 else 1 + i


def fill_base(g, phase):
    t = len(GROUPS[g])
    base = NADA if g == 0 else NADA + 64 + 16 * len(GROUPS[0])
    return base + {"q": 0, "k": 8, "v": 8 + 4 * t, "u": 8 + 8 * t, "gv": 16 + 8 * t,
                   "merge": 16 + 12 * t, "out": 48 + 12 * t, "query": 48 + 16 * t}[phase]


def turn_base(g, phase):
    t = len(GROUPS[g])
    base = 8 if g == 0 else 8 + 10 * len(GROUPS[0])
    return base + {"norm1": 0, "kT": 2 * t, "gate": 6 * t, "norm2": 8 * t}[phase]


def chunk_base(g, phase):
    return NADA + NCH * g + {"q": 0, "k": 4, "v": 8, "u": 12, "gv": 16, "merge": 20, "out": 36, "query": 40}[phase]


def last_fill(n):
    if n < NADA:
        return n
    g, m = divmod(n - NADA, NCH)
    t = len(GROUPS[g])
    for phase, fills in (("query", 2), ("out", t), ("merge", 2), ("gv", t), ("u", 2), ("v", t), ("k", t), ("q", 2)):
        c = n - chunk_base(g, phase)
        if c >= 0:
            return fill_base(g, phase) + fills * (c + 1) - 1


def tables(g):
    if g == 0:
        return [("A1", "p"), ("B1", "p"), ("A1", "s"), ("B1", "s"), ("gv", ""), ("bv", ""),
                ("G1", "p"), ("G1", "s"), ("A2", "p"), ("B2", "p"), ("A2", "s"), ("B2", "s")]
    return [("A1", "p"), ("B1", "p"), ("gv", ""), ("bv", ""), ("G1", "p"), ("A2", "p"), ("B2", "p")]


def table_number(g, what, kind):
    return (len(tables(0)) if g else 0) + tables(g).index((what, kind))


def build(nc, x_prompt, x_sample, cache_k, cache_v, page_table, c_prompt, c_sample, w_ada, b_ada,
          g_norm1, w_in, sb_bias, g_v, b_v, w_spatial, b_spatial, w_branch_a, w_branch_b, w_out,
          g_norm2, w_query, sub_keys, expert_down, expert_up, g_final,
          y_prompt, y_sample, nk_prompt, nv_prompt, nk_sample, nv_sample, ngv_sample):
    n_phys = cache_k.shape[1]
    xp = x_prompt.rearrange("b (t p) d -> (b t) p d", p=P)
    xs = x_sample.rearrange("b i d -> (b i) d")
    kpages = cache_k.rearrange("l n p h d -> (l n p) (h d)")
    vpages = cache_v.rearrange("l n p h d -> (l n p) (h d)")
    yp = y_prompt.rearrange("b (t p) d -> (b t) p d", p=P)
    ys = y_sample.rearrange("b i d -> (b i) d")
    nkp = nk_prompt.rearrange("l b (t p) h d -> (l b t) p (h d)", p=P)
    nvp = nv_prompt.rearrange("l b (t p) h d -> (l b t) p (h d)", p=P)
    nks = nk_sample.rearrange("l b i h d -> (l b i) (h d)")
    nvs = nv_sample.rearrange("l b i h d -> (l b i) (h d)")
    ngs = ngv_sample.rearrange("l b i h d -> (l b i) (h d)")
    down = expert_down.rearrange("l e d -> (l e) d")
    up = expert_up.rearrange("l e d -> (l e) d")

    def weights(w):
        return w.rearrange("l (k p) n -> p (l k) n", p=P)

    wv = {"ada": weights(w_ada), "in": weights(w_in), "ba": weights(w_branch_a),
          "bb": weights(w_branch_b), "out": weights(w_out), "query": weights(w_query)}

    mod_p = nc.dram_tensor("mod_prompt", (1, NMOD * D), F32, kind="Internal").ap()
    mod_s = nc.dram_tensor("mod_sample", (NS, NMOD * D), F32, kind="Internal").ap()
    score_dram = [nc.dram_tensor(f"key_scores_{g}", (NH * P, len(ts) * 2 * NKEY), F32, kind="Internal").ap()
                  for g, ts in enumerate(GROUPS)]
    x1_dram = nc.dram_tensor("x1_tiles", (TILES, P, D), F32, kind="Internal").ap()

    with ExitStack() as ctx:
        def sb(name, shape, dt=F32):
            return ctx.enter_context(nc.sbuf_tensor(name, shape, dt))

        def sem(name):
            return ctx.enter_context(nc.semaphore(name))

        bank = [ctx.enter_context(nc.psum_tensor(f"bank{i}", [P, 512], F32)) for i in range(8)]

        ring = sb("gather_ring", [P, SLOTS, D])
        wbuf = sb("weight_chunks", [P, 4, KC, WC])
        h2keep = sb("h2_group0", [P, 2, D])
        hTf = sb("hT", [P, 3072])
        kT = sb("kT", [P, 4, NH, P])
        vv = sb("v_tokens", [P, 4, D])
        qTf = sb("qT", [P, 3072])
        U = sb("u_and_gv", [P, 6144])
        sg = sb("sigmoids", [P, 4, 384])
        tab = sb("row_tables", [P, 3, D])
        acc = sb("expert_sums", [P, 2, D])
        WsT = sb("spatialT", [P, NH, P])
        bsb = sb("spatial_bias", [P, NH, P])
        skT = sb("sub_keysT", [P, 2, NKEY])
        junk = sb("scratch_row", [P, D])
        ident = sb("identity", [P, P])
        later = sb("later_keys", [P, P])
        ones = sb("ones", [P, P])
        since = sb("since_keys", [P, P])
        hidden = sb("hidden_keys", [P, P])
        expert = sb("expert_numbers", [P, TILES, P], I32)
        gates = sb("expert_gates", [P, TILES, P])
        stage = sb("gather_rows", [P, 2, TOPK], I32)
        cT = sb("condT", [P, KC, NG])
        bias_b = sb("stick_bias", [P, NH])
        iota_i = sb("iota_int", [P, TOPK], I32)
        iota_f = sb("iota", [P, TOPK])
        st = sb("norm_stats", [P, 16])
        dots = sb("expert_dots", [P, 2, TOPK])
        acts = sb("expert_acts", [P, 2, TOPK])
        coef = sb("expert_coefs", [P, TOPK])
        pt_sb = sb("page_numbers", [1, 2 * NDEC], I32)
        nbias_b = sb("minus_stick_bias", [P, NH])
        sc = sb("key_scores", [P, 3, 2, NKEY])
        work = junk[:, 0:6 * NKEY].rearrange("p (i n) -> p i n", i=3)
        cand = sb("pair_scores", [P, 3, TOPK * TOPK])
        top_v = sb("top_values", [P, 3, 2, TOPK])
        top_i = sb("top_places", [P, 3, 2, TOPK], U32)
        top_k = sb("top_keys", [P, 3, 2, TOPK])
        best_v = sb("best_values", [P, 3, TOPK])
        best_i = sb("best_places", [P, 3, TOPK], U32)
        halves_i = top_i[:].rearrange("p i a k -> p (i a k)").rearrange("p (a i k) -> p a i k", a=2, i=3)
        halves = sb("best_halves", [P, 2, 3, TOPK])
        pick = halves
        nmax = sb("minus_best", [P, 3])
        expo = sb("exponentials", [P, 3, TOPK])
        esum = sb("exponential_sums", [P, 2, 3])

        flat = ring[:, :, :].rearrange("p s d -> p (s d)")
        mod9 = flat[0:NG, 0:NMOD * D]
        c9 = flat[0:NG, 6144:7168]
        g1row = flat[0:NG, 7168:8192]
        g2row = acc[0:NG, 0, :]
        ws_nat = U[:, 2048:3072].rearrange("p (g s) -> p g s", g=NH)
        wss_nat = U[:, 5120:6144].rearrange("p (g s) -> p g s", g=NH)
        WsTs = hTf[:, 2048:3072].rearrange("p (g t) -> p g t", g=NH)
        bsbs = qTf[:, 2048:3072].rearrange("p (g t) -> p g t", g=NH)
        sk_nat = sg[:, 2, 0:256].rearrange("p (a d) -> p a d", a=2)
        causal = sg[:, 0, 0:P]

        def width(g):
            return P * len(GROUPS[g])

        def distinct(g):
            return width(g) - (P - NS) * (SAMPLE in GROUPS[g])

        def hT(g):
            return hTf[:, 0:KC * width(g)].rearrange("p (k n) -> p k n", k=KC)

        def qT(g):
            return qTf[:, 0:NH * width(g)].rearrange("p (k n) -> p k n", k=NH)

        def uT(g):
            return U[:, 0:NH * width(g)].rearrange("p (k n) -> p k n", k=NH)

        def mT(g):
            return U[:, 3072:3072 + NH * width(g)].rearrange("p (k n) -> p k n", k=NH)

        def gvt(i):
            return U[:, 3072 + D * i:3072 + D * (i + 1)]

        def h2(g, i):
            return h2keep[:, i, :] if g == 0 else gvt(i)

        def att(what, n):
            at = {"log": 0, "pos": 2048, "neg": 4096}[what] + 512 * (n % 4)
            return U[:, at:at + 512]

        def head_pairs(g):
            items = [(i, t, hd) for i, t in enumerate(GROUPS[g]) if t != SAMPLE for hd in range(NH)]
            first = NH * sum(t != SAMPLE for ts in GROUPS[:g] for t in ts)
            items = [(first + w, *item) for w, item in enumerate(items)]
            return [items[w:w + 2] for w in range(0, len(items), 2)]

        kTf = kT[:, 2:4].rearrange("p s h d -> p (s h d)")
        vf = vv[:, 2:4].rearrange("p s d -> p (s d)")
        ef = ring[:, 6:8].rearrange("p s d -> p (s d)")
        pos_s = [kTf[:, 0:512], kTf[:, 512:1024], kTf[0:NS, 1024:1536]]
        neg_s = [vf[:, 0:512], vf[:, 512:1024], vf[0:NS, 1024:1536]]
        bias_row = ef[0:1, 1536:2048]
        log_s = [ef[:, 0:512], ef[:, 512:1024], ef[0:NS, 1024:1536]]

        diag = acc[:, 1, :].rearrange("p (k n) -> p k n", k=SLOTS)

        hidden_s = cand[0:NS, 0, 0:NS]

        def end_rows(t):
            return [ring[:, END_SLOT[t] + r, :] for r in range(3)]

        qh = U[:, 0:1536].rearrange("p (b a n) -> p b a n", b=2, a=2)
        sc_out = U[:, 1536:3072].rearrange("p (b n) -> p b n", b=2)

        s_const = sem("s_const")
        s_cond = sem("s_cond")
        s_small = sem("s_small")
        s_pt = sem("s_pt")
        s_silu = sem("s_silu")
        s_zero = sem("s_zero")
        s_wss = sem("s_wss")
        s_mod = sem("s_mod")
        s_modst = sem("s_modst")
        s_wload = [sem(f"s_wload{i}") for i in range(4)]
        s_full = [sem(f"s_full{i}") for i in range(4)]
        s_free = [sem(f"s_free{i}") for i in range(4)]
        s_tfull = [sem(f"s_tfull{i}") for i in range(2)]
        s_tfree = [sem(f"s_tfree{i}") for i in range(2)]
        s_tab = [sem(f"s_tab{i}") for i in range(3)]
        s_tabfree = sem("s_tabfree")
        s_x = [sem("s_x_g0"), sem("s_x_g1")]
        s_xr = [sem("s_xr_g0"), sem("s_xr_g1")]
        s_n1v, s_n1s, s_n1h = sem("s_n1v"), sem("s_n1s"), sem("s_n1h")
        s_n2v, s_n2s, s_n2h = sem("s_n2v"), sem("s_n2s"), sem("s_n2h")
        s_lnv, s_lns, s_lnh = sem("s_lnv"), sem("s_lns"), sem("s_lnh")
        s_kst = sem("s_kst")
        s_vst = sem("s_vst")
        s_gvst = sem("s_gvst")
        s_az = sem("s_az")
        s_ar = sem("s_ar")
        s_al = sem("s_al")
        s_ac = sem("s_ac")
        s_aw = sem("s_aw")
        s_ao = sem("s_ao")
        s_ae = sem("s_ae")
        s_page = [sem(f"s_page{i}") for i in range(4)]
        s_ktf = [sem("s_ktf0"), sem("s_ktf1")]
        s_kte = sem("s_kte")
        s_sz = sem("s_sz")
        s_sn = sem("s_sn")
        s_sl = sem("s_sl")
        s_scm = sem("s_scm")
        s_sw = sem("s_sw")
        s_sv = sem("s_sv")
        s_se = sem("s_se")
        s_twice = sem("s_twice")
        s_bias = sem("s_bias")
        s_x1st = sem("s_x1st")
        s_sfull = [sem(f"s_sfull{i}") for i in range(3)]
        s_sev = [sem(f"s_sev{i}") for i in range(3)]
        s_scst = [sem("s_scst0"), sem("s_scst1")]
        s_scld = sem("s_scld")
        s_tk = sem("s_tk")
        s_nb = sem("s_nb")
        s_ex = sem("s_ex")
        s_dn = sem("s_dn")
        s_up = sem("s_up")
        s_gath = [sem(f"s_gath{i}") for i in range(SLOTS)]
        s_ring = sem("s_ring")
        s_dotted = sem("s_dotted")
        s_summed = sem("s_summed")
        s_ended = sem("s_ended")
        s_diag = sem("s_diag")
        s_dots = sem("s_dots")
        s_acts = sem("s_acts")
        s_coef = sem("s_coef")
        s_fin = sem("s_fin")
        s_half = sem("s_half")
        s_fold = sem("s_fold")
        s_fv, s_fs, s_fy = sem("s_fv"), sem("s_fs"), sem("s_fy")
        s_y = sem("s_y")

        NCONST = 14

        def evacuated(eng, f):
            for b in range(4):
                n = (f - b + 3) // 4
                if n > 0:
                    eng.wait_ge(s_free[b], n)

        def turned(eng, t):
            for b in range(2):
                eng.wait_ge(s_tfree[b], (t - b + 1) // 2)

        block = ctx.enter_context(nc.Block())

        @block.sync
        def _(sp):
            def load_weight(n, src):
                if n >= 4:
                    f = last_fill(n - 4)
                    sp.wait_ge(s_full[f % 4], f // 4 + 1)
                sp.dma_start(wbuf[:, n % 4], src).then_inc(s_wload[n % 4], 16)

            def columns(name, at):
                return wv[name][:, :, at:at + WC]

            def load_table(g, what, kind):
                n = table_number(g, what, kind)
                if n >= 3:
                    sp.wait_ge(s_tabfree, n - 2)
                dst = tab[:, n % 3, :]
                if what in ("gv", "bv"):
                    sp.dma_start(dst, (g_v if what == "gv" else b_v).broadcast_to([P, D])).then_inc(s_tab[n % 3], 32)
                    return
                m = {"B1": 0, "A1": 1, "G1": 2, "B2": 3, "A2": 4}[what]
                if kind == "p":
                    sp.dma_start(dst, mod_p[:, m * D:(m + 1) * D].broadcast_to([P, D])).then_inc(s_tab[n % 3], 32)
                else:
                    for half in range(2):
                        sp.dma_start(tab[half * NS:(half + 1) * NS, n % 3, :],
                                     mod_s[:, m * D:(m + 1) * D]).then_inc(s_tab[n % 3], 16)

            def load_x(g, slots, signal):
                for i, t in enumerate(GROUPS[g]):
                    dst = vv[:, slots[i], :]
                    if t == SAMPLE:
                        for half in range(2):
                            sp.dma_start(vv[half * NS:(half + 1) * NS, slots[i], :], xs).then_inc(signal, 16)
                    else:
                        sp.dma_start(dst, xp[t]).then_inc(signal, 32)

            sp.dma_start(c9[0:1, :], c_prompt).then_inc(s_cond, 16)
            sp.dma_start(c9[1:NG, :], c_sample).then_inc(s_cond, 16)
            for n in range(4):
                load_weight(n, columns("ada", n * WC))
            sp.dma_start(mod9, b_ada.broadcast_to([NG, NMOD * D])).then_inc(s_cond, 16)
            sp.dma_start(g1row, g_norm1.broadcast_to([NG, D])).then_inc(s_cond, 16)
            sp.dma_start(g2row, g_norm2.broadcast_to([NG, D])).then_inc(s_cond, 16)
            sp.dma_start(pt_sb[:], page_table.rearrange("(o b) n -> o (b n)", o=1)).then_inc(s_pt, 16)
            sp.dma_start(ws_nat, w_spatial.rearrange("l g t s -> t (l g) s")).then_inc(s_small, 16)
            sp.dma_start(sk_nat, sub_keys.rearrange("l a k d -> k (l a) d")).then_inc(s_small, 16)
            sp.dma_start(bias_b[:], sb_bias.broadcast_to([P, NH])).then_inc(s_small, 16)
            sp.dma_start(bsb[:].rearrange("p g t -> p (g t)"),
                         b_spatial.rearrange("l g t -> l (g t)").broadcast_to([P, NH * P])).then_inc(s_small, 16)
            for b in range(P // DSEQ):
                sp.dma_start(bsbs[:, :, b * DSEQ:(b + 1) * DSEQ],
                             b_spatial[:, :, 0:DSEQ].broadcast_to([P, NH, DSEQ])).then_inc(s_small, 16)
            sp.wait_ge(s_zero, 1)
            for b in range(P // DSEQ):
                sp.dma_start(wss_nat[b * DSEQ:(b + 1) * DSEQ, :, b * DSEQ:(b + 1) * DSEQ],
                             w_spatial[0, :, 0:DSEQ, 0:DSEQ].rearrange("g t s -> t g s")).then_inc(s_wss, 16)
            load_x(0, [slot_of(0, i) for i in range(2)], s_x[0])
            for n in range(4, NADA):
                load_weight(n, columns("ada", n * WC))
            sp.wait_ge(s_pt, 16)
            page_number = [sp.value_load(pt_sb[0:1, m:m + 1], min_val=0, max_val=n_phys - 1) for m in range(2 * NDEC)]
            evacuated(sp, NADA)
            sp.wait_ge(s_mod, 2)
            sp.dma_start(mod_p, mod9[0:1, :]).then_inc(s_modst, 16)
            sp.dma_start(mod_s.rearrange("(b i) n -> b i n", i=DSEQ),
                         mod9[1:NG, :].unsqueeze(1).broadcast_to([NDEC, DSEQ, NMOD * D])).then_inc(s_modst, 16)
            sp.wait_ge(s_modst, 32)

            for g, tiles in enumerate(GROUPS):
                T = len(tiles)
                before = sum(len(GROUPS[j]) for j in range(g))
                def load_merge(j, part):
                    name, at = (("in", 5 * D), ("ba", 0), ("in", 6 * D), ("bb", 0))[part]
                    load_weight(chunk_base(g, "merge") + 4 * j + part, columns(name, at + j * WC))

                for n in range(4):
                    load_weight(chunk_base(g, "q") + n, columns("in", n * WC))
                if g == 0:
                    for w in ("A1", "B1"):
                        load_table(g, w, "p")
                    for w in ("A1", "B1"):
                        load_table(g, w, "s")
                for n in range(4, 12):
                    load_weight(chunk_base(g, "q") + n, columns("in", n * WC))
                evacuated(sp, fill_base(g, "k") + 4 * T)
                for i, t in enumerate(tiles):
                    if t == SAMPLE:
                        sp.dma_start(nks, gvt(i)[0:NS, :]).then_inc(s_kst, 16)
                    else:
                        sp.dma_start(nkp[t], gvt(i)).then_inc(s_kst, 16)
                evacuated(sp, fill_base(g, "v") + 4 * T)
                for i, t in enumerate(tiles):
                    if t == SAMPLE:
                        sp.dma_start(nvs, vv[0:NS, slot_of(g, i), :]).then_inc(s_vst, 16)
                    else:
                        sp.dma_start(nvp[t], vv[:, slot_of(g, i), :]).then_inc(s_vst, 16)
                for n in range(12, 16):
                    load_weight(chunk_base(g, "q") + n, columns("in", n * WC))
                load_table(g, "gv", "")
                load_table(g, "bv", "")
                if g == 0:
                    for m in range(4 * NDEC):
                        number = page_number[m % (2 * NDEC)]
                        if 4 <= m < 2 * NDEC + 4:
                            sp.wait_ge(s_ktf[1], m - 3)
                        elif m >= 2 * NDEC + 4:
                            sp.wait_ge(s_sv, (m - 4 - 2 * NDEC) // 2 + 1)
                        store = kpages if m < 2 * NDEC else vpages
                        sp.dma_start(ring[:, m % 4, :], store[bass.ds(number * P, P), :]).then_inc(s_page[m % 4], 16)
                        if 2 * NDEC <= m < 2 * NDEC + 4:
                            load_merge(0, m - 2 * NDEC)
                        if m in (6, 8, 10, 12):
                            n = 16 + (m - 6) // 2
                            load_weight(chunk_base(g, "q") + n, columns("in", n * WC))
                else:
                    for n in range(16, 20):
                        load_weight(chunk_base(g, "q") + n, columns("in", n * WC))
                if g == 0:
                    sp.wait_ge(s_lnh, 2)
                    sp.dma_start(ngs, gvt(1)[0:NS, :]).then_inc(s_gvst, 16)
                load_table(g, "G1", "p")
                if g == 0:
                    load_table(g, "G1", "s")
                sp.wait_ge(s_ae, NH * (1 if g == 0 else 4))
                if g == 0:
                    sp.wait_ge(s_se, 1)
                sp.wait_ge(s_vst, 16 * (before + T))
                load_x(g, [xslot_of(g, i) for i in range(T)], s_xr[g])
                for j in range(4):
                    for part in range(4):
                        if g or j:
                            load_merge(j, part)
                for c in range(4):
                    load_weight(chunk_base(g, "out") + c, columns("out", c * WC))
                load_table(g, "A2", "p")
                load_table(g, "B2", "p")
                if g == 0:
                    load_table(g, "A2", "s")
                    load_table(g, "B2", "s")
                for c in range(4):
                    load_weight(chunk_base(g, "query") + c, columns("query", c * WC))
                evacuated(sp, fill_base(g, "out") + 4 * T)
                for i, t in enumerate(tiles):
                    sp.dma_start(x1_dram[t], vv[:, xslot_of(g, i), :]).then_inc(s_x1st, 16)
                if g == 0:
                    sp.wait_ge(s_x1st, 16 * T)
                    sp.wait_ge(s_n2h, T)
                    load_x(1, [slot_of(1, i) for i in range(3)], s_x[1])
                    for w in ("A1", "B1"):
                        load_table(1, w, "p")
                for c in range(4, 8):
                    load_weight(chunk_base(g, "query") + c, columns("query", c * WC))
            sp.wait_ge(s_kst, 16 * TILES)
            sp.wait_ge(s_vst, 16 * TILES)
            sp.wait_ge(s_gvst, 16)
            sp.wait_ge(s_x1st, 16 * TILES)
            sp.wait_ge(s_y, 16 * TILES)

        @block.gpsimd
        def _(pool):
            done = [0]

            def const(ins):
                done[0] += 1
                ins.then_inc(s_const, 1)
                pool.wait_ge(s_const, done[0])

            const(nc.gpsimd.memset(ident[:], 0.0))
            const(nc.gpsimd.affine_select(out=ident[:], in_=ident[:], compare_op=ALU.not_equal, fill=1.0,
                                          base=0, pattern=[[-1, P]], channel_multiplier=1))
            const(nc.gpsimd.memset(ones[:], 1.0))
            const(nc.gpsimd.affine_select(out=later[:], in_=ones[:], compare_op=ALU.is_gt, fill=0.0,
                                          base=0, pattern=[[-1, P]], channel_multiplier=1))
            const(nc.gpsimd.affine_select(out=since[:], in_=ones[:], compare_op=ALU.is_ge, fill=0.0,
                                          base=0, pattern=[[-1, P]], channel_multiplier=1))
            const(nc.gpsimd.memset(hidden[:], 0.0))
            const(nc.gpsimd.affine_select(out=hidden[:], in_=hidden[:], compare_op=ALU.is_gt, fill=MASKED,
                                          base=0, pattern=[[1, P]], channel_multiplier=-1))
            const(nc.gpsimd.affine_select(out=causal, in_=ones[:], compare_op=ALU.is_ge, fill=0.0,
                                          base=0, pattern=[[1, P]], channel_multiplier=-1))
            blocks = hidden_s.rearrange("p (b i) -> p b i", i=DSEQ)
            const(nc.gpsimd.affine_select(out=blocks, in_=hidden[0:NS, 0:NS].rearrange("p (b i) -> p b i", i=DSEQ),
                                          compare_op=ALU.is_ge, fill=MASKED, base=0,
                                          pattern=[[-DSEQ, NDEC], [0, DSEQ]], channel_multiplier=1))
            const(nc.gpsimd.affine_select(out=blocks, in_=blocks, compare_op=ALU.is_ge, fill=MASKED, base=DSEQ - 1,
                                          pattern=[[DSEQ, NDEC], [0, DSEQ]], channel_multiplier=-1))
            const(nc.gpsimd.iota(iota_i[:], pattern=[[1, TOPK]], base=0, channel_multiplier=0))
            const(nc.gpsimd.tensor_copy(iota_f[:], iota_i[:]))
            const(nc.gpsimd.memset(wss_nat, 0.0))
            const(nc.gpsimd.memset(stage[:], 0))
            assert done[0] == NCONST

            rows_used = {s_dotted: pool.alloc_register("dotted_rows"), s_summed: pool.alloc_register("summed_rows")}
            for r in rows_used.values():
                pool.reg_mov(r, 0)

            def used(signal):
                pool.reg_add(rows_used[signal], rows_used[signal], 1)
                pool.wait_ge(s_const, NCONST)
                pool.wait_ge(signal, rows_used[signal])

            def gather(table, which, own, before, ring_free=None):
                for k in range(TOPK):
                    if ring_free is not None and k == ring_free[0]:
                        pool.wait_ge(s_ring, ring_free[1])
                    if k >= SLOTS:
                        used(own)
                    elif before is not None:
                        used(before)
                    pool.indirect_dma_start(
                        out=ring[:, k % SLOTS, :], out_offset=None, in_=table,
                        in_offset=bass.IndirectOffsetOnAxis(ap=stage[:, which, k:k + 1], axis=0),
                    ).then_inc(s_gath[k % SLOTS], 16)

            def gather_down(n, before, ring_free=None):
                pool.wait_ge(s_dn, n)
                gather(down, 0, s_dotted, before, ring_free)

            def gather_up(n, before):
                pool.wait_ge(s_up, n)
                gather(up, 1, s_summed, before)

            def load_scores(g, h):
                last = h if isinstance(h, int) else NH - 1
                for b in range(min(last + 1, 2)):
                    pool.wait_ge(s_scst[b], 16 * ((NH // 2) * g + (last - b) // 2 + 1))
                if isinstance(h, int):
                    if g + h:
                        pool.wait_ge(s_tk, NH * g + h)
                else:
                    pool.wait_ge(s_tk, h + NH * g)
                T = len(GROUPS[g])
                pool.dma_start(sc[:, 0:T].rearrange("p i a k -> p (i a k)"),
                               score_dram[g][bass.ds(h * P, P), :]).then_inc(s_scld, 16)

            def first_steps(t, ring_free, at_once=0):
                first, g = FIRST[t], CHOOSING.get(t)
                if g is not None:
                    load_scores(g, 0)
                    load_scores(g, 1)
                gather_down(first + 1, None, (at_once, ring_free))
                if g is not None:
                    load_scores(g, 2)
                gather_down(first + 2, s_dotted)
                gather_up(first + 1, s_dotted)

            def further_steps(t):
                H, first, g = STEPS[t], FIRST[t], CHOOSING.get(t)
                if g is not None:
                    with pool.Fori(2, H - 1) as h:
                        load_scores(g, h + 1)
                        gather_down(h + (first + 1), s_summed)
                        gather_up(h + first, s_dotted)
                    gather_down(first + H, s_summed)
                    gather_up(first + H - 1, s_dotted)
                else:
                    with pool.Fori(2, H) as h:
                        gather_down(h + (first + 1), s_summed)
                        gather_up(h + first, s_dotted)

            def load_ends(t, gate, gain, residual):
                if t == SAMPLE:
                    for half in range(2):
                        pool.dma_start(gate[half * NS:(half + 1) * NS, :], mod_s[:, 5 * D:6 * D]).then_inc(s_fin, 16)
                else:
                    pool.dma_start(gate, mod_p[:, 5 * D:6 * D].broadcast_to([P, D])).then_inc(s_fin, 32)
                pool.dma_start(gain, g_final.rearrange("(o d) -> o d", o=1).broadcast_to([P, D])).then_inc(s_fin, 16)
                pool.dma_start(residual, x1_dram[t]).then_inc(s_fin, 16)

            for order, t in enumerate(WOVEN):
                H, first = STEPS[t], FIRST[t]
                first_steps(t, order + 1, END_SLOT[WOVEN[order - 1]] if order else 0)
                further_steps(t)
                gather_up(first + H, s_summed)
                pool.wait_ge(s_summed, TOPK * (first + H))
                pool.reg_add(rows_used[s_summed], rows_used[s_summed], SLOTS)
                load_ends(t, *end_rows(t))
                if t == SAMPLE:
                    pool.wait_ge(s_half, 1)
                    pool.dma_start(ring[0:NS, 3, :], acc[NS:P, 0, :]).then_inc(s_fold, 16)

            for order, t in enumerate(LATER):
                H, first = STEPS[t], FIRST[t]
                if order == 0:
                    first_steps(t, len(WOVEN) + 1)
                    pool.wait_ge(s_tabfree, len(tables(0)) + len(tables(1)))
                else:
                    for h in range(2):
                        gather_down(first + h + 1, s_summed)
                        gather_up(first + h, s_dotted)
                    pool.wait_ge(s_ended, order)
                load_ends(t, tab[:, 0, :], tab[:, 1, :], tab[:, 2, :])
                further_steps(t)
            gather_up(first + H, s_summed)

        @block.tensor
        def _(pe):
            def weight(n):
                pe.wait_ge(s_wload[n % 4], 16 * (n // 4 + 1))
                return wbuf[:, n % 4]

            def take(f):
                if f >= 4:
                    pe.wait_ge(s_free[f % 4], f // 4)
                return bank[f % 4]

            def take_turn(t):
                if t >= 2:
                    pe.wait_ge(s_tfree[t % 2], t // 2)
                return bank[4 + t % 2]

            def token_major(n, f, src):
                w = weight(n)
                out = take(f)
                for k in range(KC):
                    mm = nc.tensor.matmul(out[:, 0:WC], src[:, k, :], w[:, k, :], start=(k == 0), stop=(k == KC - 1))
                mm.then_inc(s_full[f % 4], 1)
                return mm

            def channel_block(n, f, j, src, N):
                w = weight(n)
                out = take(f)
                for k in range(KC):
                    mm = nc.tensor.matmul(out[:, 0:N], w[:, k, j * P:(j + 1) * P], src[:, k, 0:N],
                                          start=(k == 0), stop=(k == KC - 1))
                mm.then_inc(s_full[f % 4], 1)

            def channel_major(n, f, src, N):
                for j in range(2):
                    channel_block(n, f + j, j, src, N)

            def turn_four(t, blocks):
                out = take_turn(t)
                for j, b in enumerate(blocks):
                    mm = nc.tensor.transpose(out[0:b.shape[1], j * P:j * P + b.shape[0]], b, ident[0:b.shape[0], 0:b.shape[0]])
                mm.then_inc(s_tfull[t % 2], 1)

            pe.wait_ge(s_const, NCONST)
            pe.wait_ge(s_silu, 1)
            for t in range(2):
                out = take_turn(t)
                for j in range(4):
                    k = 4 * t + j
                    mm = nc.tensor.transpose(out[:, j * NG:(j + 1) * NG], c9[:, k * P:(k + 1) * P], ident[0:NG, 0:NG])
                mm.then_inc(s_tfull[t], 1)
            pe.wait_ge(s_tfree[0], 1)
            pe.wait_ge(s_tfree[1], 1)
            for n in range(NADA):
                w = weight(n)
                out = take(n)
                for k in range(KC):
                    mm = nc.tensor.matmul(out[0:NG, 0:WC], cT[:, k, :], w[:, k, :], start=(k == 0), stop=(k == KC - 1))
                mm.then_inc(s_full[n % 4], 1)
            pe.wait_ge(s_small, 16 * 20)
            pe.wait_ge(s_wss, 16 * (P // DSEQ))
            for half in range(2):
                turn_four(2 + half, [ws_nat[:, 4 * half + j, :] for j in range(4)])
            for half in range(2):
                turn_four(4 + half, [wss_nat[:, 4 * half + j, :] for j in range(4)])
            for a in range(2):
                turn_four(6 + a, [sk_nat[:, a, :]])

            heads = 0
            for g, tiles in enumerate(GROUPS):
                T, N = len(tiles), distinct(g)
                before = sum(len(GROUPS[j]) for j in range(g))
                for i in range(T):
                    pe.wait_ge(s_n1h, before + i + 1)
                    for half in range(2):
                        x = vv[:, slot_of(g, i), :]
                        turn_four(turn_base(g, "norm1") + 2 * i + half,
                                  [x[:, (4 * half + j) * P:(4 * half + j + 1) * P] for j in range(4)])
                turned(pe, turn_base(g, "kT"))
                h = hT(g)
                for c in range(4):
                    channel_major(chunk_base(g, "q") + c, fill_base(g, "q") + 2 * c, h, N)
                for c in range(4):
                    n = chunk_base(g, "k") + c
                    for i in range(T):
                        token_major(n, fill_base(g, "k") + c * T + i, h[:, :, i * P:(i + 1) * P])
                    if c:
                        evacuated(pe, fill_base(g, "k") + c * T)
                        for i in range(T):
                            turn_four(turn_base(g, "kT") + (c - 1) * T + i,
                                      [gvt(i)[:, (2 * (c - 1) + j) * P:(2 * (c - 1) + j + 1) * P] for j in range(2)])
                for c in range(4):
                    n = chunk_base(g, "v") + c
                    for i in range(T):
                        token_major(n, fill_base(g, "v") + c * T + i, h[:, :, i * P:(i + 1) * P])
                    if c == 0:
                        evacuated(pe, fill_base(g, "k") + 4 * T)
                        for i in range(T):
                            turn_four(turn_base(g, "kT") + 3 * T + i,
                                      [gvt(i)[:, (6 + j) * P:(7 + j) * P] for j in range(2)])
                turned(pe, turn_base(g, "gate"))
                evacuated(pe, fill_base(g, "u"))
                pe.wait_ge(s_bias, 1)
                q = qT(g)

                def mix(i, t):
                    pe.wait_ge(s_lnh, before + i + 1)
                    by = WsTs if t == SAMPLE else WsT
                    for half in range(2):
                        f = turn_base(g, "gate") + 2 * i + half
                        out = take_turn(f)
                        for j in range(4):
                            gr = 4 * half + j
                            mm = nc.tensor.matmul(out[:, j * P:(j + 1) * P], gvt(i)[:, gr * P:(gr + 1) * P], by[:, gr, :],
                                                  start=True, stop=True)
                        mm.then_inc(s_tfull[f % 2], 1)

                def scores(n, i, t, hd):
                    if n >= 2:
                        pe.wait_ge(s_ar, n - 1)
                    z = bank[6 + n % 2]
                    for kb in range(t + 1):
                        nc.tensor.matmul(z[:, kb * P:(kb + 1) * P], kT[:, kb, hd, :], q[:, hd, i * P:(i + 1) * P],
                                         start=True, stop=(kb < t))
                    nc.tensor.matmul(z[:, t * P:(t + 1) * P], ident[:], hidden[:], start=False, stop=True).then_inc(s_az, 1)

                def exponents(n, t):
                    pe.wait_ge(s_al, n + 1)
                    if n >= 2:
                        pe.wait_ge(s_aw, n - 1)
                    for kb in range(t + 1):
                        out = bank[4 + n % 2][:, kb * P:(kb + 1) * P]
                        cols = slice(kb * P, (kb + 1) * P)
                        nc.tensor.matmul(out, since[:], att("log", n)[:, cols], start=True, stop=False)
                        nc.tensor.matmul(out, later[:], att("pos", n)[:, cols], start=False, stop=False)
                        mm = nc.tensor.matmul(out, ident[:], att("neg", n)[:, cols], start=False, stop=(kb == t))
                        for k2 in range(kb + 1, t + 1):
                            cols = slice(k2 * P, (k2 + 1) * P)
                            nc.tensor.matmul(out, ones[:], att("log", n)[:, cols], start=False, stop=False)
                            mm = nc.tensor.matmul(out, ones[:], att("pos", n)[:, cols], start=False, stop=(k2 == t))
                    mm.then_inc(s_ac, 1)

                def outputs(n, t, hd):
                    pe.wait_ge(s_aw, n + 1)
                    if n >= 2:
                        pe.wait_ge(s_ae, n - 1)
                    for kb in range(t + 1):
                        mm = nc.tensor.matmul(bank[2 + n % 2][:, 0:P], vv[:, kb, hd * P:(hd + 1) * P],
                                              att("log", n)[:, kb * P:(kb + 1) * P], start=(kb == 0), stop=(kb == t))
                    mm.then_inc(s_ao, 1)

                pairs = head_pairs(g)
                for n, i, t, hd in pairs[0]:
                    scores(n, i, t, hd)
                for w in range(len(pairs) + 1):
                    for n, i, t, hd in pairs[w + 1] if w + 1 < len(pairs) else []:
                        scores(n, i, t, hd)
                    for n, i, t, hd in pairs[w] if w < len(pairs) else []:
                        exponents(n, t)
                    for n, i, t, hd in pairs[w - 1] if w else []:
                        outputs(n, t, hd)
                heads += 2 * len(pairs)
                pe.wait_ge(s_ae, heads)

                if g == 0:
                    for page in range(2):
                        nc.tensor.matmul(bank[6 + page][:, :], ones[0:1, :], bias_row, start=True, stop=False)

                    def turn_page(m):
                        pe.wait_ge(s_page[m % 4], 16 * (m // 4 + 1))
                        for half in range(2):
                            if m:
                                pe.wait_ge(s_kte, 2 * (m - 1) + half + 1)
                            for j in range(4):
                                mm = nc.tensor.transpose(bank[4 + half][:, j * P:(j + 1) * P],
                                                         ring[:, m % 4, (4 * half + j) * P:(4 * half + j + 1) * P], ident[:])
                            mm.then_inc(s_ktf[half], 1)

                    turn_page(0)
                    for m in range(2 * NDEC):
                        if m < NH:
                            channel_block(chunk_base(g, "u") + m // 2, fill_base(g, "u") + m, m % 2, h, N)
                        else:
                            c, i = divmod(m - NH, T)
                            token_major(chunk_base(g, "gv") + c, fill_base(g, "gv") + m - NH, h[:, :, i * P:(i + 1) * P])
                        b, page = m // 2, m % 2
                        pe.wait_ge(s_kte, 2 * m + 2)
                        for hd in range(NH):
                            at = hd * NS + b * DSEQ
                            mm = nc.tensor.matmul(bank[6 + page][:, at:at + DSEQ],
                                                  ring[:, 4 + m % 2, hd * P:(hd + 1) * P],
                                                  q[:, hd, P + b * DSEQ:P + (b + 1) * DSEQ], start=False,
                                                  stop=(b == NDEC - 1 and hd == NH - 1))
                        mm.then_inc(s_sz, 1)
                        if m + 1 < 2 * NDEC:
                            turn_page(m + 1)
                    evacuated(pe, fill_base(g, "merge"))
                    nc.tensor.matmul(bank[0][0:NS, :], ones[0:1, 0:NS], bias_row, start=True, stop=False)
                    for hd in range(NH):
                        nc.tensor.matmul(bank[0][0:NS, hd * NS:(hd + 1) * NS], kT[:, 1, hd, 0:NS],
                                         q[:, hd, P:P + NS], start=False, stop=False)
                    nc.tensor.matmul(bank[0][0:NS, :].rearrange("p (h n) -> p h n", h=NH), ident[0:NS, 0:NS],
                                     hidden_s.unsqueeze(1).broadcast_to([NS, NH, NS]), start=False, stop=True).then_inc(s_sn, 1)
                    pe.wait_ge(s_sl, 1)
                    for part in (2, 1, 0):
                        rows = NS if part == 2 else P
                        out = bank[1 + part][0:rows, :]
                        nc.tensor.matmul(out, since[0:rows, 0:rows], log_s[part], start=True, stop=False)
                        nc.tensor.matmul(out, later[0:rows, 0:rows], pos_s[part], start=False, stop=False)
                        mm = nc.tensor.matmul(out, ident[0:rows, 0:rows], neg_s[part], start=False, stop=(part == 2))
                        for behind in range(part + 1, 3):
                            r = NS if behind == 2 else P
                            nc.tensor.matmul(out, ones[0:r, :], log_s[behind], start=False, stop=False)
                            mm = nc.tensor.matmul(out, ones[0:r, :], pos_s[behind], start=False, stop=(behind == 2))
                    mm.then_inc(s_scm, 1)
                    n, f = chunk_base(g, "merge"), fill_base(g, "merge")
                    pe.wait_ge(s_sw, 1)
                    for b in range(NDEC):
                        m0 = 2 * NDEC + 2 * b
                        for page in range(2):
                            m = m0 + page
                            pe.wait_ge(s_page[m % 4], 16 * (m // 4 + 1))
                        for hd in range(NH):
                            at = slice(hd * NS + b * DSEQ, hd * NS + (b + 1) * DSEQ)
                            nc.tensor.matmul(bank[6][:, at], vv[0:NS, 1, hd * P:(hd + 1) * P], log_s[2][:, at],
                                             start=True, stop=False)
                            for page in range(2):
                                mm = nc.tensor.matmul(bank[6][:, at], ring[:, (m0 + page) % 4, hd * P:(hd + 1) * P],
                                                      log_s[page][:, at], start=False, stop=(page == 1))
                        mm.then_inc(s_sv, 1)
                        if b < 2:
                            channel_block(n, f + b, b, h, N)
                        elif b < 4:
                            mix(b - 2, tiles[b - 2])
                        elif b < 6:
                            if b == 4:
                                turned(pe, turn_base(g, "norm2"))
                            channel_block(n + 1, f + b - 2, b - 4, uT(g), N)
                        else:
                            channel_block(n + 2, f + b - 2, b - 6, h, N)
                    pe.wait_ge(s_se, 1)
                    channel_major(n + 3, f + 6, q, N)

                else:
                    for c in range(4):
                        channel_major(chunk_base(g, "u") + c, fill_base(g, "u") + 2 * c, h, N)
                    for c in range(4):
                        n = chunk_base(g, "gv") + c
                        for i in range(T):
                            token_major(n, fill_base(g, "gv") + c * T + i, h[:, :, i * P:(i + 1) * P])
                    for i, t in enumerate(tiles):
                        mix(i, t)
                    turned(pe, turn_base(g, "norm2"))
                u = uT(g)
                for j in range(4):
                    if g == 0 and j == 0:
                        continue
                    n, f = chunk_base(g, "merge") + 4 * j, fill_base(g, "merge") + 8 * j
                    channel_major(n, f, h, N)
                    channel_major(n + 1, f + 2, u, N)
                    channel_major(n + 2, f + 4, h, N)
                    channel_major(n + 3, f + 6, q, N)
                evacuated(pe, fill_base(g, "out"))
                if g == 0:
                    pe.wait_ge(s_twice, 1)
                m = mT(g)
                for c in range(4):
                    n = chunk_base(g, "out") + c
                    for i in range(T):
                        token_major(n, fill_base(g, "out") + c * T + i, m[:, :, i * P:(i + 1) * P])
                for i in range(T):
                    pe.wait_ge(s_n2h, before + i + 1)
                    for half in range(2):
                        turn_four(turn_base(g, "norm2") + 2 * i + half,
                                  [h2(g, i)[:, (4 * half + j) * P:(4 * half + j + 1) * P] for j in range(4)])
                turned(pe, turn_base(g, "norm2") + 2 * T)
                def key_scores(c):
                    evacuated(pe, fill_base(g, "query") + 2 * c + 2)
                    for i in range(T):
                        if c or g:
                            done = c + (8 * g if i < 2 else 0)
                            if done:
                                pe.wait_ge(s_sev[i], done)
                        for a in range(2):
                            mm = nc.tensor.matmul(bank[5 + i][:, a * NKEY:(a + 1) * NKEY], qh[:, c % 2, a, i * P:(i + 1) * P],
                                                  skT[:, a, :], start=True, stop=True)
                        mm.then_inc(s_sfull[i], 1)
                for c in range(NH):
                    channel_major(chunk_base(g, "query") + c, fill_base(g, "query") + 2 * c, h, N)
                    if c:
                        key_scores(c - 1)
                key_scores(NH - 1)
                for i in range(T):
                    pe.wait_ge(s_sev[i], NH * (g + 1) if i < 2 else NH)

            def sum_step(n, batch, opens, closes):
                for k in range(TOPK):
                    pe.wait_ge(s_diag, (n - FIRST[LATER[0]]) * TOPK + k + 1)
                    pe.wait_ge(s_gath[k % SLOTS], batch * 32 + 16 * (k // SLOTS + 1))
                    for half in range(2):
                        mm = nc.tensor.matmul(bank[6 + half][:, :], diag[:, k % SLOTS, :],
                                              ring[:, k % SLOTS, half * 512:(half + 1) * 512],
                                              start=(opens and k == 0), stop=(closes and k == TOPK - 1))
                    mm.then_inc(s_summed, 1)

            for order, t in enumerate(LATER):
                H, first = STEPS[t], FIRST[t]
                if order:
                    pe.wait_ge(s_ended, order)
                sum_step(first, 2 * (first + 1), True, False)
                with pe.Fori(2, H) as h:
                    sum_step(h + (first - 1), (h + first) * 2, False, False)
                sum_step(first + H - 1, 2 * (first + H) - (1 if t == LATER[-1] else 0), False, True)

        @block.scalar
        def _(act):
            def read(f):
                act.wait_ge(s_full[f % 4], f // 4 + 1)
                return bank[f % 4]

            def read_turn(t):
                act.wait_ge(s_tfull[t % 2], t // 2 + 1)
                return bank[4 + t % 2]

            def root(wait, n, signal, col):
                act.wait_ge(wait, n)
                nc.scalar.activation(st[:, col + 1:col + 2], st[:, col:col + 1], ACT.Sqrt).then_inc(signal, 1)

            act.wait_ge(s_cond, 16 * 5)
            nc.scalar.activation(c9, c9, ACT.Silu).then_inc(s_silu, 1)
            for t in range(2):
                out = read_turn(t)
                nc.scalar.copy(cT[:, 4 * t:4 * t + 4, :].rearrange("p k r -> p (k r)"), out[:, 0:4 * NG]).then_inc(s_tfree[t], 1)
            for a in range(2):
                f = 6 + a
                nc.scalar.copy(skT[:, a, :], read_turn(f)[:, 0:NKEY]).then_inc(s_tfree[f % 2], 1)

            def exponentials(g, ready):
                act.wait_ge(s_nb, ready)
                for i in range(len(GROUPS[g])):
                    nc.scalar.activation(expo[:, i, :], best_v[:, i, :], ACT.Exp, bias=nmax[:, i:i + 1],
                                         accum_out=esum[:, 0, i:i + 1]).then_inc(s_ex, 1)

            def front(g):
                tiles = GROUPS[g]
                T, N = len(tiles), distinct(g)
                before = sum(len(GROUPS[j]) for j in range(g))

                def transposed(phase, i):
                    for half in range(2):
                        f = turn_base(g, phase) + 2 * i + half
                        src = read_turn(f)[:, :].rearrange("p (j n) -> p j n", j=4)
                        nc.scalar.copy(hT(g)[:, 4 * half:4 * half + 4, i * P:(i + 1) * P], src).then_inc(s_tfree[f % 2], 1)

                for i in range(T):
                    root(s_n1v, before + i + 1, s_n1s, 0)
                yield
                for i in range(T):
                    transposed("norm1", i)
                yield
                for j in range(NH):
                    f = fill_base(g, "q") + j
                    nc.scalar.copy(qT(g)[:, j, 0:N], read(f)[:, 0:N]).then_inc(s_free[f % 4], 1)
                    if j % 4 == 3:
                        yield

                def keys_turned(c):
                    for i in range(T):
                        f = turn_base(g, "kT") + c * T + i
                        nc.scalar.copy(kT[:, slot_of(g, i), 2 * c:2 * c + 2, :].rearrange("p h n -> p (h n)"),
                                       read_turn(f)[:, 0:2 * P]).then_inc(s_tfree[f % 2], 1)
                for c in range(4):
                    for i in range(T):
                        f = fill_base(g, "k") + c * T + i
                        nc.scalar.copy(gvt(i)[:, c * WC:(c + 1) * WC], read(f)[:, 0:WC]).then_inc(s_free[f % 4], 1)
                    if c:
                        keys_turned(c - 1)
                    yield
                for c in range(4):
                    for i in range(T):
                        f = fill_base(g, "v") + c * T + i
                        nc.scalar.copy(vv[:, slot_of(g, i), c * WC:(c + 1) * WC], read(f)[:, 0:WC]).then_inc(s_free[f % 4], 1)
                    if c == 0:
                        keys_turned(3)
                    yield

                def gelu_u(j):
                    f = fill_base(g, "u") + j
                    nc.scalar.activation(uT(g)[:, j, 0:N], read(f)[:, 0:N], ACT.Gelu).then_inc(s_free[f % 4], 1)

                def gelu_gv(c, i):
                    f = fill_base(g, "gv") + c * T + i
                    nc.scalar.activation(gvt(i)[:, c * WC:(c + 1) * WC], read(f)[:, 0:WC], ACT.Gelu).then_inc(s_free[f % 4], 1)

                def gate_sigmoids(j, which):
                    f = fill_base(g, "merge") + 8 * j + 4 * which
                    for b in range(2):
                        if j:
                            used = f - 8 + 2 + b
                            act.wait_ge(s_free[used % 4], used // 4 + 1)
                        nc.scalar.activation(sg[:, 2 * which + b, 0:N], read(f + b)[:, 0:N],
                                             ACT.Sigmoid).then_inc(s_free[(f + b) % 4], 1)

                def log_parts(pair):
                    for n, i, t, hd in pair:
                        cols = (t + 1) * P
                        act.wait_ge(s_az, n + 1)
                        if n >= 4:
                            act.wait_ge(s_ao, n - 3)
                        z = bank[6 + n % 2][:, 0:cols]
                        nc.scalar.activation(att("log", n)[:, 0:cols], z, ACT.Abs, scale=SCALE, bias=bias_b[:, hd:hd + 1])
                        nc.scalar.activation(att("pos", n)[:, 0:cols], z, ACT.Relu, scale=SCALE, bias=bias_b[:, hd:hd + 1])
                        nc.scalar.activation(att("neg", n)[:, 0:cols], z, ACT.Relu, scale=-SCALE,
                                             bias=nbias_b[:, hd:hd + 1]).then_inc(s_ar, 1)
                    act.wait_ge(s_ar, pair[-1][0] + 1)
                    for n, i, t, hd in pair:
                        log = att("log", n)[:, 0:(t + 1) * P]
                        nc.scalar.activation(log, log, ACT.Exp, scale=-1.0)
                    act.drain()
                    for n, i, t, hd in pair:
                        log = att("log", n)[:, 0:(t + 1) * P]
                        nc.scalar.activation(log, log, ACT.Ln, bias=1.0).then_inc(s_al, 1)

                if g:
                    for b in range(2):
                        act.wait_ge(s_scst[b], 16 * (NH // 2))
                act.wait_ge(s_bias, 1)
                act.wait_ge(s_kst, 16 * (before + T))
                pairs = head_pairs(g)
                log_parts(pairs[0])
                for w in range(len(pairs) + 1):
                    if w + 1 < len(pairs):
                        log_parts(pairs[w + 1])
                    for n, i, t, hd in pairs[w] if w < len(pairs) else []:
                        act.wait_ge(s_ac, n + 1)
                        nc.scalar.activation(att("log", n)[:, 0:(t + 1) * P], bank[4 + n % 2][:, 0:(t + 1) * P], ACT.Exp,
                                             scale=-1.0).then_inc(s_aw, 1)
                    for n, i, t, hd in pairs[w - 1] if w else []:
                        act.wait_ge(s_ao, n + 1)
                        nc.scalar.copy(qT(g)[:, hd, i * P:(i + 1) * P], bank[2 + n % 2][:, 0:P]).then_inc(s_ae, 1)
                    yield
                if g == 0:
                    for m in range(2 * NDEC):
                        if m >= 2:
                            act.wait_ge(s_sz, m - 1)
                        for half in range(2):
                            act.wait_ge(s_ktf[half], m + 1)
                            nc.scalar.copy(ring[:, 4 + m % 2, half * 512:(half + 1) * 512],
                                           bank[4 + half][:, :]).then_inc(s_kte, 1)
                        if m < NH:
                            gelu_u(m)
                        else:
                            gelu_gv(*divmod(m - NH, T))
                    act.wait_ge(s_sn, 1)
                    for part, src in enumerate((bank[6][:, :], bank[7][:, :], bank[0][0:NS, :])):
                        nc.scalar.activation(log_s[part], src, ACT.Abs, scale=SCALE)
                        nc.scalar.activation(pos_s[part], src, ACT.Relu, scale=SCALE)
                        nc.scalar.activation(neg_s[part], src, ACT.Relu, scale=-SCALE)
                    act.drain()
                    for part in range(3):
                        nc.scalar.activation(log_s[part], log_s[part], ACT.Exp, scale=-1.0)
                    act.drain()
                    for part in range(3):
                        ins = nc.scalar.activation(log_s[part], log_s[part], ACT.Ln, bias=1.0)
                    ins.then_inc(s_sl, 1)
                    act.wait_ge(s_scm, 1)
                    for part in range(3):
                        rows = NS if part == 2 else P
                        ins = nc.scalar.activation(log_s[part], bank[1 + part][0:rows, :], ACT.Exp, scale=-1.0)
                    ins.then_inc(s_sw, 1)
                    for i in range(T):
                        root(s_lnv, before + i + 1, s_lns, 4)
                    for which in range(2):
                        gate_sigmoids(0, which)
                    act.wait_ge(s_sv, NDEC)
                    src = bank[6][:, :].rearrange("p (h n) -> p h n", h=NH)
                    nc.scalar.copy(qT(g)[:, :, P:P + NS], src).then_inc(s_se, 1)
                else:
                    for j in range(NH):
                        gelu_u(j)
                        if j % 4 == 3:
                            yield
                    for c in range(4):
                        for i in range(T):
                            gelu_gv(c, i)
                        yield
                    for i in range(T):
                        root(s_lnv, before + i + 1, s_lns, 4)
                    yield
                for j in range(4):
                    for which in range(2):
                        if g or j:
                            gate_sigmoids(j, which)
                        yield
                for i in range(T):
                    root(s_n2v, before + i + 1, s_n2s, 8)
                yield
                for i in range(T):
                    transposed("norm2", i)
                yield

                def scores_out(c):
                    if c >= 2:
                        act.wait_ge(s_scst[c % 2], 16 * (NH // 2 * g + c // 2))
                    for i in range(T):
                        done = c + (NH * g if i < 2 else 0)
                        act.wait_ge(s_sfull[i], done + 1)
                        nc.scalar.copy(sc_out[:, c % 2, i * 2 * NKEY:(i + 1) * 2 * NKEY],
                                       bank[5 + i][:, 0:2 * NKEY]).then_inc(s_sev[i], 1)
                    for i in range(T):
                        act.wait_ge(s_sev[i], c + (NH * g if i < 2 else 0) + 1)
                    act.dma_start(score_dram[g][c * P:(c + 1) * P, :],
                                  sc_out[:, c % 2, 0:T * 2 * NKEY]).then_inc(s_scst[c % 2], 16)
                for c in range(NH):
                    for a in range(2):
                        f = fill_base(g, "query") + 2 * c + a
                        if c >= 2:
                            for i in range(T):
                                act.wait_ge(s_sfull[i], c - 1 + (NH * g if i < 2 else 0))
                        src = read(f)
                        if g == 0:
                            nc.scalar.copy(qh[:, c % 2, a, N:N + NS], src[:, N - NS:N])
                        nc.scalar.copy(qh[:, c % 2, a, 0:N], src[:, 0:N]).then_inc(s_free[f % 4], 1)
                    if c:
                        scores_out(c - 1)
                    yield c
                scores_out(NH - 1)

            def two_heads_queried(pieces):
                while next(pieces) != 1:
                    pass

            ours, theirs = front(0), front(1)
            two_heads_queried(ours)
            next(theirs)
            other = chain(ours, theirs)
            def gelu(t, h, b=0):
                act.wait_ge(s_dots, h + (FIRST[t] + 1))
                nc.scalar.activation(acts[:, b], dots[:, b], ACT.Gelu).then_inc(s_acts, 1)

            def diagonals(t, h):
                first = FIRST[t]
                act.wait_ge(s_summed, (h + first) * TOPK)
                act.wait_ge(s_coef, h + (first - FIRST[LATER[0]] + 1))
                for k in range(TOPK):
                    if k >= SLOTS:
                        act.wait_ge(s_summed, (h + first) * TOPK + (k - SLOTS + 1))
                    nc.scalar.activation(diag[:, k % SLOTS, :], ident[:], ACT.Copy,
                                         scale=coef[:, k:k + 1]).then_inc(s_diag, 1)

            def store_y(t):
                order = ORDER.index(t)
                root(s_fv, order + 1, s_fs, 12)
                act.wait_ge(s_fy, order + 1)
                dst = ys if t == SAMPLE else yp[t]
                act.dma_start(dst, acc[0:dst.shape[0], 0, :]).then_inc(s_y, 16)

            for t in WOVEN:
                H, g = STEPS[t], CHOOSING.get(t)
                if g is not None:
                    exponentials(g, NH * g + 1)
                for h in range(H):
                    for _ in range(ACT_PIECES[t][h]):
                        next(other, None)
                    if g is not None and h == 0:
                        exponentials(g, NH * g + 2)
                    gelu(t, h, h % 2)
                    if g is not None and 0 < h < H - 1:
                        exponentials(g, NH * g + h + 2)
                for _ in range(ACT_PIECES[t][H]):
                    next(other, None)
                store_y(t)
            two_heads_queried(other)

            for order, t in enumerate(LATER):
                H, g = STEPS[t], CHOOSING.get(t)
                if g is not None:
                    exponentials(g, NH * g + 1)
                    for _ in other:
                        pass
                if order:
                    last = LATER[order - 1]
                    diagonals(last, STEPS[last] - 1)
                if g is not None:
                    exponentials(g, NH * g + 2)
                gelu(t, 0)
                if order:
                    store_y(last)
                with act.Fori(1, H - 1) as h:
                    diagonals(t, h - 1)
                    gelu(t, h)
                    if g is not None:
                        exponentials(g, h + (NH * g + 2))
                diagonals(t, H - 2)
                gelu(t, H - 1)
            diagonals(t, H - 1)
            store_y(t)

        @block.vector
        def _(dve):

            def read(f):
                dve.wait_ge(s_full[f % 4], f // 4 + 1)
                return bank[f % 4]

            def read_turn(t):
                dve.wait_ge(s_tfull[t % 2], t // 2 + 1)
                return bank[4 + t % 2]

            def table(g, what, kind):
                n = table_number(g, what, kind)
                dve.wait_ge(s_tab[n % 3], 32 * (n // 3 + 1))
                return tab[:, n % 3, :]

            def mean_square(src, col, signal):
                nc.vector.tensor_tensor_reduce(out=junk[:], in0=src, in1=src, scale=1.0, scalar=0.0,
                                               op0=ALU.mult, op1=ALU.add, accum_out=st[:, col:col + 1])
                dve.drain()
                nc.vector.tensor_scalar(st[:, col:col + 1], st[:, col:col + 1], 1.0 / D, EPS, ALU.mult, ALU.add).then_inc(signal, 1)

            def reciprocal_root(wait, n, col):
                dve.wait_ge(wait, n)
                nc.vector.reciprocal(st[:, col + 2:col + 3], st[:, col + 1:col + 2])
                dve.drain()
                return st[:, col + 2:col + 3]

            dve.wait_ge(s_const, NCONST)
            nc.vector.memset(acc[0:1, 1, 0:1], 0.0).then_inc(s_zero, 1)
            dve.wait_ge(s_cond, 16 * 5)
            for n in range(NADA):
                m = mod9[:, n * WC:(n + 1) * WC]
                nc.vector.tensor_tensor(m, read(n)[0:NG, 0:WC], m, ALU.add).then_inc(s_free[n % 4], 1)
            dve.drain()
            for m, gain in ((1, g1row), (4, g2row)):
                row = mod9[:, m * D:(m + 1) * D]
                nc.vector.scalar_tensor_tensor(out=row, in0=row, scalar=1.0, in1=gain, op0=ALU.add,
                                               op1=ALU.mult).then_inc(s_mod, 1)
            for f, dst in ((2, WsT[:]), (4, WsTs)):
                for half in range(2):
                    src = read_turn(f + half)[:, :].rearrange("p (j n) -> p j n", j=4)
                    nc.vector.tensor_tensor(dst[:, 4 * half:4 * half + 4, :], src,
                                            causal.unsqueeze(1).broadcast_to([P, 4, P]), ALU.mult).then_inc(s_tfree[half], 1)

            dve.wait_ge(s_small, 16 * 20)
            nc.vector.tensor_scalar(nbias_b[:], bias_b[:], -1.0, None, ALU.mult)
            nc.vector.tensor_scalar(bias_row.rearrange("p (h n) -> p h n", h=NH),
                                    bias_b[0:1, :].unsqueeze(2).broadcast_to([1, NH, NS]),
                                    1.0 / SCALE, None, ALU.mult).then_inc(s_bias, 1)

            def front(g):
                tiles = GROUPS[g]
                T, N = len(tiles), distinct(g)
                before = sum(len(GROUPS[j]) for j in range(g))

                dve.wait_ge(s_x[g], 32 * T)
                for i, t in enumerate(tiles):
                    kind = "s" if t == SAMPLE else "p"
                    x = vv[:, slot_of(g, i), :]
                    dve.drain()
                    mean_square(x, 0, s_n1v)
                    r = reciprocal_root(s_n1s, before + i + 1, 0)
                    nc.vector.scalar_tensor_tensor(out=x, in0=x, scalar=r, in1=table(g, "A1", kind), op0=ALU.mult, op1=ALU.mult)
                    dve.drain()
                    nc.vector.tensor_tensor(x, x, table(g, "B1", kind), ALU.add).then_inc(s_n1h, 1)
                    if g == 0 or i == T - 1:
                        nc.vector.drain().then_inc(s_tabfree, 2)
                    yield

                for i, t in enumerate(tiles):
                    evacuated(dve, fill_base(g, "gv") + 4 * T)
                    x = gvt(i)
                    dve.drain()
                    nc.vector.tensor_reduce(st[:, 7:8], x, AX.X, ALU.add)
                    dve.drain()
                    nc.vector.tensor_scalar(st[:, 7:8], st[:, 7:8], -1.0 / D, None, ALU.mult)
                    dve.drain()
                    nc.vector.tensor_scalar(x, x, st[:, 7:8], None, ALU.add)
                    dve.drain()
                    mean_square(x, 4, s_lnv)
                    r = reciprocal_root(s_lns, before + i + 1, 4)
                    nc.vector.scalar_tensor_tensor(out=x, in0=x, scalar=r, in1=table(g, "gv", ""), op0=ALU.mult, op1=ALU.mult)
                    dve.drain()
                    nc.vector.tensor_tensor(x, x, table(g, "bv", ""), ALU.add).then_inc(s_lnh, 1)
                nc.vector.drain().then_inc(s_tabfree, 2)
                for i, t in enumerate(tiles):
                    bs = bsbs if t == SAMPLE else bsb[:]
                    n = NS if t == SAMPLE else P
                    for half in range(2):
                        f = turn_base(g, "gate") + 2 * i + half
                        src = read_turn(f)[:, :].rearrange("p (j n) -> p j n", j=4)[:, :, 0:n]
                        mixed = junk[:, half * 512:(half + 1) * 512].rearrange("p (j n) -> p j n", j=4)[:, :, 0:n]
                        uu = uT(g)[:, 4 * half:4 * half + 4, i * P:i * P + n]
                        dve.drain()
                        nc.vector.tensor_tensor(mixed, src, bs[:, 4 * half:4 * half + 4, 0:n], ALU.add)
                        dve.drain()
                        nc.vector.tensor_tensor(uu, uu, mixed, ALU.mult).then_inc(s_tfree[f % 2], 1)
                yield

                if g == 0:
                    dve.wait_ge(s_gvst, 16)
                m = mT(g)
                for j in range(4):
                    for which in range(2):
                        f = fill_base(g, "merge") + 8 * j + 4 * which + 2
                        for b in range(2):
                            dve.wait_ge(s_free[(f - 2 + b) % 4], (f - 2 + b) // 4 + 1)
                            s = sg[:, 2 * which + b, 0:N]
                            src = read(f + b)[:, 0:N]
                            if which == 0:
                                ins = nc.vector.tensor_tensor(m[:, 2 * j + b, 0:N], src, s, ALU.mult)
                            else:
                                nc.vector.tensor_tensor(s, src, s, ALU.mult)
                                dve.drain()
                                ins = nc.vector.tensor_tensor(m[:, 2 * j + b, 0:N], m[:, 2 * j + b, 0:N], s, ALU.add)
                            ins.then_inc(s_free[(f + b) % 4], 1)
                        yield

                if g == 0:
                    dve.drain()
                    nc.vector.tensor_copy(m[:, :, N:N + NS], m[:, :, N - NS:N]).then_inc(s_twice, 1)

                dve.wait_ge(s_xr[g], 32 * T)
                for c in range(4):
                    for i, t in enumerate(tiles):
                        f = fill_base(g, "out") + c * T + i
                        cols = slice(c * WC, (c + 1) * WC)
                        part = junk[:, (f % 2) * 512:(f % 2) * 512 + WC]
                        gate = table(g, "G1", "s" if t == SAMPLE else "p")
                        nc.vector.tensor_tensor(part, read(f)[:, 0:WC], gate[:, cols], ALU.mult)
                        dve.drain()
                        x = vv[:, xslot_of(g, i), cols]
                        ins = nc.vector.tensor_tensor(x, x, part, ALU.add)
                        ins.then_inc(s_free[f % 4], 1)
                    if c % 2:
                        yield
                nc.vector.drain().then_inc(s_tabfree, 2 if g == 0 else 1)

                for i, t in enumerate(tiles):
                    kind = "s" if t == SAMPLE else "p"
                    x, out = vv[:, xslot_of(g, i), :], h2(g, i)
                    dve.drain()
                    mean_square(x, 8, s_n2v)
                    r = reciprocal_root(s_n2s, before + i + 1, 8)
                    nc.vector.scalar_tensor_tensor(out=out, in0=x, scalar=r, in1=table(g, "A2", kind), op0=ALU.mult, op1=ALU.mult)
                    dve.drain()
                    nc.vector.tensor_tensor(out, out, table(g, "B2", kind), ALU.add).then_inc(s_n2h, 1)
                    if g == 0 or i == T - 1:
                        nc.vector.drain().then_inc(s_tabfree, 2)
                yield

            loaded = dve.alloc_register("score_loads")
            raised = dve.alloc_register("exponentials_made")
            dve.reg_mov(loaded, 0)
            dve.reg_mov(raised, 0)

            def top16(sets, last=None):
                for src, _, values, _ in sets:
                    nc.vector.max(values[:, 0:8], src)
                dve.drain()
                for src, work_, values, places in sets:
                    nc.vector.max_index(places[:, 0:8], values[:, 0:8], src)
                    ins = nc.vector.match_replace(work_, values[:, 0:8], src, LOWEST)
                if last is not None:
                    ins.then_inc(last, 1)
                dve.drain()
                for _, work_, values, _ in sets:
                    nc.vector.max(values[:, 8:16], work_)
                dve.drain()
                for _, work_, values, places in sets:
                    nc.vector.max_index(places[:, 8:16], values[:, 8:16], work_)
                dve.drain()

            def choose(g, h):
                tiles = GROUPS[g]
                T = len(tiles)
                dve.reg_add(loaded, loaded, 16)
                dve.wait_ge(s_const, NCONST)
                dve.wait_ge(s_scld, loaded)
                top16([(sc[:, i, a, :], work[:, i, a * NKEY:(a + 1) * NKEY], top_v[:, i, a, :], top_i[:, i, a, :])
                       for i in range(T) for a in range(2)], s_tk)
                pairs = cand[:, 0:T].rearrange("p i (a b) -> p i a b", a=TOPK)
                nc.vector.tensor_copy(top_k[:, 0:T], top_i[:, 0:T])
                for i in range(T):
                    nc.vector.tensor_tensor(pairs[:, i], top_v[:, i, 0, :].unsqueeze(2).broadcast_to([P, TOPK, TOPK]),
                                            top_v[:, i, 1, :].unsqueeze(1).broadcast_to([P, TOPK, TOPK]), ALU.add)
                dve.drain()
                top16([(cand[:, i, :], work[:, i, :], best_v[:, i, :], best_i[:, i, :]) for i in range(T)])
                nc.vector.tensor_scalar(nmax[:, 0:T], best_v[:, 0:T, 0], -1.0, None, ALU.mult).then_inc(s_nb, 1)
                nc.vector.tensor_scalar(halves_i[:, 0, 0:T], best_i[:, 0:T], 4, None, ALU.logical_shift_right)
                nc.vector.tensor_scalar(halves_i[:, 1, 0:T], best_i[:, 0:T], TOPK - 1, None, ALU.bitwise_and)
                dve.drain()
                nc.vector.tensor_copy(halves[:, :, 0:T], halves_i[:, :, 0:T])
                dve.drain()
                hots = [buf[:, 0:T].rearrange("p i (j r) -> p i j r", r=TOPK) for buf in (work, cand)]
                for a in range(2):
                    nc.vector.tensor_tensor(hots[a].rearrange("p i j r -> p (i j) r"),
                                            halves[:, a, 0:T].rearrange("p i j -> p (i j)").unsqueeze(2).broadcast_to([P, T * TOPK, TOPK]),
                                            iota_f[:].unsqueeze(1).broadcast_to([P, T * TOPK, TOPK]), ALU.is_equal)
                dve.drain()
                for a in range(2):
                    nc.vector.tensor_tensor(hots[a], hots[a], top_k[:, 0:T, a, :].unsqueeze(2).broadcast_to([P, T, TOPK, TOPK]),
                                            ALU.mult)
                dve.drain()
                for a in range(2):
                    nc.vector.tensor_reduce(pick[:, a, 0:T].rearrange("p i j -> p (i j)"),
                                            hots[a].rearrange("p i j r -> p (i j) r"), AX.X, ALU.add)
                dve.drain()
                nc.vector.scalar_tensor_tensor(out=pick[:, 0, 0:T], in0=pick[:, 0, 0:T], scalar=float(NKEY),
                                               in1=pick[:, 1, 0:T], op0=ALU.mult, op1=ALU.add)
                dve.drain()
                for i, t in enumerate(tiles):
                    write_choice(expert, pick[:, 0, i, :], t, h)
                dve.drain()

            def write_choice(dst, src, t, h):
                if t == SAMPLE:
                    for half in range(2):
                        rows = slice(half * NS, (half + 1) * NS)
                        nc.vector.tensor_copy(dst[rows, t, bass.ds(h * (TOPK // 2), TOPK // 2)],
                                              src[rows, :].rearrange("p (k two) -> p k two", two=2)[:, :, half])
                else:
                    nc.vector.tensor_copy(dst[:, t, bass.ds(h * TOPK, TOPK)], src)

            def weigh(g, h):
                tiles = GROUPS[g]
                T = len(tiles)
                dve.reg_add(raised, raised, T)
                dve.wait_ge(s_const, NCONST)
                dve.wait_ge(s_ex, raised)
                nc.vector.reciprocal(esum[:, 1, 0:T], esum[:, 0, 0:T])
                dve.drain()
                nc.vector.tensor_tensor(expo[:, 0:T], expo[:, 0:T],
                                        esum[:, 1, 0:T].unsqueeze(2).broadcast_to([P, T, TOPK]), ALU.mult)
                dve.drain()
                for i, t in enumerate(tiles):
                    write_choice(gates, expo[:, i, :], t, h)
                dve.drain()

            def stage_rows(which, t, h, signal):
                nc.vector.tensor_copy(stage[:, which, :], expert[:, t, bass.ds(h * TOPK, TOPK)]).then_inc(signal, 1)

            def dots_of(t, batch, before, between, b=0):
                for k in range(TOPK):
                    if k == SLOTS and before is not None:
                        stage_rows(1, *before, s_up)
                    row = ring[:, k % SLOTS, :]
                    dve.wait_ge(s_gath[k % SLOTS], batch * 32 + 16 * (k // SLOTS + 1))
                    nc.vector.tensor_tensor_reduce(out=row, in0=row, in1=x_of[t], scale=1.0, scalar=0.0, op0=ALU.mult,
                                                   op1=ALU.add, accum_out=dots[:, b, k:k + 1]).then_inc(s_dotted, 1)
                    if k % 4 == 3:
                        between()
                nc.vector.drain().then_inc(s_dots, 1)

            def coefficients(t, h, b=0):
                dve.wait_ge(s_acts, h + (FIRST[t] + 1))
                if t not in WOVEN:
                    ins = nc.vector.tensor_tensor(coef[:], acts[:, b], gates[:, t, bass.ds(h * TOPK, TOPK)], ALU.mult)
                    ins.then_inc(s_coef, 1)
                else:
                    dve.drain()
                    nc.vector.tensor_tensor(coef[:], acts[:, b], gates[:, t, bass.ds(h * TOPK, TOPK)], ALU.mult)
                    dve.drain()

            def sums_of(n, batch, between):
                for k in range(TOPK):
                    row = ring[:, k % SLOTS, :]
                    a = acc[:, k % 2, :]
                    dve.wait_ge(s_gath[k % SLOTS], batch * 32 + 16 * (k // SLOTS + 1))
                    if n * TOPK + k - 1 > 0:
                        dve.wait_ge(s_summed, n * TOPK + k - 1)
                    nc.vector.scalar_tensor_tensor(out=a, in0=row, scalar=coef[:, k:k + 1], in1=a, op0=ALU.mult,
                                                   op1=ALU.add).then_inc(s_summed, 1)
                    if k % 4 == 3:
                        between()

            x_of = {t: h2(g, i) for g, ts in enumerate(GROUPS) for i, t in enumerate(ts)}

            for _ in front(0):
                pass
            other = front(1)
            for _ in GROUPS[1]:
                next(other)

            def stage_last(t, batches):
                for slot in range(SLOTS):
                    dve.wait_ge(s_gath[slot], 32 * batches)
                stage_rows(1, t, STEPS[t] - 1, s_up)

            def finish(order, t, parts, gate, gain, residual):
                total = acc[:, 0, :]
                if t == SAMPLE:
                    nc.vector.drain().then_inc(s_half, 1)
                    dve.wait_ge(s_fold, 16)
                    nc.vector.tensor_tensor(total[0:NS, :], total[0:NS, :], ring[0:NS, 3, :], ALU.add)
                    dve.drain()
                dve.wait_ge(s_fin, 64 * (order + 1))
                for half, part in enumerate(parts):
                    cols = slice(half * 512, (half + 1) * 512)
                    nc.vector.tensor_tensor(total[:, cols], part, gate[:, cols], ALU.mult)
                dve.drain()
                nc.vector.tensor_tensor(total, total, residual, ALU.add)
                dve.drain()
                mean_square(total, 12, s_fv)
                r = reciprocal_root(s_fs, order + 1, 12)
                nc.vector.scalar_tensor_tensor(out=total, in0=total, scalar=r, in1=gain, op0=ALU.mult,
                                               op1=ALU.mult).then_inc(s_fy, 1)

            for order, t in enumerate(WOVEN):
                H, first, g = STEPS[t], FIRST[t], CHOOSING.get(t)
                nc.vector.drain().then_inc(s_ring, 1)
                if order:
                    dve.wait_ge(s_y, 16 * order)
                nc.vector.memset(acc[:], 0.0)
                dve.drain()
                at = {"step": 0, "call": 0, "pieces": 0}
                calls = TOPK // 4

                def weave():
                    at["call"] += 1
                    in_step = calls if at["step"] in (0, 1) else 2 * calls
                    while at["pieces"] * in_step < DVE_PIECES[t][at["step"]] * at["call"]:
                        next(other, None)
                        at["pieces"] += 1
                    if at["call"] == in_step:
                        at.update(step=at["step"] + 1, call=0, pieces=0)

                if g is not None:
                    choose(g, 0)
                if order == 0:
                    stage_rows(0, t, 0, s_dn)
                if g is not None:
                    weigh(g, 0)
                    choose(g, 1)
                dots_of(t, 2 * first, None, weave)
                stage_rows(0, t, 1, s_dn)
                for h in range(1, H):
                    dots_of(t, (h + first) * 2 - 1, (t, h - 1), weave, h % 2)
                    if g is not None:
                        weigh(g, h)
                    if h < H - 1:
                        if g is not None:
                            choose(g, h + 1)
                        stage_rows(0, t, h + 1, s_dn)
                    coefficients(t, h - 1, (h - 1) % 2)
                    sums_of(h + (first - 1), (h + first) * 2, weave)
                stage_last(t, 2 * (first + H) - 1)
                if order + 1 < len(WOVEN):
                    stage_rows(0, WOVEN[order + 1], 0, s_dn)
                coefficients(t, H - 1, (H - 1) % 2)
                sums_of(first + H - 1, 2 * (first + H) - 1, weave)
                dve.drain()
                nc.vector.tensor_tensor(acc[:, 0, :], acc[:, 0, :], acc[:, 1, :], ALU.add)
                dve.drain()
                finish(order, t, (acc[:, 0, 0:512], acc[:, 0, 512:1024]), *end_rows(t))
            for _ in other:
                pass

            def finish_later(t):
                dve.wait_ge(s_summed, (FIRST[t] + STEPS[t]) * TOPK)
                order = ORDER.index(t)
                dve.wait_ge(s_y, 16 * order)
                finish(order, t, (bank[6][:, :], bank[7][:, :]), tab[:, 0, :], tab[:, 1, :], tab[:, 2, :])
                nc.vector.drain().then_inc(s_ended, 1)

            def no_weave():
                pass

            nc.vector.drain().then_inc(s_ring, 1)
            for order, t in enumerate(LATER):
                H, first, g = STEPS[t], FIRST[t], CHOOSING.get(t)
                following = LATER[order + 1] if order + 1 < len(LATER) else None
                if order == 0:
                    if g is not None:
                        choose(g, 0)
                    stage_rows(0, t, 0, s_dn)
                    if g is not None:
                        weigh(g, 0)
                        choose(g, 1)
                    dots_of(t, 2 * first, None, no_weave)
                else:
                    last = LATER[order - 1]
                    coefficients(last, STEPS[last] - 1)
                    dots_of(t, 2 * first - 1, (last, STEPS[last] - 1), no_weave)
                stage_rows(0, t, 1, s_dn)
                if order:
                    finish_later(LATER[order - 1])

                def step(h, more):
                    if g is not None:
                        weigh(g, h)
                    coefficients(t, h - 1)
                    dots_of(t, (h + first) * 2 - 1, (t, h - 1), no_weave)
                    if more:
                        if g is not None:
                            choose(g, h + 1)
                        stage_rows(0, t, h + 1, s_dn)

                with dve.Fori(1, H - 1) as h:
                    step(h, True)
                step(H - 1, False)
                if following is not None:
                    stage_rows(0, following, 0, s_dn)
            stage_last(t, 2 * (first + H) - 1)
            coefficients(t, H - 1)
            finish_later(t)


_OUTS = [((1, SEQ, D), "y_prompt"), ((NDEC, DSEQ, D), "y_sample"),
         ((1, 1, SEQ, NH, P), "new_k_prompt"), ((1, 1, SEQ, NH, P), "new_v_prompt"),
         ((1, NDEC, DSEQ, NH, P), "new_k_sample"), ((1, NDEC, DSEQ, NH, P), "new_v_sample"),
         ((1, NDEC, DSEQ, NH, P), "new_gmlp_v_sample")]
_INS = ["x_prompt", "x_sample", "cache_k", "cache_v", "page_table", "c_prompt", "c_sample", "w_ada", "b_ada",
        "g_norm1", "w_in", "sb_bias", "g_v", "b_v", "w_spatial", "b_spatial", "w_branch_a", "w_branch_b",
        "w_out", "g_norm2", "w_query", "sub_keys", "expert_down", "expert_up", "g_final"]


def kernel(**inputs):
    import concourse.bacc as bacc
    from concourse.bass_utils import run_bass_kernel_spmd

    nc = bacc.Bacc("TRN2", target_bir_lowering=False, num_devices=1)
    arrays, args = {}, []
    for name in _INS:
        a = np.ascontiguousarray(inputs[name])
        arrays[f"in_{name}"] = a
        args.append(nc.dram_tensor(f"in_{name}", a.shape, mybir.dt.from_np(a.dtype), kind="ExternalInput").ap())
    for shape, name in _OUTS:
        args.append(nc.dram_tensor(f"out_{name}", shape, F32, kind="ExternalOutput").ap())
    build(nc, *args)
    got = run_bass_kernel_spmd(nc, [arrays], core_ids=[0])
    return tuple(got.results[0][f"out_{name}"] for _, name in _OUTS)
```
